# Optimizing a Trainium2 kernel written in Bass

```python
import jax
import jax.numpy as jnp
from jax import lax
import numpy as np

D_MODEL = 1024
BATCH = 1
SEQ = 1024
DEPTH = 2

GRID_W = 64
CTX_LEN = 256
N_EVEN = (DEPTH + 1) // 2
N_ODD = DEPTH // 2
NORM_EPS = 1e-6

A_HEAD_DIM = 64
A_HEADS = D_MODEL // (2 * A_HEAD_DIM)
A_WIDTH = A_HEADS * A_HEAD_DIM
A_DECAY_RANK = 64
A_ICLR_RANK = 64
A_GATE_RANK = 128
A_DECAY_SCALE = 0.606531
A_LN_EPS = 64e-5
A_COLS = 3 * A_WIDTH + 2 * A_DECAY_RANK + 2 * A_ICLR_RANK + A_GATE_RANK

B_HEADS = D_MODEL // 128
B_NOPE = 64
B_ROPE = 32
B_QK = B_NOPE + B_ROPE
B_V = 64
B_WIDTH = B_HEADS * B_V
B_Q_RANK = D_MODEL // 4
B_KV_RANK = D_MODEL // 8
B_COLS = B_Q_RANK + B_KV_RANK + B_ROPE
ATTN_SCALE = B_QK ** -0.5
ROPE_BASE = 10000.0
Q_BLOCK = 128

IN_COLS = A_COLS + B_COLS
MIX_WIDTH = A_WIDTH + B_WIDTH

C_GROUPS = 8
C_GROUP_DIM = D_MODEL // C_GROUPS

N_EXPERTS = 16
N_GROUPS = 4
EXPERTS_PER_GROUP = N_EXPERTS // N_GROUPS
TOP_K = 2
D_EXPERT = D_MODEL // 2
D_SHARED = D_MODEL // 2
MOE_BLOCK = 128

kernel_name = 'hybrid_rwkv7_mla_fnet_moe_dit'

def rms_norm(x, g, eps=NORM_EPS):
    xf = x.astype(jnp.float32)
    y = xf * lax.rsqrt(jnp.mean(xf * xf, axis=-1, keepdims=True) + eps)
    return (y * g.astype(jnp.float32)).astype(x.dtype)

def modulate(x, g, shift, scale):
    return rms_norm(x, g) * (1 + scale) + shift

def centred_shift(p, mu):
    zeros = jnp.zeros_like(p[:, :1])
    prev = jnp.concatenate([zeros, p[:, :-1]], axis=1)
    nxt = jnp.concatenate([p[:, 1:], zeros], axis=1)
    return p + mu * (0.5 * (prev + nxt) - p)

def rwkv7_scan(s0, r, w, k, v, a_vec, b_vec, reverse):
    def step(s, xs):
        r_t, w_t, k_t, v_t, a_t, b_t = xs
        sa = jnp.einsum('bhvk,bhk->bhv', s, a_t)
        s = s * w_t[:, :, None, :] + sa[..., None] * b_t[:, :, None, :] + v_t[..., None] * k_t[:, :, None, :]
        return s, jnp.einsum('bhvk,bhk->bhv', s, r_t)
    xs = (jnp.swapaxes(r, 0, 1), jnp.swapaxes(w, 0, 1), jnp.swapaxes(k, 0, 1),
          jnp.swapaxes(v, 0, 1), jnp.swapaxes(a_vec, 0, 1), jnp.swapaxes(b_vec, 0, 1))
    s, ys = lax.scan(step, s0, xs, reverse=reverse)
    return s, jnp.swapaxes(ys, 0, 1)

def heads_a(t):
    return t.reshape(t.shape[:-1] + (A_HEADS, A_HEAD_DIM))

def rwkv7_mix(p, s0, mu, w0, w2, a0, a2, g2, k_k, k_a, r_k, ln_w, ln_b):
    dt = p.dtype
    bsz, t_len, _ = p.shape
    p = centred_shift(p, mu).astype(jnp.float32)
    o1, o2, o3 = A_WIDTH, 2 * A_WIDTH, 3 * A_WIDTH
    o4 = o3 + 2 * A_DECAY_RANK
    o5 = o4 + 2 * A_ICLR_RANK
    r, k, v = p[..., :o1], p[..., o1:o2], p[..., o2:o3]
    wd = p[..., o3:o4].reshape(bsz, t_len, 2, A_DECAY_RANK)
    ad = p[..., o4:o5].reshape(bsz, t_len, 2, A_ICLR_RANK)
    gd = p[..., o5:]
    w = jnp.exp(-A_DECAY_SCALE * jax.nn.sigmoid(w0 + jnp.einsum('btdr,drc->btdc', jnp.tanh(wd), w2)))
    a = jax.nn.sigmoid(a0 + jnp.einsum('btdr,drc->btdc', ad, a2))
    g = jnp.einsum('btr,rc->btc', jax.nn.sigmoid(gd), g2)
    kk = heads_a(k * k_k)
    kk = kk * lax.rsqrt(jnp.sum(kk * kk, axis=-1, keepdims=True) + 1e-12)
    kd = heads_a(k[:, :, None, :] * (1 + (a - 1) * k_a))
    bd = kk[:, :, None] * heads_a(a)
    w_h = heads_a(w)
    r_h, v_h = heads_a(r), heads_a(v)
    s_f, y_f = rwkv7_scan(s0[0], r_h, w_h[:, :, 0], kd[:, :, 0], v_h, -kk, bd[:, :, 0], False)
    s_b, y_b = rwkv7_scan(s0[1], r_h, w_h[:, :, 1], kd[:, :, 1], v_h, -kk, bd[:, :, 1], True)
    y = y_f + y_b
    mean = jnp.mean(y, axis=-1, keepdims=True)
    var = jnp.mean(jnp.square(y - mean), axis=-1, keepdims=True)
    y = ((y - mean) * lax.rsqrt(var + A_LN_EPS)).reshape(bsz, t_len, A_WIDTH) * ln_w + ln_b
    bonus = jnp.sum(jnp.sum(r_h[:, :, None] * kd * r_k, axis=-1, keepdims=True) * v_h[:, :, None], axis=2)
    y = (y + bonus.reshape(bsz, t_len, A_WIDTH)) * g
    return y.astype(dt), jnp.stack([s_f, s_b])

def axial_rope_tables(seq_len):
    rows = seq_len // GRID_W
    row = jnp.repeat(jnp.arange(rows), GRID_W).astype(jnp.float32)
    col = jnp.tile(jnp.arange(GRID_W), rows).astype(jnp.float32)
    axis_dim = B_ROPE // 2
    inv = ROPE_BASE ** (-jnp.arange(0, axis_dim, 2, dtype=jnp.float32) / axis_dim)
    ang = jnp.concatenate([row[:, None] * inv, col[:, None] * inv], axis=-1)
    return jnp.cos(ang), jnp.sin(ang)

def apply_axial_rope(x, cos, sin):
    half = B_ROPE // 2
    xn, x1, x2 = x[..., :B_NOPE], x[..., B_NOPE:B_NOPE + half], x[..., B_NOPE + half:]
    c = cos[None, :, None, :].astype(x.dtype)
    s = sin[None, :, None, :].astype(x.dtype)
    return jnp.concatenate([xn, x1 * c - x2 * s, x2 * c + x1 * s], axis=-1)

def mla_qkv(p, rope, q_norm, w_q_up, kv_norm, w_kv_up, q_gain, k_gain):
    bsz, t_len, _ = p.shape
    pq = p[..., :B_Q_RANK]
    pkv = p[..., B_Q_RANK:B_Q_RANK + B_KV_RANK]
    pkr = p[..., B_Q_RANK + B_KV_RANK:]
    q = jnp.einsum('btr,rc->btc', rms_norm(pq, q_norm), w_q_up).reshape(bsz, t_len, B_HEADS, B_QK)
    kv = jnp.einsum('btr,rc->btc', rms_norm(pkv, kv_norm), w_kv_up).reshape(bsz, t_len, B_HEADS, B_NOPE + B_V)
    k = jnp.concatenate([kv[..., :B_NOPE], jnp.broadcast_to(pkr[:, :, None, :], (bsz, t_len, B_HEADS, B_ROPE))], axis=-1)
    v = kv[..., B_NOPE:]
    q, k = rms_norm(q, q_gain), rms_norm(k, k_gain)
    if rope is not None:
        q, k = apply_axial_rope(q, *rope), apply_axial_rope(k, *rope)
    return q, k, v

def attention(q, k, v):
    s = jnp.einsum('bqhd,bkhd->bhqk', q, k).astype(jnp.float32) * ATTN_SCALE
    pr = jax.nn.softmax(s, axis=-1).astype(v.dtype)
    return jnp.einsum('bhqk,bkhd->bqhd', pr, v)

def blocked_attention(q, k, v):
    bsz, t_len, nh, dq = q.shape
    nb = t_len // Q_BLOCK
    qb = jnp.moveaxis(q.reshape(bsz, nb, Q_BLOCK, nh, dq), 1, 0)
    out = lax.map(lambda qi: attention(qi, k, v), qb)
    return jnp.moveaxis(out, 0, 1).reshape(bsz, t_len, nh, v.shape[-1])

def even_mixer(h_lat, h_ctx, w_in, w_out, a_prm, b_prm, rope, need_ctx_out):
    bsz, seq, _ = h_lat.shape
    ctx_len = h_ctx.shape[1]
    p_lat = jnp.einsum('btd,dc->btc', h_lat, w_in)
    p_ctx = jnp.einsum('btd,dc->btc', h_ctx, w_in)
    s_zero = jnp.zeros((2, bsz, A_HEADS, A_HEAD_DIM, A_HEAD_DIM), jnp.float32)
    ya_ctx, s_ctx = rwkv7_mix(p_ctx[..., :A_COLS], s_zero, *a_prm)
    ya_lat, _ = rwkv7_mix(p_lat[..., :A_COLS], s_ctx, *a_prm)
    q_c, k_c, v_c = mla_qkv(p_ctx[..., A_COLS:], None, *b_prm)
    q_l, k_l, v_l = mla_qkv(p_lat[..., A_COLS:], rope, *b_prm)
    yb_lat = blocked_attention(q_l, jnp.concatenate([k_c, k_l], axis=1), jnp.concatenate([v_c, v_l], axis=1))
    o_lat = jnp.einsum('btc,cd->btd', jnp.concatenate([ya_lat, yb_lat.reshape(bsz, seq, B_WIDTH)], axis=-1), w_out)
    if not need_ctx_out:
        return o_lat, None
    yb_ctx = attention(q_c, k_c, v_c)
    o_ctx = jnp.einsum('btc,cd->btd', jnp.concatenate([ya_ctx, yb_ctx.reshape(bsz, ctx_len, B_WIDTH)], axis=-1), w_out)
    return o_lat, o_ctx

def fourier_mixer(h, w_out):
    bsz, t_len, d = h.shape
    hg = h.astype(jnp.float32).reshape(bsz, t_len, C_GROUPS, C_GROUP_DIM)
    f = jnp.fft.fft2(hg, axes=(1, 3), norm='ortho').real.reshape(bsz, t_len, d).astype(h.dtype)
    return jnp.einsum('btd,de->bte', f, w_out)

def swiglu(h, wg, wu, wd):
    return jnp.dot(jax.nn.silu(jnp.dot(h, wg)) * jnp.dot(h, wu), wd)

def moe_ffn(h, router_w, router_b, w_gate, w_up, w_down, sh_gate, sh_up, sh_down):
    n_tok, d = h.shape
    scores = jax.nn.sigmoid(jnp.dot(h.astype(jnp.float32), router_w.astype(jnp.float32)))
    sel = (scores + router_b.astype(jnp.float32)).reshape(n_tok, N_GROUPS, EXPERTS_PER_GROUP)
    group_score = jnp.sum(lax.top_k(sel, 2)[0], axis=-1)
    g_idx = jnp.argmax(group_score, axis=-1)
    sel_in = jnp.take_along_axis(sel, g_idx[:, None, None], axis=1)[:, 0]
    _, local = lax.top_k(sel_in, TOP_K)
    e_idx = g_idx[:, None] * EXPERTS_PER_GROUP + local
    wts = jnp.take_along_axis(scores, e_idx, axis=1)
    wts = wts / jnp.sum(wts, axis=-1, keepdims=True)
    n_asg = n_tok * TOP_K
    flat_e = e_idx.reshape(n_asg)
    flat_tok = jnp.repeat(jnp.arange(n_tok), TOP_K)
    order = jnp.argsort(flat_e)
    e_sorted, tok_sorted, w_sorted = flat_e[order], flat_tok[order], wts.reshape(n_asg)[order]
    counts = jnp.bincount(flat_e, length=N_EXPERTS)
    start = jnp.cumsum(counts) - counts
    padded = (counts + MOE_BLOCK - 1) // MOE_BLOCK * MOE_BLOCK
    pend = jnp.cumsum(padded)
    pstart = pend - padded
    dest = pstart[e_sorted] + (jnp.arange(n_asg) - start[e_sorted])
    n_blocks = (n_asg + N_EXPERTS * (MOE_BLOCK - 1) + MOE_BLOCK - 1) // MOE_BLOCK
    slot_tok = jnp.full((n_blocks * MOE_BLOCK,), n_tok, jnp.int32).at[dest].set(tok_sorted.astype(jnp.int32))
    block_e = jnp.minimum(jnp.searchsorted(pend, jnp.arange(n_blocks) * MOE_BLOCK, side='right'), N_EXPERTS - 1)
    h_pad = jnp.concatenate([h, jnp.zeros((1, d), h.dtype)], axis=0)
    xb = h_pad[slot_tok].reshape(n_blocks, MOE_BLOCK, d)
    yb = lax.map(lambda a: swiglu(a[0], w_gate[a[1]], w_up[a[1]], w_down[a[1]]), (xb, block_e))
    y_asg = yb.reshape(n_blocks * MOE_BLOCK, d)[dest] * w_sorted[:, None]
    routed = jax.ops.segment_sum(y_asg, tok_sorted, num_segments=n_tok)
    return (swiglu(h, sh_gate, sh_up, sh_down) + routed).astype(h.dtype)

def setup_inputs(seed: int = 0) -> dict:
    key = jax.random.key(seed)
    ks = iter(jax.random.split(key, 40))
    f32 = jnp.float32

    def nrm(shape, scale):
        return jax.random.normal(next(ks), shape, f32) * scale

    def gain(shape):
        return 1.0 + nrm(shape, 0.02)

    return {
        'x': nrm((BATCH, SEQ, D_MODEL), 1.0),
        'c': nrm((BATCH, D_MODEL), 1.0),
        'ctx': nrm((BATCH, CTX_LEN, D_MODEL), 1.0),
        'c_ctx': nrm((D_MODEL,), 1.0),
        'norm1_g': gain((DEPTH, D_MODEL)),
        'norm2_g': gain((DEPTH, D_MODEL)),
        'mod_w': nrm((DEPTH, D_MODEL, 6 * D_MODEL), 0.5 * D_MODEL ** -0.5),
        'mod_b': nrm((DEPTH, 6 * D_MODEL), 0.02),
        'w_in': nrm((N_EVEN, D_MODEL, IN_COLS), D_MODEL ** -0.5),
        'a_mu': jax.random.uniform(next(ks), (N_EVEN, A_COLS), f32),
        'a_w0': nrm((N_EVEN, 2, A_WIDTH), 1.5) - 1.0,
        'a_w2': nrm((N_EVEN, 2, A_DECAY_RANK, A_WIDTH), 0.5 * A_DECAY_RANK ** -0.5),
        'a_a0': nrm((N_EVEN, 2, A_WIDTH), 0.3),
        'a_a2': nrm((N_EVEN, 2, A_ICLR_RANK, A_WIDTH), 0.5 * A_ICLR_RANK ** -0.5),
        'a_g2': nrm((N_EVEN, A_GATE_RANK, A_WIDTH), A_GATE_RANK ** -0.5),
        'a_k_k': 0.85 + nrm((N_EVEN, A_WIDTH), 0.05),
        'a_k_a': 1.0 + nrm((N_EVEN, A_WIDTH), 0.05),
        'a_r_k': nrm((N_EVEN, A_HEADS, A_HEAD_DIM), 0.1),
        'a_ln_w': gain((N_EVEN, A_WIDTH)),
        'a_ln_b': nrm((N_EVEN, A_WIDTH), 0.02),
        'b_q_norm': gain((N_EVEN, B_Q_RANK)),
        'b_w_q_up': nrm((N_EVEN, B_Q_RANK, B_HEADS * B_QK), B_Q_RANK ** -0.5),
        'b_kv_norm': gain((N_EVEN, B_KV_RANK)),
        'b_w_kv_up': nrm((N_EVEN, B_KV_RANK, B_HEADS * (B_NOPE + B_V)), B_KV_RANK ** -0.5),
        'b_q_gain': gain((N_EVEN, B_QK)),
        'b_k_gain': gain((N_EVEN, B_QK)),
        'w_out_even': nrm((N_EVEN, MIX_WIDTH, D_MODEL), MIX_WIDTH ** -0.5),
        'w_out_fourier': nrm((N_ODD, D_MODEL, D_MODEL), D_MODEL ** -0.5),
        'router_w': nrm((D_MODEL, N_EXPERTS), D_MODEL ** -0.5),
        'router_b': nrm((N_EXPERTS,), 0.01),
        'moe_w_gate': nrm((DEPTH, N_EXPERTS, D_MODEL, D_EXPERT), D_MODEL ** -0.5),
        'moe_w_up': nrm((DEPTH, N_EXPERTS, D_MODEL, D_EXPERT), D_MODEL ** -0.5),
        'moe_w_down': nrm((DEPTH, N_EXPERTS, D_EXPERT, D_MODEL), D_EXPERT ** -0.5),
        'shared_w_gate': nrm((DEPTH, D_MODEL, D_SHARED), D_MODEL ** -0.5),
        'shared_w_up': nrm((DEPTH, D_MODEL, D_SHARED), D_MODEL ** -0.5),
        'shared_w_down': nrm((DEPTH, D_SHARED, D_MODEL), D_SHARED ** -0.5),
    }

def reference(x, c, ctx, c_ctx, norm1_g, norm2_g, mod_w, mod_b, w_in, a_mu, a_w0, a_w2, a_a0, a_a2, a_g2,
              a_k_k, a_k_a, a_r_k, a_ln_w, a_ln_b, b_q_norm, b_w_q_up, b_kv_norm, b_w_kv_up, b_q_gain, b_k_gain,
              w_out_even, w_out_fourier, router_w, router_b, moe_w_gate, moe_w_up, moe_w_down,
              shared_w_gate, shared_w_up, shared_w_down):
    bsz, seq, d = x.shape
    ctx_len = ctx.shape[1]
    rope = axial_rope_tables(seq)
    for i in range(DEPTH):
        last = i == DEPTH - 1
        j = i // 2
        sh1, sc1, g1, sh2, sc2, g2 = jnp.split((jnp.dot(jax.nn.silu(c), mod_w[i]) + mod_b[i])[:, None, :], 6, axis=-1)
        sh1c, sc1c, g1c, sh2c, sc2c, g2c = jnp.split(jnp.dot(jax.nn.silu(c_ctx), mod_w[i]) + mod_b[i], 6, axis=-1)
        h_l = modulate(x, norm1_g[i], sh1, sc1)
        h_c = modulate(ctx, norm1_g[i], sh1c, sc1c)
        if i % 2 == 0:
            a_prm = (a_mu[j], a_w0[j], a_w2[j], a_a0[j], a_a2[j], a_g2[j], a_k_k[j], a_k_a[j], a_r_k[j], a_ln_w[j], a_ln_b[j])
            b_prm = (b_q_norm[j], b_w_q_up[j], b_kv_norm[j], b_w_kv_up[j], b_q_gain[j], b_k_gain[j])
            o_l, o_c = even_mixer(h_l, h_c, w_in[j], w_out_even[j], a_prm, b_prm, rope, not last)
        else:
            o_l = fourier_mixer(h_l, w_out_fourier[j])
            o_c = None if last else fourier_mixer(h_c, w_out_fourier[j])
        x = x + g1 * o_l
        moe_prm = (router_w, router_b, moe_w_gate[i], moe_w_up[i], moe_w_down[i],
                   shared_w_gate[i], shared_w_up[i], shared_w_down[i])
        h2_l = modulate(x, norm2_g[i], sh2, sc2).reshape(bsz * seq, d)
        if last:
            x = x + g2 * moe_ffn(h2_l, *moe_prm).reshape(bsz, seq, d)
        else:
            ctx = ctx + g1c * o_c
            h2_c = modulate(ctx, norm2_g[i], sh2c, sc2c).reshape(bsz * ctx_len, d)
            y = moe_ffn(jnp.concatenate([h2_l, h2_c], axis=0), *moe_prm)
            x = x + g2 * y[:bsz * seq].reshape(bsz, seq, d)
            ctx = ctx + g2c * y[bsz * seq:].reshape(bsz, ctx_len, d)
    return x


_drawn_inputs = setup_inputs


def setup_inputs(seed=0):
    import zlib

    import numpy as np

    out = dict(_drawn_inputs(seed))
    spreads = {}
    factors = {'norm1_g': 2.735,
     'a_k_k': 12.152,
     'a_ln_w': 24.12,
     'a_ln_b': 23.772,
     'b_q_norm': 8.0,
     'b_kv_norm': 8.0,
     'b_q_gain': 8.0,
     'b_k_gain': 8.0,
     'norm2_g': 3.574}
    for name, (base, spread) in spreads.items():
        noise = np.random.default_rng([zlib.crc32(name.encode()), seed]).standard_normal(out[name].shape)
        drawn = base * np.exp(spread * noise) if base else spread * noise
        out[name] = jnp.asarray(drawn.astype(out[name].dtype))
    for name, factor in factors.items():
        out[name] = (out[name] * factor).astype(out[name].dtype)
    return out
```

```python
from contextlib import ExitStack

import numpy as np

import concourse.bass as bass
from concourse import mybir

ALU = mybir.AluOpType
ACT = mybir.ActivationFunctionType
AX = mybir.AxisListType
F32 = mybir.dt.float32
I32 = mybir.dt.int32
U32 = mybir.dt.uint32

P = 128
D = 1024
KD = D // P
CTX = 256
SEQ = 1024
N = CTX + SEQ
NT = N // P
NTC = CTX // P
BANK = 512
EPS = 1e-6
SEGS = ((0, 512), (512, 1024), (1024, 1280))
PARTS = ((0, CTX, 1), (CTX, N, 0))

COLS = {}
_n = 0
for _name, _w in (("cond", 16), ("norm1", 16), ("norm2", 16), ("mu", 20), ("w0", 8), ("a0", 8), ("k_k", 4), ("k_a", 4),
                  ("r_k", 4), ("ln_w", 4), ("ln_b", 4), ("q_norm", 2), ("kv_norm", 1), ("q_gain", 1), ("k_gain", 1)):
    COLS[_name] = _n
    _n += _w
N_COLS = _n
A_CHUNKS = 15
R0, K0, V0, WD, AD, GD = 0, 4, 8, 12, 13, 14
Q_CH, KV_CH, KR_CH = 15, 17, 18


def free(m):
    return m + 1


def done(m):
    return m + 3


def col(name, i=0):
    return COLS[name] + i


class Stage(ExitStack):

    def __init__(self, nc):
        super().__init__()
        self.nc, self.sems = nc, []

    def sem(self, name):
        self.sems.append(self.nc.alloc_semaphore(name))
        return self.sems[-1]

    def __exit__(self, *raised):
        super().__exit__(*raised)
        if raised[0] is None:
            self.nc.clear_and_free_semaphores(self.sems)
            self.nc.all_engine_barrier()


class Kit:

    def __init__(self, nc, args, stack):
        self.nc, self.args = nc, args
        sb = lambda name, shape, dt=F32: stack.enter_context(nc.sbuf_tensor(name, shape, dt))
        self.cols = sb("cols", [P, N_COLS])
        self.mod = sb("mod", [P, 96, 2])
        self.gain = sb("gain", [P, 4, KD, 2])
        self.ident = sb("ident", [P, P])
        self.ones = sb("ones", [P, P])
        self.head_ones = sb("head_ones", [P, P])


def modulation(kit):
    nc, a = kit.nc, kit.args
    blocks = 24
    with Stage(nc) as st:
        sb = lambda name, shape: st.enter_context(nc.sbuf_tensor(name, shape, F32))
        sem = lambda name: st.sem(name)
        w = [sb(f"mod_w{u}", [P, KD, 512]) for u in range(2)]
        cs = sb("mod_silu", [P, KD, 2])
        bias = sb("mod_bias", [P, 96, 2])
        row = [sb(f"mod_row{u}", [P, 512]) for u in range(2)]
        ps_row = [st.enter_context(nc.psum_tensor(f"ps_row{u}", [2, 512], F32)) for u in range(2)]
        ps_col = [st.enter_context(nc.psum_tensor(f"ps_col{u}", [P, 4, P], F32)) for u in range(2)]
        small_in, silu_done, ones_done = sem("small_in"), sem("silu_done"), sem("ones_done")
        w_in = [sem(f"mod_w_in{u}") for u in range(2)]
        rows_summed, rows_copied, rows_turned, cols_kept = (
            sem("rows_summed"), sem("rows_copied"), sem("rows_turned"), sem("cols_kept"))
        gain_step = sem("gain_step")
        block = st.enter_context(nc.Block("modulation"))

        @block.sync
        def _(sp):
            sp.dma_start(kit.cols[:], a["cols"][:, :]).then_inc(small_in, 16)
            sp.dma_start(kit.ident[:], a["ident"][:, :]).then_inc(small_in, 16)
            sp.dma_start(kit.head_ones[:], a["head_ones"][:, :]).then_inc(small_in, 16)
            sp.dma_start(bias[:], a["mod_bias"][:, :, :]).then_inc(small_in, 16)
            with sp.Fori(0, blocks // 2) as i:
                for u in range(2):
                    sp.wait_ge(rows_summed, free(i * 2 + u))
                    sp.dma_start(w[u][:], a["mod_w"][:, :, bass.ds(i * 1024 + u * 512, 512)]).then_inc(w_in[u], 16)

        @block.scalar
        def _(act):
            act.wait_ge(small_in, 64)
            nc.scalar.activation(cs[:], kit.cols[:, 0:16].rearrange("p (k v) -> p k v", v=2), ACT.Silu).then_inc(silu_done, 1)

        @block.tensor
        def _(pe):
            pe.sem_inc(rows_summed, 2)
            pe.wait_ge(silu_done, 1)
            with pe.Fori(0, blocks // 2) as i:
                for u in range(2):
                    pe.wait_ge(w_in[u], i * 16 + 16)
                    for k in range(KD):
                        mm = nc.tensor.matmul(ps_row[u][:], cs[:, k, :], w[u][:, k, :], start=k == 0, stop=k == KD - 1)
                    mm.then_inc(rows_summed, 1)
                    pe.wait_ge(rows_copied, i * 2 + u + 1)
                    for q in range(4):
                        t = nc.tensor.transpose(ps_col[u][:, q, :], row[u][:, q * P:(q + 1) * P], kit.ident[:])
                    t.then_inc(rows_turned, 1)

        @block.vector
        def _(dve):
            nc.vector.memset(kit.ones[:], 1.0).then_inc(ones_done, 1)
            for u in range(2):
                nc.vector.memset(row[u][:], 0.0).then_inc(ones_done, 1)
            dve.wait_ge(small_in, 64)
            dve.wait_ge(ones_done, 3)
            with dve.Fori(0, blocks // 2) as i:
                for u in range(2):
                    dve.wait_ge(rows_summed, done(i * 2 + u))
                    nc.vector.tensor_copy(row[u][0:2, :], ps_row[u][:]).then_inc(rows_copied, 1)
                    dve.wait_ge(rows_turned, i * 2 + u + 1)
                    at = bass.ds(i * 8 + u * 4, 4)
                    nc.vector.tensor_tensor(kit.mod[:, at, :], ps_col[u][:, :, 0:2], bias[:, at, :], ALU.add).then_inc(cols_kept, 1)
            dve.wait_ge(cols_kept, blocks)
            for layer in range(2):
                for which, sixth in ((0, 1), (1, 4)):
                    for v in range(2):
                        c0 = layer * 48 + sixth * KD
                        g = kit.cols[:, col(("norm1", "norm2")[which], layer * KD):][:, 0:KD]
                        nc.vector.scalar_tensor_tensor(
                            out=kit.gain[:, layer * 2 + which, :, v], in0=kit.mod[:, c0:c0 + KD, v], scalar=1.0, in1=g,
                            op0=ALU.add, op1=ALU.mult).then_inc(gain_step, 1)
            dve.wait_ge(gain_step, 8)


def normalise(kit, name, x, h, lo, which, shift, load=None):
    nc = kit.nc
    parts = [p for p in PARTS if p[1] > lo]
    segs = [(s, e) for s, e in SEGS] if lo == 0 else [(lo, lo + 512), (lo + 512, N)]
    with Stage(nc) as st:
        sem = lambda s: st.sem(f"{name}_{s}")
        sq = [st.enter_context(nc.sbuf_tensor(f"{name}_sq{u}", [P, N], F32)) for u in range(2)]
        rstd = st.enter_context(nc.sbuf_tensor(f"{name}_rstd", [P, N], F32))
        ps = st.enter_context(nc.psum_tensor(f"{name}_ps", [P, 3, BANK], F32))
        x_in = [sem(f"x_in{k}") for k in range(KD)]
        squared, summed, chain, root, scaled, done = (
            sem("squared"), sem("summed"), sem("chain"), sem("root"), sem("scaled"), sem("done"))
        block = st.enter_context(nc.Block(name))

        @block.sync
        def _(sp):
            if load is not None:
                for k in range(KD):
                    for s, e, v in parts:
                        sp.dma_start(x[:, k, s:e], load[v][k * P:(k + 1) * P, :]).then_inc(x_in[k], 16)

        @block.scalar
        def _(act):
            for k in range(KD):
                if load is not None:
                    act.wait_ge(x_in[k], 16 * len(parts))
                if k >= 2:
                    act.wait_ge(summed, k - 1)
                nc.scalar.activation(sq[k % 2][:, lo:], x[:, k, lo:], ACT.Square).then_inc(squared, 1)
            act.wait_ge(chain, 1)
            nc.scalar.activation(rstd[:, lo:], rstd[:, lo:], ACT.Sqrt).then_inc(root, 1)
            for k in range(KD):
                act.wait_ge(scaled, k + 1)
                for s, e, v in parts:
                    a = nc.scalar.activation(h[:, k, s:e], h[:, k, s:e], ACT.Identity, scale=kit.gain[:, which, k, v:v + 1],
                                             bias=kit.mod[:, shift + k, v:v + 1])
                a.then_inc(done, 1)

        @block.tensor
        def _(pe):
            for k in range(KD):
                pe.wait_ge(squared, k + 1)
                for n, (s, e) in enumerate(segs):
                    mm = nc.tensor.matmul(ps[:, n, 0:e - s], kit.ones[:], sq[k % 2][:, s:e], start=k == 0, stop=k == KD - 1)
                mm.then_inc(summed, 1)

        @block.vector
        def _(dve):
            dve.wait_ge(summed, KD)
            width = N - lo
            flat = ps[:, :, :].rearrange("p b c -> p (b c)")[:, 0:width]
            nc.vector.tensor_scalar(rstd[:, lo:], flat, 1.0 / D, EPS, ALU.mult, ALU.add).then_inc(chain, 1)
            dve.wait_ge(root, 1)
            nc.vector.reciprocal(rstd[:, lo:], rstd[:, lo:]).then_inc(chain, 1)
            dve.wait_ge(chain, 2)
            for k in range(KD):
                nc.vector.tensor_tensor(h[:, k, lo:], x[:, k, lo:], rstd[:, lo:], ALU.mult).then_inc(scaled, 1)


def project_in(kit, h, out):
    nc, a = kit.nc, kit.args
    loops = 9
    with Stage(nc) as st:
        sb = lambda name, shape: st.enter_context(nc.sbuf_tensor(name, shape, F32))
        sem = lambda name: st.sem(name)
        w = [sb(f"in_w{u}", [P, KD, P]) for u in range(2)]
        w32 = sb("in_w32", [P, KD, 32])
        raw = [sb(f"in_raw{u}", [P, N + 3]) for u in range(2)]
        kept = [sb(f"in_kept{u}", [P, N]) for u in range(2)]
        mixed = [sb(f"in_mixed{u}", [P, N]) for u in range(2)]
        keep_col = sb("in_keep_col", [P, 20])
        half_col = sb("in_half_col", [P, 20])
        ps = [st.enter_context(nc.psum_tensor(f"in_ps{u}", [P, 3, BANK], F32)) for u in range(2)]
        w_in = [sem(f"in_w_in{u}") for u in range(2)]
        w32_in = sem("in_w32_in")
        stored = [sem(f"in_stored{u}") for u in range(2)]
        setup, multiplied, copied, summed, shifted, mixed_free = (
            sem("in_setup"), sem("in_multiplied"), sem("in_copied"), sem("in_summed"), sem("in_shifted"), sem("in_mixed_free"))
        block = st.enter_context(nc.Block("project_in"))
        gaps = ((0, CTX, 1), (CTX, N, 2))

        @block.sync
        def _(sp):
            sp.dma_start(w32[:], a["w_in"][:, :, 18 * P:18 * P + 32]).then_inc(w32_in, 16)
            with sp.Fori(0, loops) as i:
                for u in range(2):
                    sp.wait_ge(multiplied, free(i * 2 + u))
                    sp.dma_start(w[u][:], a["w_in"][:, :, bass.ds(i * 256 + u * P, P)]).then_inc(w_in[u], 16)

        @block.tensor
        def _(pe):
            pe.sem_inc(multiplied, 2)
            with pe.Fori(0, loops) as i:
                for u in range(2):
                    pe.wait_ge(w_in[u], i * 16 + 16)
                    pe.wait_ge(copied, free(i * 2 + u))
                    for n, (s, e) in enumerate(SEGS):
                        for k in range(KD):
                            mm = nc.tensor.matmul(ps[u][:, n, 0:e - s], w[u][:, k, :], h[:, k, s:e], start=k == 0, stop=k == KD - 1)
                    mm.then_inc(multiplied, 1)
            pe.wait_ge(w32_in, 16)
            pe.wait_ge(copied, free(2 * loops))
            for n, (s, e) in enumerate(SEGS):
                for k in range(KD):
                    mm = nc.tensor.matmul(ps[0][0:32, n, 0:e - s], w32[:, k, :], h[:, k, s:e], start=k == 0, stop=k == KD - 1)
            mm.then_inc(multiplied, 1)

        @block.scalar
        def _(act):
            act.sem_inc(copied, 2)
            act.wait_ge(setup, 4)
            with act.Fori(0, loops) as i:
                for u in range(2):
                    act.wait_ge(multiplied, done(i * 2 + u))
                    act.wait_ge(shifted, free(i * 2 + u))
                    flat = ps[u][:, :, :].rearrange("p b c -> p (b c)")
                    for s, e, off in gaps:
                        nc.scalar.activation(raw[u][:, s + off:e + off], flat[:, s:e], ACT.Copy)
                    nc.scalar.activation(kept[u][:], flat[:, 0:N], ACT.Copy, scale=keep_col[:, bass.ds(i * 2 + u, 1)]).then_inc(copied, 1)
            act.wait_ge(multiplied, done(2 * loops))
            act.wait_ge(shifted, free(2 * loops))
            flat = ps[0][:, :, :].rearrange("p b c -> p (b c)")
            nc.scalar.activation(kept[0][0:32, :], flat[0:32, 0:N], ACT.Copy).then_inc(copied, 1)

        @block.vector
        def _(dve):
            mu = kit.cols[:, col("mu"):col("mu") + 20]
            nc.vector.tensor_scalar(keep_col[:], mu, -1.0, 1.0, ALU.mult, ALU.add).then_inc(setup, 1)
            nc.vector.tensor_scalar(half_col[:], mu, 0.5, None, ALU.mult).then_inc(setup, 1)
            for u in range(2):
                nc.vector.memset(raw[u][:], 0.0).then_inc(setup, 1)
            dve.wait_ge(setup, 4)
            nc.vector.sem_inc(shifted, 2)
            with dve.Fori(0, loops) as i:
                for u in range(2):
                    dve.wait_ge(copied, done(i * 2 + u))
                    dve.wait_ge(mixed_free, i * 2 + u + 1)
                    for s, e, off in gaps:
                        t = nc.vector.tensor_tensor(mixed[u][:, s:e], raw[u][:, s + off - 1:e + off - 1], raw[u][:, s + off + 1:e + off + 1], ALU.add)
                    t.then_inc(summed, 1)
                    dve.wait_ge(summed, i * 2 + u + 1)
                    nc.vector.scalar_tensor_tensor(out=mixed[u][:], in0=mixed[u][:], scalar=half_col[:, bass.ds(i * 2 + u, 1)],
                                                   in1=kept[u][:], op0=ALU.mult, op1=ALU.add).then_inc(shifted, 1)

        @block.gpsimd
        def _(pool):
            pool.sem_inc(mixed_free, 2)
            with pool.Fori(0, loops) as i:
                for u in range(2):
                    pool.wait_ge(shifted, done(i * 2 + u))
                    pool.dma_start(out[bass.ds(i * 2 + u, 1), :, :].rearrange("o p n -> p (o n)"), mixed[u][:]).then_inc(stored[u], 16)
                    pool.wait_ge(stored[u], i * 16 + 16)
                    pool.sem_inc(mixed_free, 1)
            pool.wait_ge(copied, done(2 * loops))
            pool.dma_start(out[18, 0:32, :], kept[0][0:32, :]).then_inc(stored[0], 16)
            pool.wait_ge(stored[0], 16 * (loops + 1))
            pool.wait_ge(stored[1], 16 * loops)


class Link:

    def __init__(self, engine, sem, start=0):
        self.engine, self.sem, self.start, self.n = engine, sem, start, 0

    def __call__(self, instruction):
        self.n += 1
        instruction.then_inc(self.sem, 1)
        self.engine.wait_ge(self.sem, self.start + self.n)


KINDS = 5
DECAY_SCALE = 0.606531
STEP_OF = {0: list(range(NT)), 1: [1, 0] + [NT + 1 - c for c in range(NTC, NT)]}


def mixing_inputs(kit, p, steps, half_decay, gate, bonus):
    nc, a = kit.nc, kit.args
    with Stage(nc) as st:
        sb = lambda name, shape=(P, N): st.enter_context(nc.sbuf_tensor(f"mi_{name}", list(shape), F32))
        sem = lambda name: st.sem(f"mi_{name}")
        r, k, v, wd, ad, gd = (sb(x) for x in ("r", "k", "v", "wd", "ad", "gd"))
        w2, a2, g2 = (sb(x, (P, P)) for x in ("w2", "a2", "g2"))
        kk, tmp, sig, iclr, cum, q, q2, ea, eb, ec, kd, kd_sum, gate_out, bonus_out, restart = (
            sb(x) for x in ("kk", "tmp", "sig", "iclr", "cum", "q", "q2", "ea", "eb", "ec", "kd", "kd_sum", "gate_out",
                            "bonus_out", "restart"))
        kinds = [sb(f"kinds{d}", (P, KINDS, N)) for d in range(2)]
        ka_rest = sb("ka_rest", (P, 4))
        psa = st.enter_context(nc.psum_tensor("mi_psa", [P, 3, BANK], F32))
        psb = st.enter_context(nc.psum_tensor("mi_psb", [P, 3, BANK], F32))
        fa, fb = (x[:, :, :].rearrange("p b c -> p (b c)")[:, 0:N] for x in (psa, psb))
        low_in, low_ready, rows_in, link = sem("low_in"), sem("low_ready"), sem("rows_in"), sem("link")
        kk_scaled, squared, norm_ps, norm_read, rooted = (
            sem("kk_scaled"), sem("squared"), sem("norm_ps"), sem("norm_read"), sem("rooted"))
        decay_ps, iclr_ps, decay_sig, iclr_sig, q_ready, exps = (
            sem("decay_ps"), sem("iclr_ps"), sem("decay_sig"), sem("iclr_sig"), sem("q_ready"), sem("exps"))
        v_copied, kinds_ready, kinds_out = sem("v_copied"), sem("kinds_ready"), [sem(f"kinds_out{d}") for d in range(2)]
        rk_ready, bonus_ps, bonus_read, gate_ps, gate_read = (
            sem("rk_ready"), sem("bonus_ps"), sem("bonus_read"), sem("gate_ps"), sem("gate_read"))
        tiles_free, after_out = sem("tiles_free"), sem("after_out")
        block = st.enter_context(nc.Block("mixing_inputs"))

        def product(pe, ps, lhsT, rhs):
            for n, (s, e) in enumerate(SEGS):
                mm = nc.tensor.matmul(ps[:, n, 0:e - s], lhsT, rhs[:, s:e], start=True, stop=True)
            return mm

        @block.sync
        def _(sp):
            for t, c in ((wd, WD), (ad, AD), (gd, GD)):
                sp.dma_start(t[:], p[c, :, :]).then_inc(low_in, 16)
            sp.dma_start(restart[:], a["restart"][:, :]).then_inc(low_in, 16)
            with sp.Fori(0, 4) as j:
                for t, c in ((r, R0), (k, K0), (v, V0)):
                    sp.dma_start(t[:], p[bass.ds(j + c, 1), :, :].rearrange("o p n -> p (o n)")).then_inc(rows_in, 16)
                for t, w in ((w2, "a_w2"), (a2, "a_a2"), (g2, "a_g2")):
                    sp.dma_start(t[:], a[w][:, bass.ds(j * P, P)]).then_inc(rows_in, 16)
                for d in range(2):
                    sp.wait_ge(kinds_ready, j * 2 + d + 1)
                    sp.wait_ge(v_copied, j * 2 + d + 1)
                    for c in range(NT):
                        sp.dma_start(steps[d, STEP_OF[d][c], :, bass.ds(j, 1), :, :].rearrange("p o k t -> p (o k) t"),
                                     kinds[d][:, :, c * P:(c + 1) * P]).then_inc(kinds_out[d], 16)
                sp.wait_ge(gate_read, j + 1)
                sp.dma_start(gate[bass.ds(j, 1), :, :].rearrange("o p n -> p (o n)"), gate_out[:]).then_inc(after_out, 16)
                sp.wait_ge(bonus_read, j + 1)
                sp.dma_start(bonus[bass.ds(j, 1), :, :].rearrange("o p n -> p (o n)"), bonus_out[:]).then_inc(after_out, 16)
                for d in range(2):
                    sp.wait_ge(kinds_out[d], j * 160 + 160)
                sp.wait_ge(after_out, j * 32 + 32)
                sp.sem_inc(tiles_free, 1)

        @block.tensor
        def _(pe):
            pe.wait_ge(low_ready, 2)
            with pe.Fori(0, 4) as j:
                pe.wait_ge(squared, j + 1)
                product(pe, psa, kit.head_ones[:], tmp).then_inc(norm_ps, 1)
                pe.wait_ge(rows_in, j * 96 + 96)
                for d in range(2):
                    half = slice(64 * d, 64 * d + 64)
                    if d:
                        pe.wait_ge(decay_sig, j * 2 + d)
                    product(pe, psb, w2[half, :], wd[half, :]).then_inc(decay_ps, 1)
                    if d:
                        pe.wait_ge(iclr_sig, j * 2 + d)
                    else:
                        pe.wait_ge(norm_read, j + 1)
                    product(pe, psa, a2[half, :], ad[half, :]).then_inc(iclr_ps, 1)
                pe.wait_ge(decay_sig, j * 2 + 2)
                product(pe, psb, g2[:], gd).then_inc(gate_ps, 1)
                pe.wait_ge(rk_ready, j + 1)
                pe.wait_ge(iclr_sig, j * 2 + 2)
                product(pe, psa, kit.head_ones[:], tmp).then_inc(bonus_ps, 1)
                pe.wait_ge(bonus_read, j + 1)
                pe.wait_ge(gate_read, j + 1)

        @block.scalar
        def _(act):
            act.wait_ge(low_in, 64)
            nc.scalar.activation(wd[:], wd[:], ACT.Tanh).then_inc(low_ready, 1)
            nc.scalar.activation(gd[:], gd[:], ACT.Sigmoid).then_inc(low_ready, 1)
            with act.Fori(0, 4) as j:
                act.wait_ge(rows_in, j * 96 + 96)
                act.wait_ge(tiles_free, j + 1)
                for d in range(2):
                    nc.scalar.activation(kinds[d][:, 4, :], v[:], ACT.Copy).then_inc(v_copied, 1)
                act.wait_ge(kk_scaled, j + 1)
                nc.scalar.activation(tmp[:], kk[:], ACT.Square).then_inc(squared, 1)
                act.wait_ge(norm_read, j + 1)
                nc.scalar.activation(q[:], q[:], ACT.Sqrt).then_inc(rooted, 1)
                for d in range(2):
                    act.wait_ge(decay_ps, j * 2 + d + 1)
                    nc.scalar.activation(sig[:], fb, ACT.Sigmoid, bias=kit.cols[:, bass.ds(j + col("w0", 4 * d), 1)]).then_inc(decay_sig, 1)
                    act.wait_ge(iclr_ps, j * 2 + d + 1)
                    if d:
                        act.wait_ge(kinds_ready, j * 2 + d)
                    nc.scalar.activation(iclr[:], fa, ACT.Sigmoid, bias=kit.cols[:, bass.ds(j + col("a0", 4 * d), 1)]).then_inc(iclr_sig, 1)
                    act.wait_ge(q_ready, j * 2 + d + 1)
                    ends = cum[:, P - 1:N:P]
                    for c in range(NT):
                        n = STEP_OF[d][c]
                        nc.scalar.activation(half_decay[:, d, n, bass.ds(j, 1)], ends[:, c:c + 1], ACT.Exp, scale=0.5)
                    for out, src, sign in (((ea, q, 1.0), (eb, q, -1.0), (ec, q2, 1.0)) if d == 0 else
                                           ((ea, q2, -1.0), (eb, q2, 1.0), (ec, q, -1.0))):
                        e = nc.scalar.activation(out[:], src[:], ACT.Exp, scale=sign)
                    e.then_inc(exps, 1)
                act.wait_ge(gate_ps, j + 1)
                act.wait_ge(tiles_free, j + 1)
                nc.scalar.activation(gate_out[:], fb, ACT.Copy).then_inc(gate_read, 1)

        @block.vector
        def _(dve):
            dve.sem_inc(tiles_free, 1)
            k_a = kit.cols[:, col("k_a"):col("k_a") + 4]
            nc.vector.tensor_scalar(ka_rest[:], k_a, -1.0, 1.0, ALU.mult, ALU.add).then_inc(link, 1)
            per = 34
            with dve.Fori(0, 4) as j:
                own = Link(dve, link, j * per + 1)
                par = lambda name: kit.cols[:, bass.ds(j + col(name), 1)]
                dve.wait_ge(tiles_free, j + 1)
                dve.wait_ge(rows_in, j * 96 + 96)
                nc.vector.tensor_scalar(kk[:], k[:], par("k_k"), None, ALU.mult).then_inc(kk_scaled, 1)
                dve.wait_ge(norm_ps, j + 1)
                nc.vector.tensor_scalar(q[:], fa, 1e-12, None, ALU.add).then_inc(norm_read, 1)
                dve.wait_ge(rooted, j + 1)
                own(nc.vector.reciprocal(q[:], q[:]))
                own(nc.vector.tensor_tensor(kk[:], kk[:], q[:], ALU.mult))
                for d in range(2):
                    dve.wait_ge(decay_sig, j * 2 + d + 1)
                    own(nc.vector.tensor_scalar(q2[:], sig[:], -DECAY_SCALE, None, ALU.mult))
                    own(nc.vector.tensor_tensor_scan(cum[:], restart[:], q2[:], 0.0, ALU.mult, ALU.add))
                    chunks = lambda t: t[:, :].rearrange("p (c t) -> p c t", t=P)
                    ends = chunks(cum)[:, :, P - 1:P].broadcast_to((P, NT, P))
                    own(nc.vector.scalar_tensor_tensor(out=chunks(q), in0=ends, scalar=-0.5, in1=chunks(cum), op0=ALU.mult, op1=ALU.add))
                    nc.vector.tensor_tensor(q2[:], q[:], q2[:], ALU.subtract).then_inc(q_ready, 1)
                    dve.wait_ge(iclr_sig, j * 2 + d + 1)
                    own(nc.vector.tensor_scalar(kd[:], iclr[:], par("k_a"), ka_rest[:, bass.ds(j, 1)], ALU.mult, ALU.add))
                    own(nc.vector.tensor_tensor(kd[:], kd[:], k[:], ALU.mult))
                    own(nc.vector.tensor_tensor(iclr[:], iclr[:], kk[:], ALU.mult))
                    if d == 0:
                        own(nc.vector.tensor_copy(kd_sum[:], kd[:]))
                    else:
                        own(nc.vector.tensor_tensor(kd_sum[:], kd_sum[:], kd[:], ALU.add))
                    dve.wait_ge(exps, j * 2 + d + 1)
                    own(nc.vector.scalar_tensor_tensor(out=kinds[d][:, 0, :], in0=kk[:], scalar=-1.0, in1=ec[:], op0=ALU.mult, op1=ALU.mult))
                    own(nc.vector.tensor_tensor(kinds[d][:, 1, :], r[:], ea[:], ALU.mult))
                    own(nc.vector.tensor_tensor(kinds[d][:, 2, :], iclr[:], eb[:], ALU.mult))
                    own(nc.vector.tensor_tensor(kinds[d][:, 3, :], kd[:], eb[:], ALU.mult))
                    dve.sem_inc(kinds_ready, 1)
                nc.vector.scalar_tensor_tensor(out=tmp[:], in0=r[:], scalar=par("r_k"), in1=kd_sum[:], op0=ALU.mult, op1=ALU.mult).then_inc(rk_ready, 1)
                dve.wait_ge(bonus_ps, j + 1)
                nc.vector.tensor_tensor(bonus_out[:], fa, v[:], ALU.mult).then_inc(bonus_read, 1)
                assert own.n <= per, own.n
                for _ in range(per - own.n):
                    dve.sem_inc(link, 1)



LEVELS = 7


def mixing_scan(kit, steps, half_decay, y_out):
    nc, a = kit.nc, kit.args
    with Stage(nc) as st:
        sb = lambda name, shape: st.enter_context(nc.sbuf_tensor(f"ms_{name}", list(shape), F32))
        sem = lambda name: st.sem(f"ms_{name}")
        lanes = range(2)
        units = [(jj, hh) for jj in range(2) for hh in range(2)]
        data = [sb(f"data{d}", (P, 4, KINDS, P)) for d in range(2)]
        y = [sb(f"y{d}", (P, 4, P)) for d in range(2)]
        pair_mask = sb("pair_mask", (P, 2, 2, P))
        level_mask = sb("level_mask", (P, 2, LEVELS, P))
        tok = [sb(f"tok{l}", (P, 2, 3, P)) for l in lanes]
        am = [sb(f"am{l}", (P, 4, 2, 2, P)) for l in lanes]
        lm = [sb(f"lm{l}", (P, LEVELS, 4, P)) for l in lanes]
        t1 = [sb(f"t1{l}", (P, 4, P)) for l in lanes]
        inv = [sb(f"inv{l}", (P, 4, P)) for l in lanes]
        inv_t = [sb(f"inv_t{l}", (P, 4, P)) for l in lanes]
        g = [sb(f"g{l}", (P, 4, 64)) for l in lanes]
        uu = [sb(f"uu{l}", (P, 4, 64)) for l in lanes]
        state = [[sb(f"state{d}{l}", (P, 2, 64)) for l in lanes] for d in range(2)]
        mid = [sb(f"mid{l}", (P, 2, 64)) for l in lanes]
        far = [sb(f"far{l}", (P, 2, 64)) for l in lanes]
        ps = st.enter_context(nc.psum_tensor("ms_ps", [P, 8, BANK], F32))
        bank = lambda l, b: ps[:, 4 * l + b, :]
        masks_in, zeroed, link, y_free = sem("masks_in"), sem("zeroed"), sem("link"), sem("y_free")
        data_in = [sem(f"data_in{d}") for d in range(2)]
        stored = sem("stored")
        lane_sems = lambda name: [sem(f"{name}{l}") for l in lanes]
        (turned, tok_copied, pairs_ps, pairs_masked, level_ready, t1_ps, t1_copied, joined_ps, inv_ready, mid_ready, g_ps,
         g_copied, u_ps, u_copied, y_ps, y_copied, s_ps, state_ready) = (lane_sems(x) for x in (
             "turned", "tok_copied", "pairs_ps", "pairs_masked", "level_ready", "t1_ps", "t1_copied", "joined_ps",
             "inv_ready", "mid_ready", "g_ps", "g_copied", "u_ps", "u_copied", "y_ps", "y_copied", "s_ps", "state_ready"))
        block = st.enter_context(nc.Block("mixing_scan"))

        @block.sync
        def _(sp):
            sp.dma_start(pair_mask[:], a["pair_mask"][:, :, :, :]).then_inc(masks_in, 16)
            sp.dma_start(level_mask[:], a["level_mask"][:, :, :, :]).then_inc(masks_in, 16)
            for d in range(2):
                sp.dma_start(data[d][:], steps[d, 0, :, :, :, :]).then_inc(data_in[d], 16)

            def turn(n, d, last):
                it = n * 2 + d
                for l in lanes:
                    sp.wait_ge(s_ps[l], it + 1)
                if not last:
                    sp.dma_start(data[d][:], steps[d, bass.ds(n + 1, 1), :, :, :, :].rearrange("o p j k t -> p (o j) k t")).then_inc(data_in[d], 16)
                for l in lanes:
                    sp.wait_ge(y_copied[l], it + 2)
                at = bass.ds(n, 1)
                sp.dma_start(y_out[d, at, :, :, :].rearrange("o p j t -> p (o j) t"), y[d][:]).then_inc(stored, 16)
                sp.wait_ge(stored, it * 16 + 16)
                sp.sem_inc(y_free, 1)

            with sp.Fori(0, NT - 1) as n:
                for d in range(2):
                    turn(n, d, False)
            for d in range(2):
                turn(NT - 1, d, True)

        @block.tensor
        def _(pe):
            pe.wait_ge(zeroed, 4)
            with pe.Fori(0, NT) as n:
                for d in range(2):
                    it = n * 2 + d
                    half = lambda hh: slice(64 * hh, 64 * hh + 64)
                    pe.wait_ge(data_in[d], n * 16 + 16)
                    for l in lanes:
                        pe.wait_ge(state_ready[l], it + 1)
                        pe.wait_ge(y_copied[l], it + 1)
                        for jj in range(2):
                            for q in range(3):
                                b, slot = divmod(jj * 3 + q, 4)
                                mm = nc.tensor.transpose(bank(l, b)[:, slot * P:slot * P + P], data[d][:, 2 * l + jj, 2 + q, :], kit.ident[:])
                        mm.then_inc(turned[l], 1)
                    for l in lanes:
                        pe.wait_ge(tok_copied[l], it + 1)
                        for u, (jj, hh) in enumerate(units):
                            for q in range(2):
                                mm = nc.tensor.matmul(bank(l, u)[:, q * 256:q * 256 + 256], data[d][half(hh), 2 * l + jj, 2 + q, :],
                                                      data[d][half(hh), 2 * l + jj, 0:2, :], start=True, stop=True)
                            mm.then_inc(pairs_ps[l], 1)
                    for v in range(LEVELS):
                        for l in lanes:
                            pe.wait_ge(level_ready[l], it * LEVELS + v + 1)
                            if v:
                                pe.wait_ge(inv_ready[l], it * LEVELS + v)
                            for u in range(4):
                                rhs = inv[l][:, u, :] if v else kit.ident[:]
                                mm = nc.tensor.matmul(bank(l, 0)[:, u * P:u * P + P], lm[l][:, v, u, :], rhs, start=True, stop=True)
                            mm.then_inc(t1_ps[l], 1)
                        for l in lanes if v else ():
                            pe.wait_ge(t1_copied[l], it * (LEVELS - 1) + v)
                            for u in range(4):
                                at = slice(u * P, u * P + P)
                                if v < LEVELS - 1:
                                    nc.tensor.matmul(bank(l, 1)[:, at], inv_t[l][:, u, :], t1[l][:, u, :], start=True, stop=True)
                                mm = nc.tensor.matmul(bank(l, 2)[:, at], t1[l][:, u, :], inv_t[l][:, u, :], start=True, stop=True)
                            mm.then_inc(joined_ps[l], 1)
                    for l in lanes:
                        pe.wait_ge(mid_ready[l], it + 1)
                        for u, (jj, hh) in enumerate(units):
                            to = bank(l, (3, 0)[hh])[:, jj * 64:jj * 64 + 64]
                            nc.tensor.matmul(to, data[d][half(hh), 2 * l + jj, 0, :], mid[l][half(hh), jj, :], start=True, stop=False)
                            mm = nc.tensor.matmul(to, am[l][:, u, 1, 0, :], tok[l][:, jj, 2, half(hh)], start=False, stop=True)
                        mm.then_inc(g_ps[l], 1)
                    for l in lanes:
                        pe.wait_ge(g_copied[l], it + 1)
                        pe.wait_ge(inv_ready[l], it * LEVELS + LEVELS)
                        for u in range(4):
                            mm = nc.tensor.matmul(bank(l, 1)[:, u * 64:u * 64 + 64], inv_t[l][:, u, :], g[l][:, u, :], start=True, stop=True)
                        mm.then_inc(u_ps[l], 1)
                    for l in lanes:
                        pe.wait_ge(u_copied[l], it + 1)
                        for u, (jj, hh) in enumerate(units):
                            to = bank(l, 2 + hh)[half(hh), jj * P:jj * P + P]
                            nc.tensor.matmul(to, uu[l][:, u, :], am[l][:, u, 0, 1, :], start=True, stop=False)
                            nc.tensor.matmul(to, tok[l][:, jj, 2, half(hh)], am[l][:, u, 1, 1, :], start=False, stop=False)
                            mm = nc.tensor.matmul(to, mid[l][half(hh), jj, :], data[d][half(hh), 2 * l + jj, 1, :], start=False, stop=True)
                        mm.then_inc(y_ps[l], 1)
                        for u, (jj, hh) in enumerate(units):
                            to = bank(l, 0)[half(hh), jj * 64:jj * 64 + 64]
                            nc.tensor.matmul(to, tok[l][:, jj, 0, half(hh)], uu[l][:, u, :], start=True, stop=False)
                            mm = nc.tensor.matmul(to, tok[l][:, jj, 1, half(hh)], tok[l][:, jj, 2, half(hh)], start=False, stop=True)
                        mm.then_inc(s_ps[l], 1)

        @block.scalar
        def _(act):
            for l in lanes:
                act.sem_inc(y_copied[l], 1)
            with act.Fori(0, NT) as n:
                for d in range(2):
                    it = n * 2 + d
                    for l in lanes:
                        act.wait_ge(turned[l], it + 1)
                        flat = ps[:, 4 * l:4 * l + 2, :].rearrange("p b c -> p (b c)")[:, 0:6 * P]
                        nc.scalar.activation(tok[l][:, :, :, :].rearrange("p j k t -> p (j k t)"), flat, ACT.Copy).then_inc(tok_copied[l], 1)
                    for v in range(1, LEVELS):
                        for l in lanes:
                            act.wait_ge(t1_ps[l], it * LEVELS + v + 1)
                            nc.scalar.activation(t1[l][:, :, :].rearrange("p u t -> p (u t)"), bank(l, 0), ACT.Copy).then_inc(t1_copied[l], 1)
                    for l in lanes:
                        act.wait_ge(g_ps[l], it + 1)
                        for hh in range(2):
                            c = nc.scalar.activation(g[l][:, hh::2, :], bank(l, (3, 0)[hh])[:, 0:P].rearrange("p (j v) -> p j v", v=64), ACT.Copy)
                        c.then_inc(g_copied[l], 1)
                    for l in lanes:
                        act.wait_ge(u_ps[l], it + 1)
                        nc.scalar.activation(uu[l][:, :, :].rearrange("p u v -> p (u v)"), bank(l, 1)[:, 0:256], ACT.Copy).then_inc(u_copied[l], 1)
                    act.wait_ge(y_free, it + 1)
                    for l in lanes:
                        act.wait_ge(y_ps[l], it + 1)
                        for hh in range(2):
                            half = slice(64 * hh, 64 * hh + 64)
                            c = nc.scalar.activation(y[d][half, 2 * l:2 * l + 2, :], bank(l, 2 + hh)[half, 0:256].rearrange("p (j t) -> p j t", t=P), ACT.Copy)
                        c.then_inc(y_copied[l], 1)

        @block.vector
        def _(dve):
            dve.sem_inc(y_free, 2)
            for d in range(2):
                for l in lanes:
                    nc.vector.memset(state[d][l][:], 0.0).then_inc(zeroed, 1)
            dve.wait_ge(zeroed, 4)
            for l in lanes:
                dve.sem_inc(state_ready[l], 1)
            dve.wait_ge(masks_in, 32)
            ident4 = kit.ident[:, :].rearrange("p (o t) -> p o t", o=1).broadcast_to((P, 4, P))
            four = lambda x: x.rearrange("p (u t) -> p u t", t=P)
            with dve.Fori(0, NT) as n:
                for d in range(2):
                    it = n * 2 + d
                    decay = lambda l, jj: half_decay[:, d, bass.ds(n, 1), 2 * l + jj]
                    for l in lanes:
                        for u in range(4):
                            dve.wait_ge(pairs_ps[l], it * 4 + u + 1)
                            m = nc.vector.tensor_tensor(
                                am[l][:, u, :, :, :].rearrange("p q r t -> p q (r t)"), bank(l, u).rearrange("p (q c) -> p q c", q=2),
                                pair_mask[:, d:d + 1, :, :].rearrange("p o r t -> p o (r t)").broadcast_to((P, 2, 2 * P)), ALU.mult)
                        m.then_inc(pairs_masked[l], 1)
                        for jj in range(2):
                            c = nc.vector.tensor_scalar(mid[l][:, jj, :], state[d][l][:, jj, :], decay(l, jj), None, ALU.mult)
                        c.then_inc(mid_ready[l], 1)
                        dve.wait_ge(mid_ready[l], it + 1)
                        for jj in range(2):
                            c = nc.vector.tensor_scalar(far[l][:, jj, :], mid[l][:, jj, :], decay(l, jj), None, ALU.mult)
                        c.then_inc(link, 1)
                    for v in range(LEVELS):
                        for l in lanes:
                            if v == 0:
                                dve.wait_ge(level_ready[l], it * LEVELS + 1)
                                dve.wait_ge(t1_ps[l], it * LEVELS + 1)
                                nc.vector.tensor_tensor(inv[l][:], four(bank(l, 0)), ident4, ALU.add)
                                x = nc.vector.tensor_tensor(inv_t[l][:], lm[l][:, 0, :, :], ident4, ALU.add)
                            else:
                                dve.wait_ge(joined_ps[l], it * (LEVELS - 1) + v)
                                dve.wait_ge(inv_ready[l], it * LEVELS + v)
                                if v < LEVELS - 1:
                                    nc.vector.tensor_tensor(inv[l][:], four(bank(l, 1)), inv[l][:], ALU.add)
                                x = nc.vector.tensor_tensor(inv_t[l][:], four(bank(l, 2)), inv_t[l][:], ALU.add)
                            x.then_inc(inv_ready[l], 1)
                    dve.wait_ge(link, it * 2 + 2)
                    for l in lanes:
                        dve.wait_ge(s_ps[l], it + 1)
                        for jj in range(2):
                            c = nc.vector.scalar_tensor_tensor(out=state[d][l][:, jj, :], in0=bank(l, 0)[:, jj * 64:jj * 64 + 64],
                                                               scalar=decay(l, jj), in1=far[l][:, jj, :], op0=ALU.mult, op1=ALU.add)
                        c.then_inc(state_ready[l], 1)
                        dve.wait_ge(state_ready[l], it + 2)

        @block.gpsimd
        def _(pool):
            pool.wait_ge(masks_in, 32)
            with pool.Fori(0, NT) as n:
                for d in range(2):
                    it = n * 2 + d
                    for l in lanes:
                        pool.wait_ge(pairs_masked[l], it + 1)
                        for v in range(LEVELS):
                            nc.gpsimd.tensor_tensor(lm[l][:, v, :, :], am[l][:, :, 0, 0, :],
                                                    level_mask[:, d, v:v + 1, :].broadcast_to((P, 4, P)), ALU.mult).then_inc(level_ready[l], 1)


LN_EPS = 64e-5


def mixing_out(kit, y_steps, gate, bonus, y_all):
    nc = kit.nc
    with Stage(nc) as st:
        sb = lambda name: st.enter_context(nc.sbuf_tensor(f"mo_{name}", [P, N], F32))
        sem = lambda name: st.sem(f"mo_{name}")
        fwd, bwd, gt, bn, sq, rs = (sb(x) for x in ("fwd", "bwd", "gt", "bn", "sq", "rs"))
        psm = st.enter_context(nc.psum_tensor("mo_psm", [P, 3, BANK], F32))
        psv = st.enter_context(nc.psum_tensor("mo_psv", [P, 3, BANK], F32))
        fm, fv = (x[:, :, :].rearrange("p b c -> p (b c)")[:, 0:N] for x in (psm, psv))
        loaded, link, both, mean_ps, centred, squared, var_ps, var_read, root, scaled, affine, ready, stored, tiles_free = (
            sem(x) for x in ("loaded", "link", "both", "mean_ps", "centred", "squared", "var_ps", "var_read", "root",
                             "scaled", "affine", "ready", "stored", "tiles_free"))
        per_turn = 16 * 13
        block = st.enter_context(nc.Block("mixing_out"))

        @block.sync
        def _(sp):
            with sp.Fori(0, 4) as j:
                sp.wait_ge(tiles_free, j + 1)
                at = bass.ds(j, 1)
                sp.dma_start(fwd[:, :].rearrange("p (n t) -> p n t", t=P), y_steps[0, :, :, at, :].rearrange("n p o t -> p n (o t)")).then_inc(loaded, 16)
                for c in range(NT):
                    sp.dma_start(bwd[:, c * P:(c + 1) * P], y_steps[1, STEP_OF[1][c], :, at, :].rearrange("p o t -> p (o t)")).then_inc(loaded, 16)
                sp.dma_start(gt[:], gate[at, :, :].rearrange("o p n -> p (o n)")).then_inc(loaded, 16)
                sp.dma_start(bn[:], bonus[at, :, :].rearrange("o p n -> p (o n)")).then_inc(loaded, 16)
                sp.wait_ge(ready, j + 1)
                sp.dma_start(y_all[at, :, :].rearrange("o p n -> p (o n)"), fwd[:]).then_inc(stored, 16)
                sp.wait_ge(stored, j * 16 + 16)
                sp.sem_inc(tiles_free, 1)

        @block.tensor
        def _(pe):
            with pe.Fori(0, 4) as j:
                for ready_sem, ps, src, out in ((both, psm, fwd, mean_ps), (squared, psv, sq, var_ps)):
                    pe.wait_ge(ready_sem, j + 1)
                    for n, (s, e) in enumerate(SEGS):
                        mm = nc.tensor.matmul(ps[:, n, 0:e - s], kit.head_ones[:], src[:, s:e], start=True, stop=True)
                    mm.then_inc(out, 1)

        @block.scalar
        def _(act):
            with act.Fori(0, 4) as j:
                act.wait_ge(centred, j + 1)
                nc.scalar.activation(sq[:], fwd[:], ACT.Square).then_inc(squared, 1)
                act.wait_ge(var_read, j + 1)
                nc.scalar.activation(rs[:], rs[:], ACT.Sqrt).then_inc(root, 1)
                act.wait_ge(scaled, j + 1)
                nc.scalar.activation(fwd[:], fwd[:], ACT.Identity, scale=kit.cols[:, bass.ds(j + col("ln_w"), 1)],
                                     bias=kit.cols[:, bass.ds(j + col("ln_b"), 1)]).then_inc(affine, 1)

        @block.vector
        def _(dve):
            dve.sem_inc(tiles_free, 1)
            with dve.Fori(0, 4) as j:
                own = Link(dve, link, j * 2)
                dve.wait_ge(loaded, j * per_turn + per_turn)
                nc.vector.tensor_tensor(fwd[:], fwd[:], bwd[:], ALU.add).then_inc(both, 1)
                dve.wait_ge(mean_ps, j + 1)
                nc.vector.scalar_tensor_tensor(out=fwd[:], in0=fm, scalar=-1.0 / 64, in1=fwd[:], op0=ALU.mult, op1=ALU.add).then_inc(centred, 1)
                dve.wait_ge(var_ps, j + 1)
                nc.vector.tensor_scalar(rs[:], fv, 1.0 / 64, LN_EPS, ALU.mult, ALU.add).then_inc(var_read, 1)
                dve.wait_ge(root, j + 1)
                own(nc.vector.reciprocal(rs[:], rs[:]))
                nc.vector.tensor_tensor(fwd[:], fwd[:], rs[:], ALU.mult).then_inc(scaled, 1)
                dve.wait_ge(affine, j + 1)
                own(nc.vector.tensor_tensor(fwd[:], fwd[:], bn[:], ALU.add))
                nc.vector.tensor_tensor(fwd[:], fwd[:], gt[:], ALU.mult).then_inc(ready, 1)


EXPERTS, GROUPS, MEMBERS = 16, 4, 4
HEADS = 8
QK = 96
Q_RANK, KV_RANK = 256, 128
SCALE = QK ** -0.5


def attention(kit, p, y_all, xb, yb):
    nc, a = kit.nc, kit.args
    with Stage(nc) as st:
        sb = lambda name, shape: st.enter_context(nc.sbuf_tensor(f"at_{name}", list(shape), F32))
        sem = lambda name: st.sem(f"at_{name}")
        pq = sb("pq", (P, 2, N))
        pkv = sb("pkv", (P, N))
        sq = [sb(f"sq{i}", (P, N)) for i in range(2)]
        rs = [sb(f"rs{i}", (P, N)) for i in range(2)]
        raw = [sb(f"raw{i}", (QK, N)) for i in range(2)]
        nrm = [sb(f"nrm{i}", (QK, N)) for i in range(2)]
        rot_sin = sb("rot_sin", (QK, SEQ))
        cos, sin = sb("cos", (QK, SEQ)), sb("sin", (QK, SEQ))
        rot = sb("rot", (QK, QK))
        w_v = sb("w_v", (P, HEADS * 64))
        wq, wk = sb("wq", (P, 2, QK)), sb("wk", (P, 64))
        v_tok, o_tok = sb("v_tok", (P, NT, HEADS * 64)), sb("o_tok", (P, NT, HEADS * 64))
        prob = [sb(f"prob{i}", (P, N)) for i in range(2)]
        prob_t = [sb(f"prob_t{i}", (P, NT, P)) for i in range(2)]
        top, neg_top, total, inv_total = (sb(x, (P, NT)) for x in ("top", "neg_top", "total", "inv_total"))
        eps_col = sb("eps", (P, 1))
        zero = sb("zero", (P, D))
        zeroed, zero_out = sem("zeroed"), sem("zero_out")
        ps = st.enter_context(nc.psum_tensor("at_ps", [P, 8, BANK], F32))
        group = lambda i: ps[:, 3 * i:3 * i + 3, :].rearrange("p b c -> p (b c)")
        turn_bank = lambda i: ps[:, 6 + i % 2, :]
        s_in, w_in, eps_set = sem("s_in"), sem("w_in"), sem("eps_set")
        squared, summed, root, normed = sem("squared"), sem("summed"), sem("root"), sem("normed")
        v_ps, v_copied = sem("v_ps"), sem("v_copied")
        proj, copied, hsq, hsum, hroot, hnorm, hrot, rot_part, roped = (sem(x) for x in (
            "proj", "copied", "hsq", "hsum", "hroot", "hnorm", "hrot", "rot_part", "roped"))
        scores, top_ready, exped, inv_ready, turned, turn_copied, o_ps, o_copied = (sem(x) for x in (
            "scores", "top_ready", "exped", "inv_ready", "turned", "turn_copied", "o_ps", "o_copied"))
        link, y_turned, y_moved, stored = sem("link"), sem("y_turned"), sem("y_moved"), sem("stored")
        keys = [NTC if t < NTC else NT for t in range(NT)]
        turns = [[(s, min(s + 4, k)) for s in range(0, k, 4)] for k in keys]
        per_turns = sum(len(x) for x in turns)

        setup = st.enter_context(ExitStack())
        block = setup.enter_context(nc.Block("attention_inputs"))

        @block.sync
        def _(sp):
            for i in range(2):
                sp.dma_start(pq[:, i, :], p[Q_CH + i, :, :]).then_inc(s_in, 16)
            sp.dma_start(pkv[:], p[KV_CH, :, :]).then_inc(s_in, 16)
            sp.dma_start(raw[1][64:QK, :], p[KR_CH, 0:32, :]).then_inc(s_in, 16)
            for t, name in ((cos, "cos"), (sin, "sin"), (rot, "rot"), (w_v, "w_v")):
                sp.dma_start(t[:], a[name][:, :]).then_inc(s_in, 16)

        @block.scalar
        def _(act):
            act.wait_ge(s_in, 128)
            act.wait_ge(eps_set, 1)
            for i, src in enumerate((pq[:, 0, :], pq[:, 1, :], pkv[:])):
                if i == 2:
                    act.wait_ge(summed, 1)
                nc.scalar.activation(sq[i % 2][:], src, ACT.Square).then_inc(squared, 1)
            nc.scalar.activation(rs[0][64:QK, :], raw[1][64:QK, :], ACT.Square).then_inc(squared, 1)
            for i, rank in enumerate((Q_RANK, KV_RANK)):
                act.wait_ge(summed, 2 + i)
                nc.scalar.activation(prob[i][:], group(i)[:, 0:N], ACT.Ln, scale=1.0 / rank, bias=eps_col[:]).then_inc(root, 1)
                act.wait_ge(root, 2 * i + 1)
                nc.scalar.activation(prob[i][:], prob[i][:], ACT.Exp, scale=-0.5).then_inc(root, 1)
            for t in range(NT):
                act.wait_ge(v_ps, t + 1)
                nc.scalar.activation(v_tok[:, t, :], turn_bank(t), ACT.Copy).then_inc(v_copied, 1)

        @block.tensor
        def _(pe):
            for i in range(3):
                pe.wait_ge(squared, i + 1)
                for n, (s, e) in enumerate(SEGS):
                    mm = nc.tensor.matmul(group(i // 2)[:, s:e], kit.ones[:], sq[i % 2][:, s:e], start=i != 1, stop=i != 0)
                mm.then_inc(summed, 1)
            pe.wait_ge(normed, 3)
            for t in range(NT):
                if t >= 2:
                    pe.wait_ge(v_copied, t - 1)
                nc.tensor.matmul(turn_bank(t), pkv[:, t * P:(t + 1) * P], w_v[:], start=True, stop=True).then_inc(v_ps, 1)

        @block.vector
        def _(dve):
            nc.vector.memset(eps_col[:], EPS).then_inc(eps_set, 1)
            dve.wait_ge(squared, 4)
            dve.wait_ge(summed, 3)
            nc.vector.tensor_copy(sq[1][64:QK, :], rs[0][64:QK, :]).then_inc(link, 1)
            for i, src in enumerate((pq[:, 0, :], pq[:, 1, :], pkv[:])):
                dve.wait_ge(root, 2 if i < 2 else 4)
                nc.vector.scalar_tensor_tensor(out=src, in0=src, scalar=kit.cols[:, col("q_norm", i):][:, 0:1], in1=prob[i // 2][:],
                                               op0=ALU.mult, op1=ALU.mult).then_inc(normed, 1)

        setup.close()
        block = st.enter_context(nc.Block("attention_heads"))
        rows = (QK, 64)

        @block.gpsimd
        def _(pool):
            nc.gpsimd.memset(zero[:], 0.0).then_inc(zeroed, 1)
            pool.wait_ge(zeroed, 1)
            blocks = [xb[s:s + P, :] for s in range(N, xb.shape[0], P)] + [yb[s:s + P, :] for s in range(N + EXPERTS * P, yb.shape[0], P)]
            for b in blocks:
                pool.dma_start(b, zero[:]).then_inc(zero_out, 16)
            pool.wait_ge(zero_out, 16 * len(blocks))

        @block.sync
        def _(sp):
            with sp.Fori(0, HEADS) as h:
                sp.wait_ge(proj, h * 2 + 1)
                sp.dma_start(wq[:], a["w_q"][:, :, bass.ds(h * QK, QK)]).then_inc(w_in, 16)
                sp.dma_start(wk[:], a["w_k"][:, bass.ds(h * 64, 64)]).then_inc(w_in, 16)
            for j in range(4):
                sp.wait_ge(y_moved, 3 * (j + 1))
                sp.dma_start(y_all[4 + j, :, :], (pq[:, 0, :], pq[:, 1, :], pkv[:], prob[0][:])[j]).then_inc(stored, 16)
            sp.wait_ge(stored, 64)

        @block.tensor
        def _(pe):
            pe.sem_inc(proj, 1)
            with pe.Fori(0, HEADS) as h:
                pe.wait_ge(w_in, h * 32 + 32)
                pe.wait_ge(o_copied, h * NT + 1)
                for i in range(2):
                    for n, (s, e) in enumerate(SEGS):
                        if i == 0:
                            for k in range(2):
                                mm = nc.tensor.matmul(group(0)[0:QK, s:e], wq[:, k, :], pq[:, k, s:e], start=k == 0, stop=k == 1)
                        else:
                            mm = nc.tensor.matmul(group(1)[0:64, s:e], wk[:], pkv[:, s:e], start=True, stop=True)
                    mm.then_inc(proj, 1)
                for i in range(2):
                    pe.wait_ge(hsq, h * 2 + i + 1)
                    for n, (s, e) in enumerate(SEGS):
                        mm = nc.tensor.matmul(group(i)[0:QK, s:e], kit.ones[0:QK, 0:QK], sq[i][0:QK, s:e], start=True, stop=True)
                    mm.then_inc(hsum, 1)
                for i in range(2):
                    pe.wait_ge(hnorm, h * 2 + i + 1)
                    for s in range(0, SEQ, BANK):
                        mm = nc.tensor.matmul(group(i)[0:QK, s:s + BANK], rot[:], nrm[i][:, CTX + s:CTX + s + BANK], start=True, stop=True)
                    mm.then_inc(hrot, 1)
                pe.wait_ge(roped, h * 2 + 2)

                def score(t):
                    if t >= 2:
                        pe.wait_ge(o_copied, h * NT + t)
                    q = nrm[0][:, t * P:(t + 1) * P]
                    for s in range(0, keys[t] * P, BANK):
                        e = min(s + BANK, keys[t] * P)
                        mm = nc.tensor.matmul(group(t % 2)[:, s:e], q, nrm[1][:, s:e], start=True, stop=True)
                    mm.then_inc(scores, 1)

                score(0)
                done_turns = 0
                for t in range(NT):
                    if t + 1 < NT:
                        score(t + 1)
                    pe.wait_ge(exped, h * NT + t + 1)
                    for s, e in turns[t]:
                        pe.wait_ge(turn_copied, h * per_turns + done_turns + 1)
                        for k in range(s, e):
                            mm = nc.tensor.transpose(turn_bank(done_turns + 0)[:, (k - s) * P:(k - s + 1) * P],
                                                     prob[t % 2][:, k * P:(k + 1) * P], kit.ident[:])
                        mm.then_inc(turned, 1)
                        done_turns += 1
                    pe.wait_ge(turn_copied, h * per_turns + done_turns + 2)
                    out = group(t % 2)[:, N:N + 64]
                    for k in range(keys[t]):
                        mm = nc.tensor.matmul(out, prob_t[t % 2][:, k, :], v_tok[:, k, bass.ds(h * 64, 64)], start=k == 0, stop=k == keys[t] - 1)
                    mm.then_inc(o_ps, 1)
            pe.wait_ge(o_copied, HEADS * NT + 1)
            for j in range(4):
                for n, (s, e) in enumerate(SEGS):
                    m = j * 3 + n
                    if m >= 2:
                        pe.wait_ge(y_moved, m - 1)
                    for t in range(s // P, e // P):
                        mm = nc.tensor.transpose(turn_bank(m)[:, t * P - s:t * P - s + P], o_tok[:, t, j * P:(j + 1) * P], kit.ident[:])
                    mm.then_inc(y_turned, 1)

        @block.scalar
        def _(act):
            act.sem_inc(o_copied, 1)
            with act.Fori(0, HEADS) as h:
                for i in range(2):
                    act.wait_ge(proj, h * 2 + i + 2)
                    nc.scalar.activation(raw[i][0:rows[i], :], group(i)[0:rows[i], 0:N], ACT.Copy).then_inc(copied, 1)
                    nc.scalar.activation(sq[i][0:rows[i], :], group(i)[0:rows[i], 0:N], ACT.Square).then_inc(hsq, 1)
                for i in range(2):
                    act.wait_ge(hsum, h * 2 + i + 1)
                    nc.scalar.activation(rs[i][0:QK, :], group(i)[0:QK, 0:N], ACT.Ln, scale=1.0 / QK, bias=eps_col[0:QK, :]).then_inc(hroot, 1)
                    act.wait_ge(hroot, h * 4 + 2 * i + 1)
                    nc.scalar.activation(rs[i][0:QK, :], rs[i][0:QK, :], ACT.Exp, scale=-0.5).then_inc(hroot, 1)

                def drain(t):
                    act.wait_ge(o_ps, h * NT + t + 1)
                    act.wait_ge(inv_ready, h * NT + t + 1)
                    nc.scalar.activation(o_tok[:, t, bass.ds(h * 64, 64)], group(t % 2)[:, N:N + 64], ACT.Copy,
                                         scale=inv_total[:, t:t + 1]).then_inc(o_copied, 1)

                for t in range(NT):
                    if t >= 2:
                        drain(t - 2)
                    act.wait_ge(top_ready, h * NT + t + 1)
                    width = keys[t] * P
                    nc.scalar.activation(prob[t % 2][:, 0:width], group(t % 2)[:, 0:width], ACT.Exp, scale=SCALE,
                                         bias=neg_top[:, t:t + 1], accum_out=total[:, t:t + 1]).then_inc(exped, 1)
                drain(NT - 2)
                drain(NT - 1)

        @block.vector
        def _(dve):
            dve.sem_inc(turn_copied, 2)
            with dve.Fori(0, HEADS) as h:
                own = Link(dve, link, h * 22 + 1)
                for i in range(2):
                    dve.wait_ge(copied, h * 2 + i + 1)
                    dve.wait_ge(hroot, h * 4 + 2 * i + 2)
                    nc.vector.scalar_tensor_tensor(out=nrm[i][:], in0=raw[i][:], scalar=kit.cols[0:QK, col("q_gain", i):][:, 0:1],
                                                   in1=rs[i][0:QK, :], op0=ALU.mult, op1=ALU.mult).then_inc(hnorm, 1)
                for i in range(2):
                    dve.wait_ge(hrot, h * 2 + i + 1)
                    nc.vector.tensor_tensor(rot_sin[:], group(i)[0:QK, 0:SEQ], sin[:], ALU.mult).then_inc(rot_part, 1)
                    own(nc.vector.tensor_tensor(nrm[i][:, CTX:], nrm[i][:, CTX:], cos[:], ALU.mult))
                    dve.wait_ge(rot_part, h * 2 + i + 1)
                    nc.vector.tensor_tensor(nrm[i][:, CTX:], nrm[i][:, CTX:], rot_sin[:], ALU.add).then_inc(roped, 1)
                    dve.wait_ge(roped, h * 2 + i + 1)

                def tops(t):
                    dve.wait_ge(scores, h * NT + t + 1)
                    own(nc.vector.reduce_max(top[:, t:t + 1], group(t % 2)[:, 0:keys[t] * P], AX.X))
                    nc.vector.tensor_scalar(neg_top[:, t:t + 1], top[:, t:t + 1], -SCALE, None, ALU.mult).then_inc(top_ready, 1)

                tops(0)
                m = 0
                for t in range(NT):
                    if t + 1 < NT:
                        tops(t + 1)
                    dve.wait_ge(exped, h * NT + t + 1)
                    nc.vector.reciprocal(inv_total[:, t:t + 1], total[:, t:t + 1]).then_inc(inv_ready, 1)
                    for s, e in turns[t]:
                        dve.wait_ge(turned, h * per_turns + m + 1)
                        nc.vector.tensor_copy(prob_t[t % 2][:, s:e, :], turn_bank(m)[:, 0:(e - s) * P].rearrange("p (k t) -> p k t", t=P)).then_inc(turn_copied, 1)
                        m += 1
                for _ in range(22 - own.n):
                    dve.sem_inc(link, 1)
            for j in range(4):
                for n, (s, e) in enumerate(SEGS):
                    dve.wait_ge(y_turned, j * 3 + n + 1)
                    nc.vector.tensor_copy((pq[:, 0, :], pq[:, 1, :], pkv[:], prob[0][:])[j][:, s:e], turn_bank(j * 3 + n)[:, 0:e - s]).then_inc(y_moved, 1)


def project_out(kit, name, y, weights, x, gate, lo, load_y=None, load_x=None):
    nc = kit.nc
    parts = [q for q in PARTS if q[1] > lo]
    segs = list(SEGS) if lo == 0 else [(lo, lo + 512), (lo + 512, N)]
    with Stage(nc) as st:
        sem = lambda s: st.sem(f"{name}_{s}")
        w = [st.enter_context(nc.sbuf_tensor(f"{name}_w{u}", [P, KD, P], F32)) for u in range(2)]
        ps = [st.enter_context(nc.psum_tensor(f"{name}_ps{u}", [P, 3, BANK], F32)) for u in range(2)]
        w_in = [sem(f"w_in{u}") for u in range(2)]
        y_in, x_in, multiplied, added = sem("y_in"), sem("x_in"), sem("multiplied"), sem("added")
        block = st.enter_context(nc.Block(name))

        @block.sync
        def _(sp):
            if load_y is not None:
                for k in range(KD):
                    sp.dma_start(y[:, k, :], load_y[k, :, :]).then_inc(y_in, 16)
            if load_x is not None:
                for k in range(KD):
                    for s, e, v in parts:
                        sp.dma_start(x[:, k, s:e], load_x[v][k * P:(k + 1) * P, :]).then_inc(x_in, 16)
            with sp.Fori(0, KD // 2) as i:
                for u in range(2):
                    sp.wait_ge(multiplied, free(i * 2 + u))
                    sp.dma_start(w[u][:], weights[:, :, bass.ds(i * 256 + u * P, P)]).then_inc(w_in[u], 16)

        @block.tensor
        def _(pe):
            pe.sem_inc(multiplied, 2)
            if load_y is not None:
                pe.wait_ge(y_in, 16 * KD)
            with pe.Fori(0, KD // 2) as i:
                for u in range(2):
                    pe.wait_ge(w_in[u], i * 16 + 16)
                    pe.wait_ge(added, free(i * 2 + u))
                    for n, (s, e) in enumerate(segs):
                        for k in range(KD):
                            mm = nc.tensor.matmul(ps[u][:, n, 0:e - s], w[u][:, k, :], y[:, k, s:e], start=k == 0, stop=k == KD - 1)
                    mm.then_inc(multiplied, 1)

        @block.vector
        def _(dve):
            dve.sem_inc(added, 2)
            if load_x is not None:
                dve.wait_ge(x_in, 16 * KD * len(parts))
            with dve.Fori(0, KD // 2) as i:
                for u in range(2):
                    dve.wait_ge(multiplied, done(i * 2 + u))
                    m = i * 2 + u
                    flat = ps[u][:, :, :].rearrange("p b c -> p (b c)")
                    for s, e, v in parts:
                        here = x[:, bass.ds(m, 1), s:e].rearrange("p o n -> p (o n)")
                        t = nc.vector.scalar_tensor_tensor(out=here, in0=flat[:, s - lo:e - lo], scalar=kit.mod[:, bass.ds(m + gate, 1), v],
                                                           in1=here, op0=ALU.mult, op1=ALU.add)
                    t.then_inc(added, 1)


def fourier(kit, h, f):
    nc, a = kit.nc, kit.args
    lat = SEQ // P
    with Stage(nc) as st:
        sb = lambda name, shape: st.enter_context(nc.sbuf_tensor(f"ft_{name}", list(shape), F32))
        sem = lambda name: st.sem(f"ft_{name}")
        chan = sb("chan", (P, 2 * P))
        pos = sb("pos", (P, 2, lat, SEQ))
        mid = [sb(f"mid{u}", (P, lat, 2 * P)) for u in range(2)]
        ps_c = [st.enter_context(nc.psum_tensor(f"ft_psc{u}", [P, 2, 2 * P], F32)) for u in range(2)]
        ps_f = [st.enter_context(nc.psum_tensor(f"ft_psf{u}", [P, 2, BANK], F32)) for u in range(2)]
        tables_in, chan_ps, mid_kept, f_ps, f_kept = sem("tables_in"), sem("chan_ps"), sem("mid_kept"), sem("f_ps"), sem("f_kept")
        block = st.enter_context(nc.Block("fourier"))

        @block.sync
        def _(sp):
            sp.dma_start(chan[:], a["dft_chan"][:, :]).then_inc(tables_in, 16)
            for q in range(2):
                sp.dma_start(pos[:, q, :, :], a["dft_pos"][:, q, :, :]).then_inc(tables_in, 16)

        @block.tensor
        def _(pe):
            def channels(g):
                for t2 in range(lat // 2):
                    m = g * 4 + t2
                    if m >= 2:
                        pe.wait_ge(mid_kept, m - 1)
                    for t in range(2):
                        s = CTX + (2 * t2 + t) * P
                        mm = nc.tensor.matmul(ps_c[m % 2][:, t, :], h[:, g, s:s + P], chan[:], start=True, stop=True)
                    mm.then_inc(chan_ps, 1)

            pe.wait_ge(tables_in, 48)
            channels(0)
            for g in range(KD):
                if g + 1 < KD:
                    channels(g + 1)
                pe.wait_ge(mid_kept, g * 4 + 4)
                if g >= 2:
                    pe.wait_ge(f_kept, g - 1)
                for n in range(2):
                    for q in range(2):
                        for t in range(lat):
                            mm = nc.tensor.matmul(ps_f[g % 2][:, n, :], mid[g % 2][:, t, q * P:(q + 1) * P], pos[:, q, t, n * BANK:(n + 1) * BANK],
                                                  start=q == 0 and t == 0, stop=q == 1 and t == lat - 1)
                mm.then_inc(f_ps, 1)

        @block.vector
        def _(dve):
            for g in range(KD):
                if g >= 2:
                    dve.wait_ge(f_ps, g - 1)
                for t2 in range(lat // 2):
                    m = g * 4 + t2
                    dve.wait_ge(chan_ps, m + 1)
                    nc.vector.tensor_copy(mid[g % 2][:, 2 * t2:2 * t2 + 2, :], ps_c[m % 2][:]).then_inc(mid_kept, 1)

        @block.scalar
        def _(act):
            for g in range(KD):
                act.wait_ge(f_ps, g + 1)
                nc.scalar.activation(f[:, g, CTX:], ps_f[g % 2][:, :, :].rearrange("p n c -> p (n c)"), ACT.Copy).then_inc(f_kept, 1)


FF = 512
KF = FF // P


def slots(n_tok):
    return 2 * n_tok // P + EXPERTS


def route(kit, name, h, lo, xb, where, weight, table):
    nc, a = kit.nc, kit.args
    n_tok = N - lo
    T = n_tok // P
    NB = slots(n_tok)
    with Stage(nc) as st:
        sb = lambda s, shape, dt=F32: st.enter_context(nc.sbuf_tensor(f"{name}_{s}", list(shape), dt))
        sem = lambda s: st.sem(f"{name}_{s}")
        rw = sb("rw", (P, KD, EXPERTS))
        rb = sb("rb", (P, EXPERTS))
        earlier = sb("earlier", (P, P))
        order = sb("order", (P, 64))
        rows = [sb(f"rows{u}", (P, D)) for u in range(T)]
        sc, sel = sb("sc", (P, T, EXPERTS)), sb("sel", (P, T, EXPERTS))
        big = lambda s: sb(s, (P, T, EXPERTS))
        rank, cmp_, first, second, both, pos, slot, tmp = (big(s) for s in ("rank", "cmp", "first", "second", "both", "pos", "slot", "tmp"))
        pair = sb("pair", (P, T, GROUPS))
        gs, grank, gcmp, ghot = (sb(s, (P, T, GROUPS)) for s in ("gs", "grank", "gcmp", "ghot"))
        tile_sum = sb("tile_sum", (P, T, EXPERTS))
        count, blocks_e, start, end = (sb(s, (P, EXPERTS)) for s in ("count", "blocks_e", "start", "end"))
        over = sb("over", (P, EXPERTS, T + 1))
        of_block = sb("of_block", (P, NB, EXPERTS))
        tab = sb("tab", (P, 4, 64))
        even = sb("even", (P, NB // 2))
        total = sb("total", (P, T))
        where_f = sb("where_f", (P, 2, T))
        ps_s = st.enter_context(nc.psum_tensor(f"{name}_pss", [P, T, EXPERTS], F32))
        ps_e = st.enter_context(nc.psum_tensor(f"{name}_pse", [P, T, EXPERTS], F32))
        ps_t = st.enter_context(nc.psum_tensor(f"{name}_pst", [P, T, EXPERTS], F32))
        ps_r = [st.enter_context(nc.psum_tensor(f"{name}_psr{u}", [P, 2, BANK], F32)) for u in range(2)]
        s_in, scored, scores_ready, link, masks_ready, counted, routed, row_ps, row_kept, stored, scattered = (
            sem(s) for s in ("s_in", "scored", "scores_ready", "link", "masks_ready", "counted", "routed", "row_ps", "row_kept",
                             "stored", "scattered"))
        block = st.enter_context(nc.Block(name))

        @block.sync
        def _(sp):
            sp.dma_start(rw[:], a["router_w"][:, :, :]).then_inc(s_in, 16)
            sp.dma_start(rb[:], a["router_b"][:, :]).then_inc(s_in, 16)
            sp.dma_start(earlier[:], a["earlier"][:, :]).then_inc(s_in, 16)
            sp.dma_start(order[:], a["order"][:, :]).then_inc(s_in, 16)
            for t in range(T):
                sp.wait_ge(row_kept, t + 1)
                sp.dma_start(xb[t * P:(t + 1) * P, :], rows[t][:]).then_inc(stored, 16)
            sp.wait_ge(stored, 16 * T)

        @block.tensor
        def _(pe):
            pe.wait_ge(s_in, 64)
            for t in range(T):
                for k in range(KD):
                    mm = nc.tensor.matmul(ps_s[:, t, :], h[:, k, lo + t * P:lo + (t + 1) * P], rw[:, k, :], start=k == 0, stop=k == KD - 1)
            mm.then_inc(scored, 1)
            for t in range(T):
                if t >= 2:
                    pe.wait_ge(row_kept, t - 1)
                for k in range(KD):
                    mm = nc.tensor.transpose(ps_r[t % 2][:, k // 4, (k % 4) * P:(k % 4 + 1) * P], h[:, k, lo + t * P:lo + (t + 1) * P], kit.ident[:])
                mm.then_inc(row_ps, 1)
            pe.wait_ge(masks_ready, 1)
            nc.tensor.matmul(ps_e[:], earlier[:], both[:], start=True, stop=True)
            nc.tensor.matmul(ps_t[:], kit.ones[:], both[:], start=True, stop=True).then_inc(counted, 1)

        @block.scalar
        def _(act):
            act.wait_ge(scored, 1)
            nc.scalar.activation(sc[:], ps_s[:], ACT.Sigmoid).then_inc(scores_ready, 1)
            for t in range(T):
                act.wait_ge(row_ps, t + 1)
                nc.scalar.activation(rows[t][:], ps_r[t % 2][:, :, :].rearrange("p b c -> p (b c)"), ACT.Copy).then_inc(row_kept, 1)

        @block.vector
        def _(dve):
            own = Link(dve, link)
            tt = lambda out, x, y, op: own(nc.vector.tensor_tensor(out, x, y, op))
            grouped = lambda x: x[:, :, :].rearrange("p t (g e) -> p (t g) e", e=MEMBERS)
            dve.wait_ge(s_in, 64)
            dve.wait_ge(scores_ready, 1)
            tt(sel[:], sc[:], rb[:, :].rearrange("p (o e) -> p o e", o=1).broadcast_to((P, T, EXPERTS)), ALU.add)
            s4, g1 = grouped(sel), gs[:, :, :].rearrange("p t (g o) -> p (t g) o", o=1)
            p1 = pair[:, :, :].rearrange("p t (g o) -> p (t g) o", o=1)
            pairs = [(i, j) for i in range(MEMBERS) for j in range(i + 1, MEMBERS)]
            for n, (i, j) in enumerate(pairs):
                tt(p1 if n else g1, s4[:, :, i:i + 1], s4[:, :, j:j + 1], ALU.add)
                if n:
                    tt(g1, g1, p1, ALU.max)
            own(nc.vector.memset(grank[:], 0.0))
            for i in range(GROUPS):
                for j in range(GROUPS):
                    if i != j:
                        tt(gcmp[:, :, i:i + 1], gs[:, :, j:j + 1], gs[:, :, i:i + 1], ALU.is_ge if j < i else ALU.is_gt)
                        tt(grank[:, :, i:i + 1], grank[:, :, i:i + 1], gcmp[:, :, i:i + 1], ALU.add)
            own(nc.vector.tensor_scalar(ghot[:], grank[:], 0.0, None, ALU.is_equal))
            own(nc.vector.memset(rank[:], 0.0))
            r4, c4 = grouped(rank), grouped(cmp_)
            for i in range(MEMBERS):
                for j in range(MEMBERS):
                    if i != j:
                        tt(c4[:, :, i:i + 1], s4[:, :, j:j + 1], s4[:, :, i:i + 1], ALU.is_ge if j < i else ALU.is_gt)
                        tt(r4[:, :, i:i + 1], r4[:, :, i:i + 1], c4[:, :, i:i + 1], ALU.add)
            gh = ghot[:, :, :].rearrange("p t (g o) -> p (t g) o", o=1).broadcast_to((P, T * GROUPS, MEMBERS))
            for out, which in ((first, 0.0), (second, 1.0)):
                own(nc.vector.tensor_scalar(out[:], rank[:], which, None, ALU.is_equal))
                tt(grouped(out), grouped(out), gh, ALU.mult)
            nc.vector.tensor_tensor(both[:], first[:], second[:], ALU.add).then_inc(masks_ready, 1)
            for i, m in enumerate((first, second)):
                tt(tmp[:], sc[:], m[:], ALU.mult)
                own(nc.vector.reduce_sum(weight[:, i, :], tmp[:], AX.X))
            tt(total[:], weight[:, 0, :], weight[:, 1, :], ALU.add)
            own(nc.vector.reciprocal(total[:], total[:]))
            for i in range(2):
                tt(weight[:, i, :], weight[:, i, :], total[:], ALU.mult)
            dve.wait_ge(counted, 1)
            own(nc.vector.tensor_copy(tile_sum[:], ps_t[:]))
            own(nc.vector.memset(count[:], 0.0))
            for t in range(T):
                tt(pos[:, t, :], ps_e[:, t, :], count[:], ALU.add)
                tt(count[:], count[:], tile_sum[:, t, :], ALU.add)
            full = order[:, 1:T + 1].rearrange("p (o m) -> p o m", o=1).broadcast_to((P, EXPERTS, T))
            own(nc.vector.scalar_tensor_tensor(out=over[:, :, 0:T], in0=full, scalar=float(P),
                                               in1=count[:, :].rearrange("p (e o) -> p e o", o=1).broadcast_to((P, EXPERTS, T)),
                                               op0=ALU.mult, op1=ALU.is_lt))
            own(nc.vector.reduce_sum(blocks_e[:], over[:, :, 0:T], AX.X))
            own(nc.vector.tensor_scalar(blocks_e[:], blocks_e[:], 1.0, None, ALU.add))
            own(nc.vector.tensor_tensor_scan(end[:], kit.ones[:, 0:EXPERTS], blocks_e[:], 0.0, ALU.mult, ALU.add))
            tt(start[:], end[:], blocks_e[:], ALU.subtract)
            own(nc.vector.tensor_scalar(start[:], start[:], float(P), float(n_tok), ALU.mult, ALU.add))
            tt(slot[:], pos[:], start[:, :].rearrange("p (o e) -> p o e", o=1).broadcast_to((P, T, EXPERTS)), ALU.add)
            for i, m in enumerate((first, second)):
                tt(tmp[:], slot[:], m[:], ALU.mult)
                own(nc.vector.reduce_sum(where_f[:, i, :], tmp[:], AX.X))
            nc.vector.tensor_copy(where[:], where_f[:]).then_inc(routed, 1)
            own(nc.vector.tensor_tensor(of_block[:], end[:, :].rearrange("p (o e) -> p o e", o=1).broadcast_to((P, NB, EXPERTS)),
                                        order[:, 0:NB].rearrange("p (b o) -> p b o", o=1).broadcast_to((P, NB, EXPERTS)), ALU.is_le))
            own(nc.vector.memset(tab[:], 0.0))
            own(nc.vector.reduce_sum(tab[:, 0, 0:NB], of_block[:], AX.X))
            own(nc.vector.tensor_scalar(tab[:, 0, 0:NB], tab[:, 0, 0:NB], float(EXPERTS - 1), None, ALU.min))
            own(nc.vector.tensor_scalar(of_block[:], order[:, 0:2 * EXPERTS:2].rearrange("p (o e) -> p o e", o=1).broadcast_to((P, NB, EXPERTS)), 0.0, None, ALU.add))
            own(nc.vector.tensor_tensor(of_block[:], of_block[:], tab[:, 0, 0:NB].rearrange("p (b o) -> p b o", o=1).broadcast_to((P, NB, EXPERTS)), ALU.is_equal))
            own(nc.vector.reduce_sum(tab[:, 1, 1:NB + 1], of_block[:], AX.X))
            own(nc.vector.tensor_scalar(tab[:, 3, 0:NB], tab[:, 0, 0:NB], 0.5, 0.5, ALU.mult, ALU.add))
            own(nc.vector.scalar_tensor_tensor(out=tab[:, 3, 0:NB], in0=tab[:, 1, 1:NB + 1], scalar=0.5, in1=tab[:, 3, 0:NB], op0=ALU.mult, op1=ALU.add))
            own(nc.vector.scalar_tensor_tensor(out=tab[:, 2, 0:NB], in0=tab[:, 1, 1:NB + 1], scalar=-1.0, in1=tab[:, 3, 0:NB], op0=ALU.mult, op1=ALU.add))
            own(nc.vector.tensor_scalar(tab[:, 2, 0:NB], tab[:, 2, 0:NB], 1.0, None, ALU.add))
            own(nc.vector.tensor_scalar(tab[:, 0, 50:64], end[:, 0:14], float(T), None, ALU.add))
            own(nc.vector.memset(tab[:, 0, 49:50], float(T)))
            own(nc.vector.tensor_tensor(even[:], order[:, 0:NB:2], end[:, EXPERTS - 1:EXPERTS].broadcast_to((P, NB // 2)), ALU.is_lt))
            own(nc.vector.reduce_sum(tab[:, 0, 48:49], even[:], AX.X))
            own(nc.vector.tensor_scalar(tab[:, 2:4, 0:NB], tab[:, 2:4, 0:NB], 48.0, None, ALU.mult))
            own(nc.vector.tensor_copy(table[:], tab[:]))

        @block.gpsimd
        def _(pool):
            pool.wait_ge(routed, 1)
            for t in range(T):
                pool.wait_ge(row_kept, t + 1)
                for i in range(2):
                    pool.indirect_dma_start(xb[:, :], bass.IndirectOffsetOnAxis(ap=where[:, i, t:t + 1], axis=0), rows[t][:], None).then_inc(scattered, 16)
            pool.wait_ge(scattered, 32 * T)


def experts(kit, name, layer, n_tok, xb, yb, table):
    nc, a = kit.nc, kit.args
    T, NB = n_tok // P, slots(n_tok)
    G_AT, U_AT, D_AT = 0, KD * FF, 2 * KD * FF
    with Stage(nc) as st:
        sb = lambda s, shape, dt=F32: st.enter_context(nc.sbuf_tensor(f"{name}_{s}", list(shape), dt))
        sem = lambda s: st.sem(f"{name}_{s}")
        psum = lambda s, b: st.enter_context(nc.psum_tensor(f"{name}_{s}", [P, b * BANK], F32))
        w = sb("w", (P, 2, 2 * KD * FF + KF * D))
        x_row = [sb(f"x_row{u}", (P, D)) for u in range(2)]
        y_row = [sb(f"y_row{u}", (P, D)) for u in range(2)]
        xt, act_g, hid, hid_t = sb("xt", (P, KD, P)), sb("act_g", (P, FF)), sb("hid", (P, FF)), sb("hid_t", (P, KF, P))
        spare = sb("spare", (P, 2, 64))
        ps_x, ps_g, ps_u, ps_h, ps_y = psum("psx", 2), psum("psg", 1), psum("psu", 1), psum("psh", 1), psum("psy", 2)
        w_in = [sem(f"w_in{u}") for u in range(2)]
        x_in = [sem(f"x_in{u}") for u in range(2)]
        y_stored = [sem(f"y_stored{u}") for u in range(2)]
        x_turned, x_copied_a, x_copied_v, gate_ps, up_ps, gated, hidden, h_turned, h_copied, y_ps, y_copied_a, y_copied_v = (
            sem(s) for s in ("x_turned", "x_copied_a", "x_copied_v", "gate_ps", "up_ps", "gated", "hidden", "h_turned",
                             "h_copied", "y_ps", "y_copied_a", "y_copied_v"))
        block = st.enter_context(nc.Block(name))
        names = ("gate", "up", "down")
        places = (G_AT, U_AT, D_AT)
        pairs_of = lambda eng: eng.value_load(table[0:1, 0, 48:49], min_val=EXPERTS // 2, max_val=NB // 2)

        @block.sync
        def _(sp):
            def load(buf, sources):
                for src, at, k in zip(sources, places, (KD, KD, KF)):
                    dst = w[:, buf, at:at + 4096].rearrange("p (k f) -> p k f", k=k)
                    sp.dma_start(dst, src.rearrange("(k p) f -> p k f", p=P)).then_inc(w_in[buf], 16)

            def expert(e):
                return [a[f"moe_{n}"][layer, bass.ds(e, 1), :, :].rearrange("o k f -> (o k) f") for n in names]

            load(0, [a[f"shared_{n}"][layer, :, :] for n in names])
            load(1, [a[f"moe_{n}"][layer, 0, :, :] for n in names])
            with sp.Fori(0, EXPERTS // 2 - 1) as i:
                for u in range(2):
                    e = i * 2 + (u + 1)
                    ready = sp.value_load(table[0:1, 0, bass.ds(i * 2 + (49 + u), 1)], min_val=1, max_val=T + NB)
                    sp.wait_ge(y_ps, ready)
                    load(u, expert(e))
            ready = sp.value_load(table[0:1, 0, 63:64], min_val=1, max_val=T + NB)
            sp.wait_ge(y_ps, ready)
            load(0, expert(EXPERTS - 1))

        @block.tensor
        def _(pe):
            wt = lambda buf, at: (w[:, buf, at:at + BANK] if isinstance(buf, int) else
                                  w[:, bass.ds(buf, 1), at:at + BANK].rearrange("p o f -> p (o f)"))

            def turn_x(m, u, i2):
                pe.wait_ge(x_in[u], i2 * 16 + 16)
                for k in range(KD):
                    mm = nc.tensor.transpose(ps_x[:, k * P:(k + 1) * P], x_row[u][:, k * P:(k + 1) * P], kit.ident[:])
                mm.then_inc(x_turned, 1)

            def gate_up(m, buf):
                pe.wait_ge(x_copied_a, m + 1)
                pe.wait_ge(x_copied_v, m + 1)
                for ps, at, sem_ in ((ps_g, G_AT, gate_ps), (ps_u, U_AT, up_ps)):
                    for k in range(KD):
                        mm = nc.tensor.matmul(ps[:], xt[:, k, :], wt(buf, at + k * FF), start=k == 0, stop=k == KD - 1)
                    mm.then_inc(sem_, 1)

            def down(m, buf):
                pe.wait_ge(h_copied, m + 1)
                pe.wait_ge(y_copied_a, m + 1)
                pe.wait_ge(y_copied_v, m + 1)
                for n in range(2):
                    for k in range(KF):
                        mm = nc.tensor.matmul(ps_y[:, n * BANK:(n + 1) * BANK], hid_t[:, k, :], wt(buf, D_AT + k * D + n * BANK), start=k == 0, stop=k == KF - 1)
                mm.then_inc(y_ps, 1)

            def turn_h(m):
                pe.wait_ge(hidden, m + 1)
                for k in range(KF):
                    mm = nc.tensor.transpose(ps_h[:, k * P:(k + 1) * P], hid[:, k * P:(k + 1) * P], kit.ident[:])
                mm.then_inc(h_turned, 1)

            pe.wait_ge(w_in[0], 48)
            turn_x(0, 0, 0)
            gate_up(0, 0)
            turn_x(1, 1, 0)
            turn_h(0)
            gate_up(1, 0)
            turn_x(2, 0, 1)
            down(0, 0)
            turn_h(1)
            with pe.Fori(1, T // 2) as i:
                for u in range(2):
                    m = i * 2 + u
                    gate_up(m, 0)
                    turn_x(m + 1, 1 - u, i + u)
                    down(m - 1, 0)
                    turn_h(m)
            with pe.Fori(0, pairs_of(pe)) as i:
                for u in range(2):
                    b = i * 2 + u
                    m = b + T
                    before = pe.value_load(table[0:1, 1, bass.ds(b, 1)], min_val=0, max_val=1)
                    buf = pe.value_load(table[0:1, 1, bass.ds(b + 1, 1)], min_val=0, max_val=1)
                    for q in range(2):
                        loads = pe.value_load(table[0:1, 2 + q, bass.ds(b, 1)], min_val=48, max_val=48 * 9)
                        pe.wait_ge(w_in[q], loads)
                    gate_up(m, buf)
                    turn_x(m + 1, 1 - u, i + (T // 2 + u))
                    down(m - 1, before)
                    turn_h(m)
            pairs = pairs_of(pe)
            last = pe.value_load(table[0:1, 1, bass.ds(pairs * 2, 1)], min_val=0, max_val=1)
            down(pairs * 2 + (T - 1), last)

        @block.scalar
        def _(act):
            act.sem_inc(y_copied_a, 1)
            for u in range(2):
                act.dma_start(x_row[u][:], xb[u * P:(u + 1) * P, :]).then_inc(x_in[u], 16)
                act.dma_start(spare[:, u, :], a["order"][:, :]).then_inc(y_stored[u], 16)

            def next_x(m, u):
                act.wait_ge(x_turned, m + 1)
                act.dma_start(x_row[u][:], xb[bass.ds(m * P + 2 * P, P), :]).then_inc(x_in[u], 16)
                nc.scalar.activation(xt[:, 4:8, :], ps_x[:, BANK:2 * BANK].rearrange("p (k t) -> p k t", t=P), ACT.Copy).then_inc(x_copied_a, 1)

            def silu(m):
                act.wait_ge(gate_ps, m + 1)
                nc.scalar.activation(act_g[:], ps_g[:], ACT.Silu).then_inc(gated, 1)

            def y_half(m, u, i2):
                act.wait_ge(y_ps, m + 1)
                act.wait_ge(y_stored[u], i2 * 16 + 16)
                nc.scalar.activation(y_row[u][:, BANK:], ps_y[:, BANK:], ACT.Copy).then_inc(y_copied_a, 1)
                act.wait_ge(y_copied_a, m + 2)
                act.wait_ge(y_copied_v, m + 2)
                act.dma_start(yb[bass.ds(m * P, P), :], y_row[u][:]).then_inc(y_stored[u], 16)

            next_x(0, 0)
            silu(0)
            next_x(1, 1)
            silu(1)
            next_x(2, 0)
            y_half(0, 0, 0)

            def rest(first, end):
                with act.Fori(first, end) as i:
                    for u in range(2):
                        m = i * 2 + u
                        silu(m)
                        next_x(m + 1, 1 - u)
                        y_half(m - 1, 1 - u, i - (1 - u))

            rest(1, pairs_of(act) + T // 2)
            pairs = pairs_of(act)
            y_half(pairs * 2 + (T - 1), 1, pairs + (T // 2 - 1))

        @block.gpsimd
        def _(pool):
            pairs = pairs_of(pool)
            for u in range(2):
                pool.wait_ge(y_stored[u], pairs * 16 + 16 * (T // 2 + 1))
                pool.wait_ge(x_in[u], pairs * 16 + 16 * (T // 2 + 1 + (1 - u)))

        @block.vector
        def _(dve):
            dve.sem_inc(y_copied_v, 1)

            def next_x(m):
                dve.wait_ge(x_turned, m + 1)
                nc.vector.tensor_copy(xt[:, 0:4, :], ps_x[:, 0:BANK].rearrange("p (k t) -> p k t", t=P)).then_inc(x_copied_v, 1)

            def product(m):
                dve.wait_ge(gated, m + 1)
                dve.wait_ge(up_ps, m + 1)
                nc.vector.tensor_tensor(hid[:], act_g[:], ps_u[:], ALU.mult).then_inc(hidden, 1)

            def h_copy(m):
                dve.wait_ge(h_turned, m + 1)
                nc.vector.tensor_copy(hid_t[:, :, :], ps_h[:, :].rearrange("p (k t) -> p k t", t=P)).then_inc(h_copied, 1)

            def y_half(m, u, i2):
                dve.wait_ge(y_ps, m + 1)
                dve.wait_ge(y_stored[u], i2 * 16 + 16)
                nc.vector.tensor_copy(y_row[u][:, 0:BANK], ps_y[:, 0:BANK]).then_inc(y_copied_v, 1)

            next_x(0)
            product(0)
            next_x(1)
            h_copy(0)
            product(1)
            next_x(2)
            y_half(0, 0, 0)
            h_copy(1)

            with dve.Fori(1, pairs_of(dve) + T // 2) as i:
                for u in range(2):
                    m = i * 2 + u
                    product(m)
                    next_x(m + 1)
                    y_half(m - 1, 1 - u, i - (1 - u))
                    h_copy(m)
            pairs = pairs_of(dve)
            y_half(pairs * 2 + (T - 1), 1, pairs + (T // 2 - 1))


def combine(kit, name, x, lo, gate, yb, where, weight, out=None):
    nc = kit.nc
    T = (N - lo) // P
    with Stage(nc) as st:
        sb = lambda s: st.enter_context(nc.sbuf_tensor(f"{name}_{s}", [P, D], F32))
        sem = lambda s: st.sem(f"{name}_{s}")
        got = [[sb(f"got{i}{u}") for u in range(2)] for i in range(2)]
        own_row = [sb(f"own{u}") for u in range(2)]
        ps = [st.enter_context(nc.psum_tensor(f"{name}_ps{u}", [P, KD, P], F32)) for u in range(2)]
        own_in = [sem(f"own_in{u}") for u in range(2)]
        got_in = [sem(f"got_in{u}") for u in range(2)]
        part, mixed, turned, added, stored = sem("part"), sem("mixed"), sem("turned"), sem("added"), sem("stored")
        block = st.enter_context(nc.Block(name))

        @block.gpsimd
        def _(pool):
            for t in range(T):
                if t >= 2:
                    pool.wait_ge(mixed, t - 1)
                for i in range(2):
                    pool.indirect_dma_start(got[i][t % 2][:], None, yb[:, :], bass.IndirectOffsetOnAxis(ap=where[:, i, t:t + 1], axis=0)).then_inc(got_in[t % 2], 16)

        @block.sync
        def _(sp):
            for t in range(T):
                if t >= 2:
                    sp.wait_ge(turned, t - 1)
                sp.dma_start(own_row[t % 2][:], yb[t * P:(t + 1) * P, :]).then_inc(own_in[t % 2], 16)
            if out is not None:
                sp.wait_ge(added, T)
                for k in range(KD):
                    sp.dma_start(out[k * P:(k + 1) * P, :], x[:, k, lo:]).then_inc(stored, 16)
                sp.wait_ge(stored, 16 * KD)

        @block.vector
        def _(dve):
            def add(t):
                s = lo + t * P
                dve.wait_ge(turned, t + 1)
                for k in range(KD):
                    c = nc.vector.scalar_tensor_tensor(out=x[:, k, s:s + P], in0=ps[t % 2][:, k, :], scalar=kit.mod[:, gate + k, int(s < CTX):int(s < CTX) + 1],
                                                       in1=x[:, k, s:s + P], op0=ALU.mult, op1=ALU.add)
                c.then_inc(added, 1)

            for t in range(T):
                row = own_row[t % 2]
                dve.wait_ge(own_in[t % 2], 16 * (t // 2 + 1))
                dve.wait_ge(got_in[t % 2], 32 * (t // 2 + 1))
                nc.vector.scalar_tensor_tensor(out=row[:], in0=got[0][t % 2][:], scalar=weight[:, 0, t:t + 1], in1=row[:], op0=ALU.mult, op1=ALU.add).then_inc(part, 1)
                dve.wait_ge(part, t + 1)
                nc.vector.scalar_tensor_tensor(out=row[:], in0=got[1][t % 2][:], scalar=weight[:, 1, t:t + 1], in1=row[:], op0=ALU.mult, op1=ALU.add).then_inc(mixed, 1)
                if t:
                    add(t - 1)
            add(T - 1)

        @block.tensor
        def _(pe):
            for t in range(T):
                pe.wait_ge(mixed, t + 1)
                if t >= 2:
                    pe.wait_ge(added, t - 1)
                for k in range(KD):
                    mm = nc.tensor.transpose(ps[t % 2][:, k, :], own_row[t % 2][:, k * P:(k + 1) * P], kit.ident[:])
                mm.then_inc(turned, 1)


def mixture(kit, layer, x, h, lo, xb, yb, out=None):
    nc = kit.nc
    T = (N - lo) // P
    with ExitStack() as st:
        where = st.enter_context(nc.sbuf_tensor(f"where{layer}", [P, 2, T], U32))
        weight = st.enter_context(nc.sbuf_tensor(f"weight{layer}", [P, 2, T], F32))
        table = st.enter_context(nc.sbuf_tensor(f"table{layer}", [P, 4, 64], I32))
        with nc.sbuf_tensor(f"h{layer}_2", [P, KD, N], F32) as h:
            normalise(kit, f"norm{layer}2", x, h, lo, 2 * layer + 1, 48 * layer + 3 * KD)
            route(kit, f"route{layer}", h, lo, xb, where, weight, table)
        experts(kit, f"experts{layer}", layer, N - lo, xb, yb, table)
        combine(kit, f"combine{layer}", x, lo, 48 * layer + 5 * KD, yb, where, weight, out)


def program(nc, a, out):
    dram = lambda name, shape: nc.dram_tensor(name, list(shape), F32).ap()
    p = dram("p", (19, P, N))
    steps = dram("steps", (2, NT, P, 4, KINDS, P))
    y_steps = dram("y_steps", (2, NT, P, 4, P))
    gate, bonus = dram("gate", (4, P, N)), dram("bonus", (4, P, N))
    y_all = dram("y_all", (KD, P, N))
    xb = dram("xb", (N + (slots(N) + 3) * P, D))
    yb = dram("yb", (N + slots(N) * P, D))
    inputs = {0: a["xT"], 1: a["ctxT"]}
    with ExitStack() as st:
        kit = Kit(nc, a, st)
        modulation(kit)
        with nc.sbuf_tensor("h01", [P, KD, N], F32) as h:
            normalise(kit, "norm01", h, h, 0, 0, 0, load=inputs)
            project_in(kit, h, p)
        with nc.sbuf_tensor("half_decay", [P, 2, NT, 4], F32) as half_decay:
            mixing_inputs(kit, p, steps, half_decay, gate, bonus)
            mixing_scan(kit, steps, half_decay, y_steps)
        mixing_out(kit, y_steps, gate, bonus, y_all)
        attention(kit, p, y_all, xb, yb)
        x = st.enter_context(nc.sbuf_tensor("x", [P, KD, N], F32))
        with nc.sbuf_tensor("y01", [P, KD, N], F32) as y:
            project_out(kit, "out0", y, a["w_out_even"], x, 2 * KD, 0, load_y=y_all, load_x=inputs)
        mixture(kit, 0, x, None, 0, xb, yb)
        with nc.sbuf_tensor("h11", [P, KD, N], F32) as h:
            normalise(kit, "norm11", x, h, CTX, 2, 48)
            fourier(kit, h, h)
            project_out(kit, "out1", h, a["w_out_fourier"], x, 48 + 2 * KD, CTX)
        mixture(kit, 1, x, None, CTX, xb, yb, out)


def constants():
    f = np.float32
    i = np.arange(P)
    restart = np.ones((P, N), f)
    restart[:, ::P] = 0
    before = i[:, None] < i[None]
    pair = np.stack([np.stack([before, before | np.eye(P, dtype=bool)], 1), np.stack([before.T, before.T | np.eye(P, dtype=bool)], 1)], 1)
    level = []
    for v in range(LEVELS):
        m = 1 << v
        same = i[:, None] // (2 * m) == i[None] // (2 * m)
        level.append(same & (i[:, None] // m % 2 == 0) & (i[None] // m % 2 == 1))
    level = np.stack(level, 1)
    at = np.arange(SEQ)
    inv = 10000.0 ** (-np.arange(0, 16, 2) / 16)
    ang = np.concatenate([(at // 64)[:, None] * inv, (at % 64)[:, None] * inv], 1).T
    cos = np.concatenate([np.ones((64, SEQ)), np.cos(ang), np.cos(ang)])
    sin = np.concatenate([np.zeros((64, SEQ)), np.sin(ang), np.sin(ang)])
    rot = np.zeros((QK, QK), f)
    for c in range(16):
        rot[80 + c, 64 + c] = -1
        rot[64 + c, 80 + c] = 1
    b = np.arange(P)[:, None] * np.arange(P)[None] % P * (2 * np.pi / P)
    c = np.arange(SEQ)[:, None] * np.arange(SEQ)[None] % SEQ * (2 * np.pi / SEQ)
    by_rows = lambda m: m.reshape(SEQ // P, P, SEQ).transpose(1, 0, 2)
    pos = np.stack([by_rows(np.cos(c)), by_rows(np.sin(c))], 1) / np.sqrt(SEQ)
    chan = np.concatenate([np.cos(b), -np.sin(b)], 1) / np.sqrt(P)
    return {"dft_pos": pos.astype(f), "dft_chan": chan.astype(f), "earlier": before.astype(f),
            "order": np.tile(np.arange(64, dtype=f), (P, 1)), "cos": cos.astype(f), "sin": sin.astype(f), "rot": rot, "pair_mask": pair.astype(f), "level_mask": np.stack([level, level.transpose(2, 1, 0)], 1).astype(f), "ident": np.eye(P, dtype=f), "restart": restart, "head_ones": (i[:, None] // 64 == i[None] // 64).astype(f)}


def laid_out(inp):
    f = np.float32
    by_col = lambda v: np.ascontiguousarray(np.asarray(v, f).reshape(-1, P).T)
    pad = lambda v, n: np.concatenate([np.asarray(v, f).ravel(), np.zeros(n - np.size(v), f)])
    cond = np.stack([by_col(inp["c"]), by_col(inp["c_ctx"])], 2).reshape(P, 16)
    cols = [cond, by_col(inp["norm1_g"]), by_col(inp["norm2_g"]), by_col(pad(inp["a_mu"], 20 * P)), by_col(inp["a_w0"]),
            by_col(inp["a_a0"]), by_col(inp["a_k_k"]), by_col(inp["a_k_a"]), by_col(inp["a_r_k"]), by_col(inp["a_ln_w"]),
            by_col(inp["a_ln_b"]), by_col(inp["b_q_norm"]), by_col(inp["b_kv_norm"]), by_col(pad(inp["b_q_gain"], P)),
            by_col(pad(inp["b_k_gain"], P))]
    bias = by_col(inp["mod_b"])
    chunked = lambda w: np.ascontiguousarray(np.asarray(w, f).reshape(-1, P, w.shape[-1]).transpose(1, 0, 2))
    return {
        "xT": np.ascontiguousarray(np.asarray(inp["x"], f)[0].T), "ctxT": np.ascontiguousarray(np.asarray(inp["ctx"], f)[0].T),
        "cols": np.concatenate(cols, 1), "mod_bias": np.stack([bias, bias], 2),
        "mod_w": chunked(np.concatenate([inp["mod_w"][0], inp["mod_w"][1]], 1)),
        "w_in": chunked(inp["w_in"][0]),
        "w_out_even": chunked(inp["w_out_even"][0]), "w_out_fourier": chunked(inp["w_out_fourier"][0]),
        "router_w": chunked(inp["router_w"]), "router_b": np.tile(np.asarray(inp["router_b"], f), (P, 1)),
        "moe_gate": inp["moe_w_gate"], "moe_up": inp["moe_w_up"], "moe_down": inp["moe_w_down"],
        "shared_gate": inp["shared_w_gate"], "shared_up": inp["shared_w_up"], "shared_down": inp["shared_w_down"],
        "w_q": chunked(inp["b_w_q_up"][0]),
        "w_k": np.ascontiguousarray(inp["b_w_kv_up"][0].reshape(P, HEADS, 2, 64)[:, :, 0]).reshape(P, -1),
        "w_v": np.ascontiguousarray(inp["b_w_kv_up"][0].reshape(P, HEADS, 2, 64)[:, :, 1]).reshape(P, -1),
        "a_w2": inp["a_w2"][0].reshape(P, -1), "a_a2": inp["a_a2"][0].reshape(P, -1), "a_g2": inp["a_g2"][0],
    }


def kernel(**inputs):
    import concourse.bacc as _bacc
    from concourse.bass_utils import run_bass_kernel_spmd as _run

    nc = _bacc.Bacc("TRN2", target_bir_lowering=False, num_devices=1)
    arrays = {k: v for k, v in laid_out({k: np.asarray(v) for k, v in inputs.items()}).items()}
    arrays.update(constants())
    args = {k: nc.dram_tensor(f"in_{k}", v.shape, mybir.dt.from_np(v.dtype), kind="ExternalInput").ap() for k, v in arrays.items()}
    out = nc.dram_tensor("outT", (D, SEQ), F32, kind="ExternalOutput").ap()
    program(nc, args, out)
    r = _run(nc, [{f"in_{k}": v for k, v in arrays.items()}], core_ids=[0])
    return np.ascontiguousarray(r.results[0]["outT"].T)[None]
```

```python
from contextlib import ExitStack

import numpy as np

import concourse.bass as bass
from concourse import mybir

ALU = mybir.AluOpType
ACT = mybir.ActivationFunctionType
AX = mybir.AxisListType
F32 = mybir.dt.float32
I32 = mybir.dt.int32
U32 = mybir.dt.uint32
F32R = mybir.dt.float32r

P = 128
D = 1024
KD = D // P
CTX = 256
SEQ = 1024
N = CTX + SEQ
NT = N // P
NTC = CTX // P
LN_EXP = "natural_log_exp_and_others"
BANK = 512
EPS, LN_EPS, KK_EPS = 1e-6, 64e-5, 1e-12
SEGS = ((0, 512), (512, 1024), (1024, 1280))
PARTS = ((0, CTX, 1), (CTX, N, 0))

COLS = {}
_n = 0
for _name, _w in (("cond", 16), ("norm1", 16), ("norm2", 16), ("mu", 20), ("w0", 8), ("a0", 8), ("k_k", 4), ("k_a", 4),
                  ("r_k", 4), ("ln_w", 4), ("ln_b", 4), ("q_norm", 2), ("kv_norm", 1), ("q_gain", 1), ("k_gain", 1)):
    COLS[_name] = _n
    _n += _w
N_COLS = _n
A_CHUNKS = 15
R0, K0, V0, WD, AD, GD = 0, 4, 8, 12, 13, 14
Q_CH, KV_CH, KR_CH = 15, 17, 18


def free(m):
    return m + 1


def done(m):
    return m + 3


def col(name, i=0):
    return COLS[name] + i


class Stage(ExitStack):

    def __init__(self, nc):
        super().__init__()
        self.nc, self.sems = nc, []

    def sem(self, name):
        self.sems.append(self.nc.alloc_semaphore(name))
        return self.sems[-1]

    def __exit__(self, *raised):
        super().__exit__(*raised)
        if raised[0] is None:
            self.nc.clear_and_free_semaphores(self.sems)
            self.nc.all_engine_barrier()


class Kit:

    def __init__(self, nc, args, stack):
        self.nc, self.args = nc, args
        sb = lambda name, shape, dt=F32: stack.enter_context(nc.sbuf_tensor(name, shape, dt))
        self.cols = sb("cols", [P, N_COLS])
        self.eps = sb("eps", [P, 3])
        self.mod = sb("mod", [P, 96, 2])
        self.gain = sb("gain", [P, 4, KD, 2])
        self.ident = sb("ident", [P, P])
        self.ones = sb("ones", [P, P])
        self.head_ones = sb("head_ones", [P, P])


def modulation(kit):
    nc, a = kit.nc, kit.args
    blocks = 24
    with Stage(nc) as st:
        sb = lambda name, shape: st.enter_context(nc.sbuf_tensor(name, shape, F32))
        sem = lambda name: st.sem(name)
        w = [sb(f"mod_w{u}", [P, KD, 512]) for u in range(2)]
        cs = sb("mod_silu", [P, KD, 2])
        bias = sb("mod_bias", [P, 96, 2])
        row = [sb(f"mod_row{u}", [P, 512]) for u in range(2)]
        ps_row = [st.enter_context(nc.psum_tensor(f"ps_row{u}", [2, 512], F32)) for u in range(2)]
        ps_col = [st.enter_context(nc.psum_tensor(f"ps_col{u}", [P, 4, P], F32)) for u in range(2)]
        small_in, silu_done, ones_done = sem("small_in"), sem("silu_done"), sem("ones_done")
        w_in = [sem(f"mod_w_in{u}") for u in range(2)]
        rows_summed, rows_copied, rows_turned, cols_kept = (
            sem("rows_summed"), sem("rows_copied"), sem("rows_turned"), sem("cols_kept"))
        gain_step = sem("gain_step")
        block = st.enter_context(nc.Block("modulation"))

        @block.sync
        def _(sp):
            sp.dma_start(kit.cols[:], a["cols"][:, :]).then_inc(small_in, 16)
            sp.dma_start(kit.ident[:], a["ident"][:, :]).then_inc(small_in, 16)
            sp.dma_start(kit.head_ones[:], a["head_ones"][:, :]).then_inc(small_in, 16)
            sp.dma_start(bias[:], a["mod_bias"][:, :, :]).then_inc(small_in, 16)
            with sp.Fori(0, blocks // 2) as i:
                for u in range(2):
                    sp.wait_ge(rows_summed, free(i * 2 + u))
                    sp.dma_start(w[u][:], a["mod_w"][:, :, bass.ds(i * 1024 + u * 512, 512)]).then_inc(w_in[u], 16)

        @block.scalar
        def _(act):
            act.wait_ge(small_in, 64)
            nc.scalar.activation(cs[:], kit.cols[:, 0:16].rearrange("p (k v) -> p k v", v=2), ACT.Silu).then_inc(silu_done, 1)

        @block.tensor
        def _(pe):
            pe.sem_inc(rows_summed, 2)
            pe.wait_ge(silu_done, 1)
            with pe.Fori(0, blocks // 2) as i:
                for u in range(2):
                    pe.wait_ge(w_in[u], i * 16 + 16)
                    for k in range(KD):
                        mm = nc.tensor.matmul(ps_row[u][:], cs[:, k, :], w[u][:, k, :], start=k == 0, stop=k == KD - 1)
                    mm.then_inc(rows_summed, 1)
                    pe.wait_ge(rows_copied, i * 2 + u + 1)
                    for q in range(4):
                        t = nc.tensor.transpose(ps_col[u][:, q, :], row[u][:, q * P:(q + 1) * P], kit.ident[:])
                    t.then_inc(rows_turned, 1)

        @block.vector
        def _(dve):
            nc.vector.memset(kit.ones[:], 1.0).then_inc(ones_done, 1)
            for i, eps in enumerate((EPS, LN_EPS, KK_EPS)):
                nc.vector.memset(kit.eps[:, i:i + 1], eps).then_inc(ones_done, 1)
            for u in range(2):
                nc.vector.memset(row[u][:], 0.0).then_inc(ones_done, 1)
            dve.wait_ge(small_in, 64)
            dve.wait_ge(ones_done, 6)
            with dve.Fori(0, blocks // 2) as i:
                for u in range(2):
                    dve.wait_ge(rows_summed, done(i * 2 + u))
                    nc.vector.tensor_copy(row[u][0:2, :], ps_row[u][:]).then_inc(rows_copied, 1)
                    dve.wait_ge(rows_turned, i * 2 + u + 1)
                    at = bass.ds(i * 8 + u * 4, 4)
                    nc.vector.tensor_tensor(kit.mod[:, at, :], ps_col[u][:, :, 0:2], bias[:, at, :], ALU.add).then_inc(cols_kept, 1)
            dve.wait_ge(cols_kept, blocks)
            for layer in range(2):
                for which, sixth in ((0, 1), (1, 4)):
                    for v in range(2):
                        c0 = layer * 48 + sixth * KD
                        g = kit.cols[:, col(("norm1", "norm2")[which], layer * KD):][:, 0:KD]
                        nc.vector.scalar_tensor_tensor(
                            out=kit.gain[:, layer * 2 + which, :, v], in0=kit.mod[:, c0:c0 + KD, v], scalar=1.0, in1=g,
                            op0=ALU.add, op1=ALU.mult).then_inc(gain_step, 1)
            dve.wait_ge(gain_step, 8)


def normalise(kit, name, x, h, lo, which, shift, load=None):
    nc = kit.nc
    parts = [p for p in PARTS if p[1] > lo]
    segs = [(s, e) for s, e in SEGS] if lo == 0 else [(lo, lo + 512), (lo + 512, N)]
    with Stage(nc) as st:
        sem = lambda s: st.sem(f"{name}_{s}")
        sq = [st.enter_context(nc.sbuf_tensor(f"{name}_sq{u}", [P, N], F32)) for u in range(2)]
        rstd = st.enter_context(nc.sbuf_tensor(f"{name}_rstd", [P, N], F32))
        ps = st.enter_context(nc.psum_tensor(f"{name}_ps", [P, 3, BANK], F32))
        x_in = [sem(f"x_in{k}") for k in range(KD)]
        squared, summed, chain, root, scaled, done = (
            sem("squared"), sem("summed"), sem("chain"), sem("root"), sem("scaled"), sem("done"))
        block = st.enter_context(nc.Block(name))

        @block.sync
        def _(sp):
            if load is not None:
                for k in range(KD):
                    for s, e, v in parts:
                        sp.dma_start(x[:, k, s:e], load[v][k * P:(k + 1) * P, :]).then_inc(x_in[k], 16)

        @block.scalar
        def _(act):
            nc.scalar.preload_act_table_set(LN_EXP)
            for k in range(KD):
                if load is not None:
                    act.wait_ge(x_in[k], 16 * len(parts))
                if k >= 2:
                    act.wait_ge(summed, k - 1)
                nc.scalar.activation(sq[k % 2][:, lo:], x[:, k, lo:], ACT.Square).then_inc(squared, 1)
            act.wait_ge(summed, KD)
            flat = ps[:, :, :].rearrange("p b c -> p (b c)")[:, 0:N - lo]
            nc.scalar.activation(rstd[:, lo:], flat, ACT.Ln, scale=1.0 / D, bias=kit.eps[:, 0:1]).then_inc(chain, 1)
            act.wait_ge(chain, 1)
            nc.scalar.activation(rstd[:, lo:], rstd[:, lo:], ACT.Exp, scale=-0.5).then_inc(root, 1)
            for k in range(KD):
                act.wait_ge(scaled, k + 1)
                for s, e, v in parts:
                    a = nc.scalar.activation(h[:, k, s:e], h[:, k, s:e], ACT.Identity, scale=kit.gain[:, which, k, v:v + 1],
                                             bias=kit.mod[:, shift + k, v:v + 1])
                a.then_inc(done, 1)

        @block.tensor
        def _(pe):
            for k in range(KD):
                pe.wait_ge(squared, k + 1)
                for n, (s, e) in enumerate(segs):
                    mm = nc.tensor.matmul(ps[:, n, 0:e - s], kit.ones[:], sq[k % 2][:, s:e], start=k == 0, stop=k == KD - 1)
                mm.then_inc(summed, 1)

        @block.vector
        def _(dve):
            dve.wait_ge(root, 1)
            for k in range(KD):
                nc.vector.tensor_tensor(h[:, k, lo:], x[:, k, lo:], rstd[:, lo:], ALU.mult).then_inc(scaled, 1)


def split(nc, high, low, src, first, second):
    nc.vector.tensor_copy(high, src).then_inc(first[0], 1)
    nc.vector.wait_ge(*first)
    nc.vector.tensor_tensor(low, src, high.bitcast(F32), ALU.subtract).then_inc(second, 1)


def product3(nc, to, weights, values, start, stop):
    for i, (w, v) in enumerate(((0, 0), (0, 1), (1, 0))):
        mm = nc.tensor.matmul(to, weights[w], values[v], start=start and i == 0, stop=stop and i == 2)
    return mm


def project_in(kit, h, out):
    nc, a = kit.nc, kit.args
    loops = 9
    with Stage(nc) as st:
        sb = lambda name, shape: st.enter_context(nc.sbuf_tensor(name, shape, F32))
        sem = lambda name: st.sem(name)
        w = [sb(f"in_w{u}", [P, KD, P]) for u in range(2)]
        parts = lambda name, shape: [st.enter_context(nc.sbuf_tensor(f"in_{name}_{x}", shape, F32R)) for x in ("high", "low")]
        w_parts = [parts(f"w{u}", [P, KD, P]) for u in range(2)]
        h_parts = parts("h", [P, KD, N])
        h_cut, h_split, w_cut, w_split = sem("in_h_cut"), sem("in_h_split"), sem("in_w_cut"), sem("in_w_split")
        w32 = sb("in_w32", [P, KD, 32])
        raw = [sb(f"in_raw{u}", [P, N + 3]) for u in range(2)]
        kept = [sb(f"in_kept{u}", [P, N]) for u in range(2)]
        mixed = [sb(f"in_mixed{u}", [P, N]) for u in range(2)]
        keep_col = sb("in_keep_col", [P, 20])
        half_col = sb("in_half_col", [P, 20])
        ps = [st.enter_context(nc.psum_tensor(f"in_ps{u}", [P, 3, BANK], F32)) for u in range(2)]
        w_in = [sem(f"in_w_in{u}") for u in range(2)]
        w32_in = sem("in_w32_in")
        stored = [sem(f"in_stored{u}") for u in range(2)]
        setup, multiplied, copied, summed, shifted, mixed_free = (
            sem("in_setup"), sem("in_multiplied"), sem("in_copied"), sem("in_summed"), sem("in_shifted"), sem("in_mixed_free"))
        block = st.enter_context(nc.Block("project_in"))
        gaps = ((0, CTX, 1), (CTX, N, 2))

        @block.sync
        def _(sp):
            sp.dma_start(w32[:], a["w_in"][:, :, 18 * P:18 * P + 32]).then_inc(w32_in, 16)
            with sp.Fori(0, loops) as i:
                for u in range(2):
                    sp.wait_ge(w_split, free(i * 2 + u))
                    sp.dma_start(w[u][:], a["w_in"][:, :, bass.ds(i * 256 + u * P, P)]).then_inc(w_in[u], 16)

        @block.tensor
        def _(pe):
            pe.sem_inc(multiplied, 2)

            def chunk(m, u, first=False):
                pe.wait_ge(w_split, done(m))
                pe.wait_ge(copied, free(m))
                for k in range(KD):
                    if first:
                        pe.wait_ge(h_split, k + 1)
                    for n, (s, e) in enumerate(SEGS):
                        mm = product3(nc, ps[u][:, n, 0:e - s], [x[:, k, :] for x in w_parts[u]], [x[:, k, s:e] for x in h_parts], k == 0, k == KD - 1)
                mm.then_inc(multiplied, 1)

            chunk(0, 0, first=True)
            chunk(1, 1)
            with pe.Fori(1, loops) as i:
                for u in range(2):
                    chunk(i * 2 + u, u)
            pe.wait_ge(w32_in, 16)
            pe.wait_ge(copied, free(2 * loops))
            for n, (s, e) in enumerate(SEGS):
                for k in range(KD):
                    mm = nc.tensor.matmul(ps[0][0:32, n, 0:e - s], w32[:, k, :], h[:, k, s:e], start=k == 0, stop=k == KD - 1)
            mm.then_inc(multiplied, 1)

        @block.scalar
        def _(act):
            act.sem_inc(copied, 2)
            act.wait_ge(setup, 4)
            with act.Fori(0, loops) as i:
                for u in range(2):
                    act.wait_ge(multiplied, done(i * 2 + u))
                    act.wait_ge(shifted, free(i * 2 + u))
                    flat = ps[u][:, :, :].rearrange("p b c -> p (b c)")
                    for s, e, off in gaps:
                        nc.scalar.activation(raw[u][:, s + off:e + off], flat[:, s:e], ACT.Copy)
                    nc.scalar.activation(kept[u][:], flat[:, 0:N], ACT.Copy, scale=keep_col[:, bass.ds(i * 2 + u, 1)]).then_inc(copied, 1)
            act.wait_ge(multiplied, done(2 * loops))
            act.wait_ge(shifted, free(2 * loops))
            flat = ps[0][:, :, :].rearrange("p b c -> p (b c)")
            nc.scalar.activation(kept[0][0:32, :], flat[0:32, 0:N], ACT.Copy).then_inc(copied, 1)

        @block.vector
        def _(dve):
            mu = kit.cols[:, col("mu"):col("mu") + 20]
            nc.vector.tensor_scalar(keep_col[:], mu, -1.0, 1.0, ALU.mult, ALU.add).then_inc(setup, 1)
            nc.vector.tensor_scalar(half_col[:], mu, 0.5, None, ALU.mult).then_inc(setup, 1)
            for u in range(2):
                nc.vector.memset(raw[u][:], 0.0).then_inc(setup, 1)
            dve.wait_ge(setup, 4)
            nc.vector.sem_inc(shifted, 2)
            dve.sem_inc(w_split, 2)

            def split_weights(m, u, i):
                dve.wait_ge(w_in[u], i * 16 + 16)
                dve.wait_ge(multiplied, free(m))
                split(nc, w_parts[u][0][:], w_parts[u][1][:], w[u][:], (w_cut, m + 1), w_split)

            def mix(m, u):
                dve.wait_ge(copied, done(m))
                dve.wait_ge(mixed_free, m + 1)
                for s, e, off in gaps:
                    t = nc.vector.tensor_tensor(mixed[u][:, s:e], raw[u][:, s + off - 1:e + off - 1], raw[u][:, s + off + 1:e + off + 1], ALU.add)
                t.then_inc(summed, 1)
                dve.wait_ge(summed, m + 1)
                nc.vector.scalar_tensor_tensor(out=mixed[u][:], in0=mixed[u][:], scalar=half_col[:, bass.ds(m, 1)],
                                               in1=kept[u][:], op0=ALU.mult, op1=ALU.add).then_inc(shifted, 1)

            split_weights(0, 0, 0)
            for k in range(KD):
                split(nc, h_parts[0][:, k, :], h_parts[1][:, k, :], h[:, k, :], (h_cut, k + 1), h_split)
            split_weights(1, 1, 0)
            mix(0, 0)
            with dve.Fori(1, loops) as i:
                for u in range(2):
                    split_weights(i * 2 + u, u, i)
                    mix(i * 2 + (u - 1), 1 - u)
            mix(2 * loops - 1, 1)

        @block.gpsimd
        def _(pool):
            pool.sem_inc(mixed_free, 2)
            with pool.Fori(0, loops) as i:
                for u in range(2):
                    pool.wait_ge(shifted, done(i * 2 + u))
                    pool.dma_start(out[bass.ds(i * 2 + u, 1), :, :].rearrange("o p n -> p (o n)"), mixed[u][:]).then_inc(stored[u], 16)
                    pool.wait_ge(stored[u], i * 16 + 16)
                    pool.sem_inc(mixed_free, 1)
            pool.wait_ge(copied, done(2 * loops))
            pool.dma_start(out[18, 0:32, :], kept[0][0:32, :]).then_inc(stored[0], 16)
            pool.wait_ge(stored[0], 16 * (loops + 1))
            pool.wait_ge(stored[1], 16 * loops)


class Link:

    def __init__(self, engine, sem, start=0):
        self.engine, self.sem, self.start, self.n = engine, sem, start, 0

    def __call__(self, instruction):
        self.n += 1
        instruction.then_inc(self.sem, 1)
        self.engine.wait_ge(self.sem, self.start + self.n)


KINDS = 5
DECAY_SCALE = 0.606531
STEP_OF = {0: list(range(NT)), 1: [1, 0] + [NT + 1 - c for c in range(NTC, NT)]}


def mixing_inputs(kit, p, steps, half_decay, gate, bonus):
    nc, a = kit.nc, kit.args
    with Stage(nc) as st:
        sb = lambda name, shape=(P, N): st.enter_context(nc.sbuf_tensor(f"mi_{name}", list(shape), F32))
        sem = lambda name: st.sem(f"mi_{name}")
        r, k, v, wd, ad, gd = (sb(x) for x in ("r", "k", "v", "wd", "ad", "gd"))
        w2, a2, g2 = (sb(x, (P, P)) for x in ("w2", "a2", "g2"))
        kk, tmp, sig, iclr, cum, q, q2, ea, eb, ec, kd, kd_sum, gate_out, bonus_out, restart = (
            sb(x) for x in ("kk", "tmp", "sig", "iclr", "cum", "q", "q2", "ea", "eb", "ec", "kd", "kd_sum", "gate_out",
                            "bonus_out", "restart"))
        kinds = [sb(f"kinds{d}", (P, KINDS, N)) for d in range(2)]
        ka_rest = sb("ka_rest", (P, 4))
        psa = st.enter_context(nc.psum_tensor("mi_psa", [P, 3, BANK], F32))
        psb = st.enter_context(nc.psum_tensor("mi_psb", [P, 3, BANK], F32))
        fa, fb = (x[:, :, :].rearrange("p b c -> p (b c)")[:, 0:N] for x in (psa, psb))
        low_in, low_ready, rows_in, link = sem("low_in"), sem("low_ready"), sem("rows_in"), sem("link")
        kk_scaled, squared, norm_ps, norm_read, rooted = (
            sem("kk_scaled"), sem("squared"), sem("norm_ps"), sem("norm_read"), sem("rooted"))
        decay_ps, iclr_ps, decay_sig, iclr_sig, q_ready, exps = (
            sem("decay_ps"), sem("iclr_ps"), sem("decay_sig"), sem("iclr_sig"), sem("q_ready"), sem("exps"))
        v_copied, kinds_ready, kinds_out = sem("v_copied"), sem("kinds_ready"), [sem(f"kinds_out{d}") for d in range(2)]
        rk_ready, bonus_ps, bonus_read, gate_ps, gate_read = (
            sem("rk_ready"), sem("bonus_ps"), sem("bonus_read"), sem("gate_ps"), sem("gate_read"))
        tiles_free, after_out = sem("tiles_free"), sem("after_out")
        block = st.enter_context(nc.Block("mixing_inputs"))

        def product(pe, ps, lhsT, rhs):
            for n, (s, e) in enumerate(SEGS):
                mm = nc.tensor.matmul(ps[:, n, 0:e - s], lhsT, rhs[:, s:e], start=True, stop=True)
            return mm

        @block.sync
        def _(sp):
            for t, c in ((wd, WD), (ad, AD), (gd, GD)):
                sp.dma_start(t[:], p[c, :, :]).then_inc(low_in, 16)
            sp.dma_start(restart[:], a["restart"][:, :]).then_inc(low_in, 16)

            def load(j):
                for t, c in ((r, R0), (k, K0), (v, V0)):
                    sp.dma_start(t[:], p[bass.ds(j + c, 1), :, :].rearrange("o p n -> p (o n)")).then_inc(rows_in, 16)
                for t, w in ((w2, "a_w2"), (a2, "a_a2"), (g2, "a_g2")):
                    sp.dma_start(t[:], a[w][:, bass.ds(j * P, P)]).then_inc(rows_in, 16)

            def turn(j, last=False):
                for d in range(2):
                    sp.wait_ge(kinds_ready, j * 2 + (d + 1))
                    sp.wait_ge(v_copied, j * 2 + (d + 1))
                    for c in range(NT):
                        sp.dma_start(steps[d, STEP_OF[d][c], :, bass.ds(j, 1), :, :].rearrange("p o k t -> p (o k) t"),
                                     kinds[d][:, :, c * P:(c + 1) * P]).then_inc(kinds_out[d], 16)
                sp.wait_ge(gate_read, j + 1)
                sp.dma_start(gate[bass.ds(j, 1), :, :].rearrange("o p n -> p (o n)"), gate_out[:]).then_inc(after_out, 16)
                sp.wait_ge(bonus_read, j + 1)
                if not last:
                    load(j + 1)
                sp.dma_start(bonus[bass.ds(j, 1), :, :].rearrange("o p n -> p (o n)"), bonus_out[:]).then_inc(after_out, 16)
                for d in range(2):
                    sp.wait_ge(kinds_out[d], j * 160 + 160)
                sp.wait_ge(after_out, j * 32 + 32)
                if not last:
                    sp.sem_inc(tiles_free, 1)

            load(0)
            with sp.Fori(0, 3) as j:
                turn(j)
            turn(3, last=True)

        @block.tensor
        def _(pe):
            pe.wait_ge(low_ready, 2)
            with pe.Fori(0, 4) as j:
                pe.wait_ge(squared, j + 1)
                product(pe, psa, kit.head_ones[:], tmp).then_inc(norm_ps, 1)
                pe.wait_ge(rows_in, j * 96 + 96)
                for d in range(2):
                    half = slice(64 * d, 64 * d + 64)
                    if d:
                        pe.wait_ge(decay_sig, j * 2 + d)
                    product(pe, psb, w2[half, :], wd[half, :]).then_inc(decay_ps, 1)
                    if d:
                        pe.wait_ge(iclr_sig, j * 2 + d)
                    else:
                        pe.wait_ge(norm_read, j + 1)
                    product(pe, psa, a2[half, :], ad[half, :]).then_inc(iclr_ps, 1)
                pe.wait_ge(decay_sig, j * 2 + 2)
                product(pe, psb, g2[:], gd).then_inc(gate_ps, 1)
                pe.wait_ge(rk_ready, j + 1)
                pe.wait_ge(iclr_sig, j * 2 + 2)
                product(pe, psa, kit.head_ones[:], tmp).then_inc(bonus_ps, 1)
                pe.wait_ge(bonus_read, j + 1)
                pe.wait_ge(gate_read, j + 1)

        @block.scalar
        def _(act):
            act.wait_ge(low_in, 64)
            nc.scalar.activation(wd[:], wd[:], ACT.Tanh).then_inc(low_ready, 1)
            nc.scalar.activation(gd[:], gd[:], ACT.Sigmoid).then_inc(low_ready, 1)
            with act.Fori(0, 4) as j:
                act.wait_ge(kk_scaled, j + 1)
                nc.scalar.activation(tmp[:], kk[:], ACT.Square).then_inc(squared, 1)
                nc.scalar.preload_act_table_set(LN_EXP)
                act.wait_ge(norm_ps, j + 1)
                nc.scalar.activation(q[:], fa, ACT.Ln, bias=kit.eps[:, 2:3]).then_inc(norm_read, 1)
                act.wait_ge(norm_read, j + 1)
                nc.scalar.activation(q[:], q[:], ACT.Exp, scale=-0.5).then_inc(rooted, 1)
                for d in range(2):
                    act.wait_ge(decay_ps, j * 2 + d + 1)
                    nc.scalar.activation(sig[:], fb, ACT.Sigmoid, bias=kit.cols[:, bass.ds(j + col("w0", 4 * d), 1)]).then_inc(decay_sig, 1)
                    act.wait_ge(iclr_ps, j * 2 + d + 1)
                    if d:
                        act.wait_ge(kinds_ready, j * 2 + d)
                    nc.scalar.activation(iclr[:], fa, ACT.Sigmoid, bias=kit.cols[:, bass.ds(j + col("a0", 4 * d), 1)]).then_inc(iclr_sig, 1)
                    act.wait_ge(q_ready, j * 2 + d + 1)
                    ends = cum[:, P - 1:N:P]
                    for c in range(NT):
                        n = STEP_OF[d][c]
                        nc.scalar.activation(half_decay[:, d, n, bass.ds(j, 1)], ends[:, c:c + 1], ACT.Exp, scale=0.5)
                    for out, src, sign in (((ea, q, 1.0), (eb, q, -1.0), (ec, q2, 1.0)) if d == 0 else
                                           ((ea, q2, -1.0), (eb, q2, 1.0), (ec, q, -1.0))):
                        e = nc.scalar.activation(out[:], src[:], ACT.Exp, scale=sign)
                    e.then_inc(exps, 1)
                    act.wait_ge(rows_in, j * 96 + 96)
                    act.wait_ge(tiles_free, j + 1)
                    nc.scalar.activation(kinds[d][:, 4, :], v[:], ACT.Copy).then_inc(v_copied, 1)
                act.wait_ge(gate_ps, j + 1)
                nc.scalar.activation(gate_out[:], fb, ACT.Copy).then_inc(gate_read, 1)

        @block.vector
        def _(dve):
            dve.sem_inc(tiles_free, 1)
            k_a = kit.cols[:, col("k_a"):col("k_a") + 4]
            nc.vector.tensor_scalar(ka_rest[:], k_a, -1.0, 1.0, ALU.mult, ALU.add).then_inc(link, 1)
            per = 34
            with dve.Fori(0, 4) as j:
                own = Link(dve, link, j * per + 1)
                par = lambda name: kit.cols[:, bass.ds(j + col(name), 1)]
                dve.wait_ge(rows_in, j * 96 + 96)
                nc.vector.tensor_scalar(kk[:], k[:], par("k_k"), None, ALU.mult).then_inc(kk_scaled, 1)
                dve.wait_ge(rooted, j + 1)
                own(nc.vector.tensor_tensor(kk[:], kk[:], q[:], ALU.mult))
                for d in range(2):
                    dve.wait_ge(decay_sig, j * 2 + d + 1)
                    own(nc.vector.tensor_scalar(q2[:], sig[:], -DECAY_SCALE, None, ALU.mult))
                    own(nc.vector.tensor_tensor_scan(cum[:], restart[:], q2[:], 0.0, ALU.mult, ALU.add))
                    chunks = lambda t: t[:, :].rearrange("p (c t) -> p c t", t=P)
                    ends = chunks(cum)[:, :, P - 1:P].broadcast_to((P, NT, P))
                    own(nc.vector.scalar_tensor_tensor(out=chunks(q), in0=ends, scalar=-0.5, in1=chunks(cum), op0=ALU.mult, op1=ALU.add))
                    nc.vector.tensor_tensor(q2[:], q[:], q2[:], ALU.subtract).then_inc(q_ready, 1)
                    dve.wait_ge(iclr_sig, j * 2 + d + 1)
                    own(nc.vector.tensor_scalar(kd[:], iclr[:], par("k_a"), ka_rest[:, bass.ds(j, 1)], ALU.mult, ALU.add))
                    own(nc.vector.tensor_tensor(kd[:], kd[:], k[:], ALU.mult))
                    own(nc.vector.tensor_tensor(iclr[:], iclr[:], kk[:], ALU.mult))
                    if d == 0:
                        own(nc.vector.tensor_copy(kd_sum[:], kd[:]))
                    else:
                        own(nc.vector.tensor_tensor(kd_sum[:], kd_sum[:], kd[:], ALU.add))
                    dve.wait_ge(exps, j * 2 + d + 1)
                    dve.wait_ge(tiles_free, j + 1)
                    own(nc.vector.scalar_tensor_tensor(out=kinds[d][:, 0, :], in0=kk[:], scalar=-1.0, in1=ec[:], op0=ALU.mult, op1=ALU.mult))
                    own(nc.vector.tensor_tensor(kinds[d][:, 1, :], r[:], ea[:], ALU.mult))
                    own(nc.vector.tensor_tensor(kinds[d][:, 2, :], iclr[:], eb[:], ALU.mult))
                    own(nc.vector.tensor_tensor(kinds[d][:, 3, :], kd[:], eb[:], ALU.mult))
                    dve.sem_inc(kinds_ready, 1)
                nc.vector.scalar_tensor_tensor(out=tmp[:], in0=r[:], scalar=par("r_k"), in1=kd_sum[:], op0=ALU.mult, op1=ALU.mult).then_inc(rk_ready, 1)
                dve.wait_ge(bonus_ps, j + 1)
                nc.vector.tensor_tensor(bonus_out[:], fa, v[:], ALU.mult).then_inc(bonus_read, 1)
                assert own.n <= per, own.n
                for _ in range(per - own.n):
                    dve.sem_inc(link, 1)



LEVELS = 7


def mixing_scan(kit, steps, half_decay, y_out):
    nc, a = kit.nc, kit.args
    with Stage(nc) as st:
        sb = lambda name, shape: st.enter_context(nc.sbuf_tensor(f"ms_{name}", list(shape), F32))
        sem = lambda name: st.sem(f"ms_{name}")
        lanes = range(2)
        units = [(jj, hh) for jj in range(2) for hh in range(2)]
        data = [sb(f"data{d}", (P, 4, KINDS, P)) for d in range(2)]
        y = [sb(f"y{d}", (P, 4, P)) for d in range(2)]
        pair_mask = sb("pair_mask", (P, 2, 2, P))
        level_mask = sb("level_mask", (P, 2, LEVELS, P))
        tok = [sb(f"tok{l}", (P, 2, 3, P)) for l in lanes]
        am = [sb(f"am{l}", (P, 4, 2, 2, P)) for l in lanes]
        t1 = [sb(f"t1{l}", (P, 4, P)) for l in lanes]
        inv = [sb(f"inv{l}", (P, 4, P)) for l in lanes]
        inv_t = [sb(f"inv_t{l}", (P, 4, P)) for l in lanes]
        g = [sb(f"g{l}", (P, 4, 64)) for l in lanes]
        uu = [sb(f"uu{l}", (P, 4, 64)) for l in lanes]
        state = [[sb(f"state{d}{l}", (P, 2, 64)) for l in lanes] for d in range(2)]
        mid = [sb(f"mid{l}", (P, 2, 64)) for l in lanes]
        far = [sb(f"far{l}", (P, 2, 64)) for l in lanes]
        ps = st.enter_context(nc.psum_tensor("ms_ps", [P, 8, BANK], F32))
        bank = lambda l, b: ps[:, 4 * l + b, :]
        masks_in, zeroed, link, y_free = sem("masks_in"), sem("zeroed"), sem("link"), sem("y_free")
        data_in = [sem(f"data_in{d}") for d in range(2)]
        stored = sem("stored")
        lane_sems = lambda name: [sem(f"{name}{l}") for l in lanes]
        (turned, tok_copied, pairs_ps, pairs_masked, first_cut, inv_t_ready, t1_ps, t1_masked, joined_ps, inv_ready, mid_ready, g_ps,
         g_copied, u_ps, u_copied, y_ps, y_copied, s_ps, state_ready) = (lane_sems(x) for x in (
             "turned", "tok_copied", "pairs_ps", "pairs_masked", "first_cut", "inv_t_ready", "t1_ps", "t1_masked", "joined_ps",
             "inv_ready", "mid_ready", "g_ps", "g_copied", "u_ps", "u_copied", "y_ps", "y_copied", "s_ps", "state_ready"))
        ident4 = kit.ident[:, :].rearrange("p (o t) -> p o t", o=1).broadcast_to((P, 4, P))
        block = st.enter_context(nc.Block("mixing_scan"))

        @block.sync
        def _(sp):
            sp.dma_start(pair_mask[:], a["pair_mask"][:, :, :, :]).then_inc(masks_in, 16)
            sp.dma_start(level_mask[:], a["level_mask"][:, :, :, :]).then_inc(masks_in, 16)
            for d in range(2):
                sp.dma_start(data[d][:], steps[d, 0, :, :, :, :]).then_inc(data_in[d], 16)

            def turn(n, d, last):
                it = n * 2 + d
                for l in lanes:
                    sp.wait_ge(s_ps[l], it + 1)
                if not last:
                    sp.dma_start(data[d][:], steps[d, bass.ds(n + 1, 1), :, :, :, :].rearrange("o p j k t -> p (o j) k t")).then_inc(data_in[d], 16)
                for l in lanes:
                    sp.wait_ge(y_copied[l], it + 2)
                at = bass.ds(n, 1)
                sp.dma_start(y_out[d, at, :, :, :].rearrange("o p j t -> p (o j) t"), y[d][:]).then_inc(stored, 16)
                sp.wait_ge(stored, it * 16 + 16)
                sp.sem_inc(y_free, 1)

            with sp.Fori(0, NT - 1) as n:
                for d in range(2):
                    turn(n, d, False)
            for d in range(2):
                turn(NT - 1, d, True)

        @block.tensor
        def _(pe):
            pe.wait_ge(zeroed, 4)
            with pe.Fori(0, NT) as n:
                for d in range(2):
                    it = n * 2 + d
                    half = lambda hh: slice(64 * hh, 64 * hh + 64)
                    pe.wait_ge(data_in[d], n * 16 + 16)
                    for l in lanes:
                        pe.wait_ge(state_ready[l], it + 1)
                        pe.wait_ge(y_copied[l], it + 1)
                        for u, (jj, hh) in enumerate(units):
                            for q in range(2):
                                mm = nc.tensor.matmul(bank(l, u)[:, q * 256:q * 256 + 256], data[d][half(hh), 2 * l + jj, 2 + q, :],
                                                      data[d][half(hh), 2 * l + jj, 0:2, :], start=True, stop=True)
                            mm.then_inc(pairs_ps[l], 1)
                    for v in range(LEVELS):
                        for l in lanes:
                            if v:
                                pe.wait_ge(inv_ready[l], it * (LEVELS - 1) + v)
                            else:
                                pe.wait_ge(pairs_masked[l], it + 1)
                            for u in range(4):
                                rhs = inv[l][:, u, :] if v else kit.ident[:]
                                mm = nc.tensor.matmul(bank(l, 0)[:, u * P:u * P + P], am[l][:, u, 0, 0, :], rhs, start=True, stop=True)
                            mm.then_inc(t1_ps[l], 1)
                        for l in lanes if v < 2 else ():
                            if v:
                                pe.wait_ge(tok_copied[l], it * 2 + v)
                            for q in range(3):
                                mm = nc.tensor.transpose(bank(l, 3)[:, q * P:q * P + P], data[d][:, 2 * l + v, 2 + q, :], kit.ident[:])
                            mm.then_inc(turned[l], 1)
                        for l in lanes if v else ():
                            pe.wait_ge(t1_masked[l], it * LEVELS + v + 1)
                            pe.wait_ge(inv_t_ready[l], it * LEVELS + v)
                            for u in range(4):
                                at = slice(u * P, u * P + P)
                                if v < LEVELS - 1:
                                    nc.tensor.matmul(bank(l, 1)[:, at], inv_t[l][:, u, :], t1[l][:, u, :], start=True, stop=True)
                                mm = nc.tensor.matmul(bank(l, 2)[:, at], t1[l][:, u, :], inv_t[l][:, u, :], start=True, stop=True)
                            mm.then_inc(joined_ps[l], 1)
                    for l in lanes:
                        pe.wait_ge(mid_ready[l], it + 1)
                        pe.wait_ge(tok_copied[l], it * 2 + 2)
                        pe.wait_ge(t1_masked[l], it * LEVELS + LEVELS)
                        for u, (jj, hh) in enumerate(units):
                            to = bank(l, (3, 0)[hh])[:, jj * 64:jj * 64 + 64]
                            nc.tensor.matmul(to, data[d][half(hh), 2 * l + jj, 0, :], mid[l][half(hh), jj, :], start=True, stop=False)
                            mm = nc.tensor.matmul(to, am[l][:, u, 1, 0, :], tok[l][:, jj, 2, half(hh)], start=False, stop=True)
                        mm.then_inc(g_ps[l], 1)
                    for l in lanes:
                        pe.wait_ge(g_copied[l], it + 1)
                        pe.wait_ge(inv_t_ready[l], it * LEVELS + LEVELS)
                        for u in range(4):
                            mm = nc.tensor.matmul(bank(l, 1)[:, u * 64:u * 64 + 64], inv_t[l][:, u, :], g[l][:, u, :], start=True, stop=True)
                        mm.then_inc(u_ps[l], 1)
                    for l in lanes:
                        pe.wait_ge(u_copied[l], it + 1)
                        for u, (jj, hh) in enumerate(units):
                            to = bank(l, 2 + hh)[half(hh), jj * P:jj * P + P]
                            nc.tensor.matmul(to, uu[l][:, u, :], am[l][:, u, 0, 1, :], start=True, stop=False)
                            nc.tensor.matmul(to, tok[l][:, jj, 2, half(hh)], am[l][:, u, 1, 1, :], start=False, stop=False)
                            mm = nc.tensor.matmul(to, mid[l][half(hh), jj, :], data[d][half(hh), 2 * l + jj, 1, :], start=False, stop=True)
                        mm.then_inc(y_ps[l], 1)
                        for u, (jj, hh) in enumerate(units):
                            to = bank(l, 0)[half(hh), jj * 64:jj * 64 + 64]
                            nc.tensor.matmul(to, tok[l][:, jj, 0, half(hh)], uu[l][:, u, :], start=True, stop=False)
                            mm = nc.tensor.matmul(to, tok[l][:, jj, 1, half(hh)], tok[l][:, jj, 2, half(hh)], start=False, stop=True)
                        mm.then_inc(s_ps[l], 1)

        @block.scalar
        def _(act):
            for l in lanes:
                act.sem_inc(y_copied[l], 1)
            with act.Fori(0, NT) as n:
                for d in range(2):
                    it = n * 2 + d
                    for jj in range(2):
                        for l in lanes:
                            act.wait_ge(turned[l], it * 2 + jj + 1)
                            nc.scalar.activation(tok[l][:, jj, :, :].rearrange("p k t -> p (k t)"), bank(l, 3)[:, 0:3 * P], ACT.Copy).then_inc(tok_copied[l], 1)
                    for l in lanes:
                        act.wait_ge(g_ps[l], it + 1)
                        for hh in range(2):
                            c = nc.scalar.activation(g[l][:, hh::2, :], bank(l, (3, 0)[hh])[:, 0:P].rearrange("p (j v) -> p j v", v=64), ACT.Copy)
                        c.then_inc(g_copied[l], 1)
                    for l in lanes:
                        act.wait_ge(u_ps[l], it + 1)
                        nc.scalar.activation(uu[l][:, :, :].rearrange("p u v -> p (u v)"), bank(l, 1)[:, 0:256], ACT.Copy).then_inc(u_copied[l], 1)
                    act.wait_ge(y_free, it + 1)
                    for l in lanes:
                        act.wait_ge(y_ps[l], it + 1)
                        for hh in range(2):
                            half = slice(64 * hh, 64 * hh + 64)
                            c = nc.scalar.activation(y[d][half, 2 * l:2 * l + 2, :], bank(l, 2 + hh)[half, 0:256].rearrange("p (j t) -> p j t", t=P), ACT.Copy)
                        c.then_inc(y_copied[l], 1)

        @block.vector
        def _(dve):
            dve.sem_inc(y_free, 2)
            for d in range(2):
                for l in lanes:
                    nc.vector.memset(state[d][l][:], 0.0).then_inc(zeroed, 1)
            dve.wait_ge(zeroed, 4)
            for l in lanes:
                dve.sem_inc(state_ready[l], 1)
            dve.wait_ge(masks_in, 32)
            four = lambda x: x.rearrange("p (u t) -> p u t", t=P)
            with dve.Fori(0, NT) as n:
                for d in range(2):
                    it = n * 2 + d
                    decay = lambda l, jj: half_decay[:, d, bass.ds(n, 1), 2 * l + jj]
                    for l in lanes:
                        for u in range(4):
                            dve.wait_ge(pairs_ps[l], it * 4 + u + 1)
                            m = nc.vector.tensor_tensor(
                                am[l][:, u, :, :, :].rearrange("p q r t -> p q (r t)"), bank(l, u).rearrange("p (q c) -> p q c", q=2),
                                pair_mask[:, d:d + 1, :, :].rearrange("p o r t -> p o (r t)").broadcast_to((P, 2, 2 * P)), ALU.mult)
                        m.then_inc(pairs_masked[l], 1)
                        for jj in range(2):
                            c = nc.vector.tensor_scalar(mid[l][:, jj, :], state[d][l][:, jj, :], decay(l, jj), None, ALU.mult)
                        c.then_inc(mid_ready[l], 1)
                        dve.wait_ge(mid_ready[l], it + 1)
                        for jj in range(2):
                            c = nc.vector.tensor_scalar(far[l][:, jj, :], mid[l][:, jj, :], decay(l, jj), None, ALU.mult)
                        c.then_inc(link, 1)
                    for v in range(LEVELS):
                        for l in lanes:
                            dve.wait_ge(t1_ps[l], it * LEVELS + v + 1)
                            nc.vector.tensor_tensor(t1[l][:], four(bank(l, 0)), level_mask[:, 1 - d, v:v + 1, :].broadcast_to((P, 4, P)), ALU.mult).then_inc(t1_masked[l], 1)
                        for l in lanes:
                            if v == 0:
                                dve.wait_ge(t1_masked[l], it * LEVELS + 1)
                                nc.vector.tensor_tensor(inv[l][:], t1[l][:], ident4, ALU.add).then_inc(inv_ready[l], 1)
                                continue
                            dve.wait_ge(joined_ps[l], it * (LEVELS - 1) + v)
                            if v < LEVELS - 1:
                                dve.wait_ge(inv_ready[l], it * (LEVELS - 1) + v)
                                nc.vector.tensor_tensor(inv[l][:], four(bank(l, 1)), inv[l][:], ALU.add).then_inc(inv_ready[l], 1)
                            dve.wait_ge(inv_t_ready[l], it * LEVELS + v)
                            nc.vector.tensor_tensor(inv_t[l][:], four(bank(l, 2)), inv_t[l][:], ALU.add).then_inc(inv_t_ready[l], 1)
                    dve.wait_ge(link, it * 2 + 2)
                    for l in lanes:
                        dve.wait_ge(s_ps[l], it + 1)
                        for jj in range(2):
                            c = nc.vector.scalar_tensor_tensor(out=state[d][l][:, jj, :], in0=bank(l, 0)[:, jj * 64:jj * 64 + 64],
                                                               scalar=decay(l, jj), in1=far[l][:, jj, :], op0=ALU.mult, op1=ALU.add)
                        c.then_inc(state_ready[l], 1)
                        dve.wait_ge(state_ready[l], it + 2)

        @block.gpsimd
        def _(pool):
            pool.wait_ge(masks_in, 32)
            with pool.Fori(0, NT) as n:
                for d in range(2):
                    it = n * 2 + d
                    for l in lanes:
                        pool.wait_ge(pairs_masked[l], it + 1)
                        nc.gpsimd.tensor_tensor(inv_t[l][:], am[l][:, :, 0, 0, :], level_mask[:, d, 0:1, :].broadcast_to((P, 4, P)), ALU.mult).then_inc(first_cut[l], 1)
                        pool.wait_ge(first_cut[l], it + 1)
                        nc.gpsimd.tensor_tensor(inv_t[l][:], inv_t[l][:], ident4, ALU.add).then_inc(inv_t_ready[l], 1)


def mixing_out(kit, y_steps, gate, bonus, y_all):
    nc = kit.nc
    with Stage(nc) as st:
        sb = lambda name: [st.enter_context(nc.sbuf_tensor(f"mo_{name}{u}", [P, N], F32)) for u in range(2)]
        sem = lambda name: [st.sem(f"mo_{name}{u}") for u in range(2)]
        fwd, bwd, gt, bn, sq, rs = (sb(x) for x in ("fwd", "bwd", "gt", "bn", "sq", "rs"))
        ps = [st.enter_context(nc.psum_tensor(f"mo_ps{u}", [P, 3, BANK], F32)) for u in range(2)]
        flat = [x[:, :, :].rearrange("p b c -> p (b c)")[:, 0:N] for x in ps]
        loaded, both, mean_ps, centred, squared, var_ps, var_read, root, scaled, affine, summed, ready, stored, tiles_free = (
            sem(x) for x in ("loaded", "both", "mean_ps", "centred", "squared", "var_ps", "var_read", "root",
                             "scaled", "affine", "summed", "ready", "stored", "tiles_free"))
        per_turn = 16 * 13
        block = st.enter_context(nc.Block("mixing_out"))

        @block.sync
        def _(sp):
            with sp.Fori(0, 2) as i:
                for u in range(2):
                    sp.wait_ge(tiles_free[u], i + 1)
                    at = bass.ds(i * 2 + u, 1)
                    sp.dma_start(fwd[u][:, :].rearrange("p (n t) -> p n t", t=P), y_steps[0, :, :, at, :].rearrange("n p o t -> p n (o t)")).then_inc(loaded[u], 16)
                    for c in range(NT):
                        sp.dma_start(bwd[u][:, c * P:(c + 1) * P], y_steps[1, STEP_OF[1][c], :, at, :].rearrange("p o t -> p (o t)")).then_inc(loaded[u], 16)
                    sp.dma_start(gt[u][:], gate[at, :, :].rearrange("o p n -> p (o n)")).then_inc(loaded[u], 16)
                    sp.dma_start(bn[u][:], bonus[at, :, :].rearrange("o p n -> p (o n)")).then_inc(loaded[u], 16)
                for u in range(2):
                    sp.wait_ge(ready[u], i + 1)
                    sp.dma_start(y_all[bass.ds(i * 2 + u, 1), :, :].rearrange("o p n -> p (o n)"), fwd[u][:]).then_inc(stored[u], 16)
                    sp.wait_ge(stored[u], i * 16 + 16)
                    sp.sem_inc(tiles_free[u], 1)

        @block.tensor
        def _(pe):
            with pe.Fori(0, 2) as i:
                for ready_sem, src, out in ((both, fwd, mean_ps), (squared, sq, var_ps)):
                    for u in range(2):
                        pe.wait_ge(ready_sem[u], i + 1)
                        for n, (s, e) in enumerate(SEGS):
                            mm = nc.tensor.matmul(ps[u][:, n, 0:e - s], kit.head_ones[:], src[u][:, s:e], start=True, stop=True)
                        mm.then_inc(out[u], 1)

        @block.scalar
        def _(act):
            nc.scalar.preload_act_table_set(LN_EXP)
            with act.Fori(0, 2) as i:
                for u in range(2):
                    act.wait_ge(centred[u], i + 1)
                    nc.scalar.activation(sq[u][:], fwd[u][:], ACT.Square).then_inc(squared[u], 1)
                for u in range(2):
                    act.wait_ge(var_ps[u], i + 1)
                    nc.scalar.activation(rs[u][:], flat[u], ACT.Ln, scale=1.0 / 64, bias=kit.eps[:, 1:2]).then_inc(var_read[u], 1)
                    act.wait_ge(var_read[u], i + 1)
                    nc.scalar.activation(rs[u][:], rs[u][:], ACT.Exp, scale=-0.5).then_inc(root[u], 1)
                for u in range(2):
                    act.wait_ge(scaled[u], i + 1)
                    nc.scalar.activation(fwd[u][:], fwd[u][:], ACT.Identity, scale=kit.cols[:, bass.ds(i * 2 + (u + col("ln_w")), 1)],
                                         bias=kit.cols[:, bass.ds(i * 2 + (u + col("ln_b")), 1)]).then_inc(affine[u], 1)

        @block.vector
        def _(dve):
            for u in range(2):
                dve.sem_inc(tiles_free[u], 1)
            with dve.Fori(0, 2) as i:
                for u in range(2):
                    dve.wait_ge(loaded[u], i * per_turn + per_turn)
                    nc.vector.tensor_tensor(fwd[u][:], fwd[u][:], bwd[u][:], ALU.add).then_inc(both[u], 1)
                for u in range(2):
                    dve.wait_ge(mean_ps[u], i + 1)
                    nc.vector.scalar_tensor_tensor(out=fwd[u][:], in0=flat[u], scalar=-1.0 / 64, in1=fwd[u][:], op0=ALU.mult, op1=ALU.add).then_inc(centred[u], 1)
                for u in range(2):
                    dve.wait_ge(root[u], i + 1)
                    nc.vector.tensor_tensor(fwd[u][:], fwd[u][:], rs[u][:], ALU.mult).then_inc(scaled[u], 1)
                for u in range(2):
                    dve.wait_ge(affine[u], i + 1)
                    nc.vector.tensor_tensor(fwd[u][:], fwd[u][:], bn[u][:], ALU.add).then_inc(summed[u], 1)
                    dve.wait_ge(summed[u], i + 1)
                    nc.vector.tensor_tensor(fwd[u][:], fwd[u][:], gt[u][:], ALU.mult).then_inc(ready[u], 1)


EXPERTS, GROUPS, MEMBERS = 16, 4, 4
HEADS = 8
QK = 96
Q_RANK, KV_RANK = 256, 128
SCALE = QK ** -0.5


def attention(kit, p, y_all, xb, yb):
    nc, a = kit.nc, kit.args
    with Stage(nc) as st:
        sb = lambda name, shape: st.enter_context(nc.sbuf_tensor(f"at_{name}", list(shape), F32))
        sem = lambda name: st.sem(f"at_{name}")
        pq = sb("pq", (P, 2, N))
        pkv = sb("pkv", (P, N))
        sq = [sb(f"sq{i}", (P, N)) for i in range(2)]
        rs = [sb(f"rs{i}", (P, N)) for i in range(2)]
        raw = [sb(f"raw{i}", (QK, N)) for i in range(2)]
        nrm = [[sb(f"nrm{u}{i}", (QK, N)) for i in range(2)] for u in range(2)]
        rot_sin = sb("rot_sin", (QK, SEQ))
        cos, sin = sb("cos", (QK, SEQ)), sb("sin", (QK, SEQ))
        rot = sb("rot", (QK, QK))
        w_v = sb("w_v", (P, HEADS * 64))
        wq, wk = sb("wq", (P, 2, QK)), sb("wk", (P, 64))
        v_tok, o_tok = sb("v_tok", (P, NT, HEADS * 64)), sb("o_tok", (P, NT, HEADS * 64))
        prob = [sb(f"prob{i}", (P, N)) for i in range(2)]
        prob_t = [sb(f"prob_t{i}", (P, NT, P)) for i in range(2)]
        top, neg_top, total, inv_total = (sb(x, (P, NT)) for x in ("top", "neg_top", "total", "inv_total"))
        zero = sb("zero", (P, D))
        zeroed, zero_out = sem("zeroed"), sem("zero_out")
        ps = st.enter_context(nc.psum_tensor("at_ps", [P, 8, BANK], F32))
        group = lambda i: ps[:, 3 * i:3 * i + 3, :].rearrange("p b c -> p (b c)")
        turn_bank = lambda i: ps[:, 6 + i % 2, :]
        s_in, w_in = sem("s_in"), sem("w_in")
        squared, summed, root, normed = sem("squared"), sem("summed"), sem("root"), sem("normed")
        v_ps, v_copied = sem("v_ps"), sem("v_copied")
        act_ps, act_read, dve_ps, dve_read, rooted, hnorm, roped = (sem(x) for x in (
            "act_ps", "act_read", "dve_ps", "dve_read", "rooted", "hnorm", "roped"))
        scores, top_ready, exped, inv_ready = (sem(x) for x in ("scores", "top_ready", "exped", "inv_ready"))
        link, y_turned, y_moved, stored = sem("link"), sem("y_turned"), sem("y_moved"), sem("stored")
        keys = [NTC if t < NTC else NT for t in range(NT)]
        turns = [[(s, min(s + 4, k)) for s in range(0, k, 4)] for k in keys]

        setup = st.enter_context(ExitStack())
        block = setup.enter_context(nc.Block("attention_inputs"))

        @block.sync
        def _(sp):
            for i in range(2):
                sp.dma_start(pq[:, i, :], p[Q_CH + i, :, :]).then_inc(s_in, 16)
            sp.dma_start(pkv[:], p[KV_CH, :, :]).then_inc(s_in, 16)
            sp.dma_start(raw[1][64:QK, :], p[KR_CH, 0:32, :]).then_inc(s_in, 16)
            for t, name in ((cos, "cos"), (sin, "sin"), (rot, "rot"), (w_v, "w_v")):
                sp.dma_start(t[:], a[name][:, :]).then_inc(s_in, 16)

        @block.scalar
        def _(act):
            nc.scalar.preload_act_table_set(LN_EXP)
            act.wait_ge(s_in, 128)
            for i, src in enumerate((pq[:, 0, :], pq[:, 1, :], pkv[:])):
                if i == 2:
                    act.wait_ge(summed, 1)
                nc.scalar.activation(sq[i % 2][:], src, ACT.Square).then_inc(squared, 1)
            nc.scalar.activation(rs[0][64:QK, :], raw[1][64:QK, :], ACT.Square).then_inc(squared, 1)
            for i, rank in enumerate((Q_RANK, KV_RANK)):
                act.wait_ge(summed, 2 + i)
                nc.scalar.activation(prob[i][:], group(i)[:, 0:N], ACT.Ln, scale=1.0 / rank, bias=kit.eps[:, 0:1]).then_inc(root, 1)
                act.wait_ge(root, 2 * i + 1)
                nc.scalar.activation(prob[i][:], prob[i][:], ACT.Exp, scale=-0.5).then_inc(root, 1)
            for t in range(NT):
                act.wait_ge(v_ps, t + 1)
                nc.scalar.activation(v_tok[:, t, :], turn_bank(t), ACT.Copy).then_inc(v_copied, 1)

        @block.tensor
        def _(pe):
            for i in range(3):
                pe.wait_ge(squared, i + 1)
                for n, (s, e) in enumerate(SEGS):
                    mm = nc.tensor.matmul(group(i // 2)[:, s:e], kit.ones[:], sq[i % 2][:, s:e], start=i != 1, stop=i != 0)
                mm.then_inc(summed, 1)
            pe.wait_ge(normed, 3)
            for t in range(NT):
                if t >= 2:
                    pe.wait_ge(v_copied, t - 1)
                nc.tensor.matmul(turn_bank(t), pkv[:, t * P:(t + 1) * P], w_v[:], start=True, stop=True).then_inc(v_ps, 1)

        @block.vector
        def _(dve):
            dve.wait_ge(squared, 4)
            dve.wait_ge(summed, 3)
            nc.vector.tensor_copy(sq[1][64:QK, :], rs[0][64:QK, :]).then_inc(link, 1)
            for i, src in enumerate((pq[:, 0, :], pq[:, 1, :], pkv[:])):
                dve.wait_ge(root, 2 if i < 2 else 4)
                nc.vector.scalar_tensor_tensor(out=src, in0=src, scalar=kit.cols[:, col("q_norm", i):][:, 0:1], in1=prob[i // 2][:],
                                               op0=ALU.mult, op1=ALU.mult).then_inc(normed, 1)

        setup.close()
        block = st.enter_context(nc.Block("attention_heads"))
        rows = (QK, 64)
        tiles = list(range(NTC, NT)) + list(range(NTC))
        prep = ([("proj", i, n) for i in range(2) for n in range(3)] + [("sum", i, n) for i in range(2) for n in range(3)]
                + [("rot", i, n) for i in range(2) for n in range(2)])
        reader = lambda item: "act" if item[0] in ("proj", "sum", "out") else "dve"
        PREP_ACT, ROTS, LINKS = 12, 4, NT + 4

        def step_items(k, with_prep):
            t = tiles[k]
            out = [("turn", k, s, e) for s, e in turns[t]]
            if with_prep and k < 8:
                out = out[:2] + prep[2 * k:2 * k + 1] + out[2:] + prep[2 * k + 1:2 * k + 2]
            return out + [("out", k)]

        full = [x for k in range(NT) for x in step_items(k, True)]
        dve_items = sum(reader(x) == "dve" for x in full)
        act_items = len(full) - dve_items
        projected = sum(reader(x) == "act" for x in full[:full.index(("proj", 1, 2)) + 1])

        class Banks:

            def __init__(self, head=None):
                self.m = 0
                self.counts = {"act": 0, "dve": 0}
                self.base = {"act": 0, "dve": 0} if head is None else {"act": head * act_items + PREP_ACT, "dve": head * dve_items + ROTS}
                self.before = [None, None] if head is None else [("dve", self.base["dve"]), ("act", self.base["act"])]
                self.squares = {}

            def next(self, item):
                who = reader(item)
                self.counts[who] += 1
                count = self.base[who] + self.counts[who]
                bank, earlier = self.m % 2, self.before.pop(0)
                self.before.append((who, count))
                if item[0] == "proj":
                    self.squares[item[1:]] = count
                self.m += 1
                return bank, who, count, earlier

        assert len(full) % 2 == 0 and len(prep) % 2 == 0

        @block.gpsimd
        def _(pool):
            nc.gpsimd.memset(zero[:], 0.0).then_inc(zeroed, 1)
            pool.wait_ge(zeroed, 1)
            blocks = [xb[s:s + P, :] for s in range(N, xb.shape[0], P)] + [yb[s:s + P, :] for s in range(N + EXPERTS * P, yb.shape[0], P)]
            for b in blocks:
                pool.dma_start(b, zero[:]).then_inc(zero_out, 16)
            pool.wait_ge(zero_out, 16 * len(blocks))

        @block.sync
        def _(sp):
            def load(h):
                sp.dma_start(wq[:], a["w_q"][:, :, bass.ds(h * QK, QK)]).then_inc(w_in, 16)
                sp.dma_start(wk[:], a["w_k"][:, bass.ds(h * 64, 64)]).then_inc(w_in, 16)

            load(0)
            sp.wait_ge(act_ps, 6)
            load(1)
            with sp.Fori(2, HEADS) as h:
                sp.wait_ge(act_ps, h * act_items + (PREP_ACT - 2 * act_items + projected))
                load(h)
            for j in range(4):
                sp.wait_ge(y_moved, 3 * (j + 1))
                sp.dma_start(y_all[4 + j, :, :], (pq[:, 0, :], pq[:, 1, :], pkv[:], prob[0][:])[j]).then_inc(stored, 16)
            sp.wait_ge(stored, 64)

        @block.tensor
        def _(pe):
            def use(banks, item, par, g, h):
                bank, who, count, earlier = banks.next(item)
                if earlier:
                    pe.wait_ge({"act": act_read, "dve": dve_read}[earlier[0]], earlier[1])
                to = ps[:, 6 + bank, :]
                if item[0] == "turn":
                    _, k, s, e = item
                    for b in range(s, e):
                        mm = nc.tensor.transpose(to[:, (b - s) * P:(b - s + 1) * P], prob[k % 2][:, b * P:(b + 1) * P], kit.ident[:])
                elif item[0] == "out":
                    k = item[1]
                    pe.wait_ge(dve_read, banks.base["dve"] + banks.counts["dve"])
                    for b in range(keys[tiles[k]]):
                        mm = nc.tensor.matmul(to[:, 0:64], prob_t[k % 2][:, b, :], v_tok[:, b, bass.ds(h * 64, 64)],
                                              start=b == 0, stop=b == keys[tiles[k]] - 1)
                else:
                    kind, i, n = item
                    s, e = SEGS[n]
                    if kind == "proj":
                        if i == 0:
                            if n == 0:
                                pe.wait_ge(w_in, g * 32 + 32)
                            for c in range(2):
                                mm = nc.tensor.matmul(to[0:QK, 0:e - s], wq[:, c, :], pq[:, c, s:e], start=c == 0, stop=c == 1)
                        else:
                            mm = nc.tensor.matmul(to[0:64, 0:e - s], wk[:], pkv[:, s:e], start=True, stop=True)
                    elif kind == "sum":
                        pe.wait_ge(act_read, banks.squares[i, n])
                        mm = nc.tensor.matmul(to[0:QK, 0:e - s], kit.ones[0:QK, 0:QK], sq[i][0:QK, s:e], start=True, stop=True)
                    else:
                        pe.wait_ge(hnorm, g * 2 + (i + 1))
                        mm = nc.tensor.matmul(to[0:QK, :], rot[:], nrm[par][i][:, CTX + n * BANK:CTX + (n + 1) * BANK], start=True, stop=True)
                mm.then_inc({"act": act_ps, "dve": dve_ps}[who], 1)

            def score(k, par, h):
                if k == 0:
                    pe.wait_ge(roped, h * ROTS + ROTS)
                t = tiles[k]
                for s in range(0, keys[t] * P, BANK):
                    e = min(s + BANK, keys[t] * P)
                    mm = nc.tensor.matmul(group(k % 2)[:, s:e], nrm[par][0][:, t * P:(t + 1) * P], nrm[par][1][:, s:e], start=True, stop=True)
                mm.then_inc(scores, 1)

            def head(h, par, last=False):
                banks = Banks(h)
                for k, t in enumerate(tiles):
                    if k + 1 < NT:
                        score(k + 1, par, h)
                    elif not last:
                        score(0, 1 - par, h + 1)
                    pe.wait_ge(exped, h * NT + (k + 1))
                    for item in step_items(k, not last):
                        use(banks, item, 1 - par, h + 1, h)

            banks = Banks()
            for item in prep:
                use(banks, item, 0, 0, 0)
            score(0, 0, 0)
            with pe.Fori(0, HEADS // 2 - 1) as i:
                for u in range(2):
                    head(i * 2 + u, u)
            head(HEADS - 2, 0)
            head(HEADS - 1, 1, last=True)
            pe.wait_ge(act_read, HEADS * act_items)
            for j in range(4):
                for n, (s, e) in enumerate(SEGS):
                    m = j * 3 + n
                    if m >= 2:
                        pe.wait_ge(y_moved, m - 1)
                    for t in range(s // P, e // P):
                        mm = nc.tensor.transpose(turn_bank(m)[:, t * P - s:t * P - s + P], o_tok[:, t, j * P:(j + 1) * P], kit.ident[:])
                    mm.then_inc(y_turned, 1)

        @block.scalar
        def _(act):
            def read(banks, item, g, first=False):
                bank, who, count, _ = banks.next(item)
                if who != "act":
                    return
                kind, i, n = item
                s, e = SEGS[n]
                from_ = ps[:, 6 + bank, 0:e - s]
                act.wait_ge(act_ps, count)
                if kind == "proj":
                    if n == 0 and not first:
                        act.wait_ge(hnorm, g * 2 + (i - 1))
                    nc.scalar.activation(raw[i][0:rows[i], s:e], from_[0:rows[i], :], ACT.Copy)
                    nc.scalar.activation(sq[i][0:rows[i], s:e], from_[0:rows[i], :], ACT.Square).then_inc(act_read, 1)
                else:
                    nc.scalar.activation(rs[i][0:QK, s:e], from_[0:QK, :], ACT.Ln, scale=1.0 / QK, bias=kit.eps[0:QK, 0:1]).then_inc(act_read, 1)
                    act.wait_ge(act_read, count)
                    nc.scalar.activation(rs[i][0:QK, s:e], rs[i][0:QK, s:e], ACT.Exp, scale=-0.5).then_inc(rooted, 1)

            def drain(k, h, bank, count):
                t = tiles[k]
                act.wait_ge(act_ps, count)
                act.wait_ge(inv_ready, h * NT + (k + 1))
                nc.scalar.activation(o_tok[:, t, bass.ds(h * 64, 64)], ps[:, 6 + bank, 0:64], ACT.Copy,
                                     scale=inv_total[:, t:t + 1]).then_inc(act_read, 1)

            def head(h, last=False):
                banks = Banks(h)
                for k, t in enumerate(tiles):
                    act.wait_ge(top_ready, h * NT + (k + 1))
                    width = keys[t] * P
                    nc.scalar.activation(prob[k % 2][:, 0:width], group(k % 2)[:, 0:width], ACT.Exp, scale=SCALE,
                                         bias=neg_top[:, t:t + 1], accum_out=total[:, t:t + 1]).then_inc(exped, 1)
                    if k:
                        drain(k - 1, h, *out)
                    *items, product = step_items(k, not last)
                    for item in items:
                        read(banks, item, h + 1)
                    bank, _, count, _ = banks.next(product)
                    out = bank, count
                drain(NT - 1, h, *out)

            nc.scalar.preload_act_table_set(LN_EXP)
            banks = Banks()
            for item in prep:
                read(banks, item, 0, first=True)
            with act.Fori(0, HEADS // 2 - 1) as i:
                for u in range(2):
                    head(i * 2 + u)
            head(HEADS - 2)
            head(HEADS - 1, last=True)

        @block.vector
        def _(dve):
            def norm(i, par, g):
                dve.wait_ge(rooted, g * 6 + (3 * i + 3))
                nc.vector.scalar_tensor_tensor(out=nrm[par][i][:], in0=raw[i][:], scalar=kit.cols[0:QK, col("q_gain", i):][:, 0:1],
                                               in1=rs[i][0:QK, :], op0=ALU.mult, op1=ALU.mult).then_inc(hnorm, 1)

            def read(banks, item, own, par, g):
                bank, who, count, _ = banks.next(item)
                if who != "dve":
                    return
                dve.wait_ge(dve_ps, count)
                if item[0] == "turn":
                    _, k, s, e = item
                    nc.vector.tensor_copy(prob_t[k % 2][:, s:e, :], ps[:, 6 + bank, 0:(e - s) * P].rearrange("p (k t) -> p k t", t=P)).then_inc(dve_read, 1)
                    return
                _, i, n = item
                at = slice(n * BANK, (n + 1) * BANK)
                to = nrm[par][i][:, CTX + n * BANK:CTX + (n + 1) * BANK]
                nc.vector.tensor_tensor(rot_sin[:, at], ps[0:QK, 6 + bank, :], sin[:, at], ALU.mult).then_inc(dve_read, 1)
                own(nc.vector.tensor_tensor(to, to, cos[:, at], ALU.mult))
                dve.wait_ge(dve_read, count)
                nc.vector.tensor_tensor(to, to, rot_sin[:, at], ALU.add).then_inc(roped, 1)
                dve.wait_ge(roped, g * ROTS + (2 * i + n + 1))

            def tops(k, own, h):
                t = tiles[k]
                dve.wait_ge(scores, h * NT + (k + 1))
                own(nc.vector.reduce_max(top[:, t:t + 1], group(k % 2)[:, 0:keys[t] * P], AX.X))
                nc.vector.tensor_scalar(neg_top[:, t:t + 1], top[:, t:t + 1], -SCALE, None, ALU.mult).then_inc(top_ready, 1)

            def head(h, par, last=False):
                own = Link(dve, link, h * LINKS + (ROTS + 2))
                banks = Banks(h)
                for k, t in enumerate(tiles):
                    dve.wait_ge(exped, h * NT + (k + 1))
                    nc.vector.reciprocal(inv_total[:, t:t + 1], total[:, t:t + 1]).then_inc(inv_ready, 1)
                    for item in step_items(k, not last):
                        read(banks, item, own, 1 - par, h + 1)
                        if item[:1] + item[3:] == ("turn", keys[t]):
                            if k + 1 < NT:
                                tops(k + 1, own, h)
                            elif not last:
                                tops(0, own, h + 1)
                            if k in (5, 6) and not last:
                                norm(k - 5, 1 - par, h + 1)

            own = Link(dve, link, 1)
            banks = Banks()
            for m, item in enumerate(prep):
                if m == 12:
                    norm(0, 0, 0)
                    norm(1, 0, 0)
                    dve.wait_ge(hnorm, 2)
                read(banks, item, own, 0, 0)
            tops(0, own, 0)
            with dve.Fori(0, HEADS // 2 - 1) as i:
                for u in range(2):
                    head(i * 2 + u, u)
            head(HEADS - 2, 0)
            head(HEADS - 1, 1, last=True)
            for j in range(4):
                for n, (s, e) in enumerate(SEGS):
                    dve.wait_ge(y_turned, j * 3 + n + 1)
                    nc.vector.tensor_copy((pq[:, 0, :], pq[:, 1, :], pkv[:], prob[0][:])[j][:, s:e], turn_bank(j * 3 + n)[:, 0:e - s]).then_inc(y_moved, 1)


def project_out(kit, name, y, weights, x, gate, lo, load_y=None, load_x=None):
    nc = kit.nc
    parts = [q for q in PARTS if q[1] > lo]
    segs = list(SEGS) if lo == 0 else [(lo, lo + 512), (lo + 512, N)]
    with Stage(nc) as st:
        sem = lambda s: st.sem(f"{name}_{s}")
        w = [st.enter_context(nc.sbuf_tensor(f"{name}_w{u}", [P, KD, P], F32)) for u in range(2)]
        w_parts = [[st.enter_context(nc.sbuf_tensor(f"{name}_w{x}{u}", [P, KD, P], F32R)) for x in ("high", "low")] for u in range(2)]
        y_parts = [st.enter_context(nc.sbuf_tensor(f"{name}_y_{x}", [P, KD, N - lo], F32R)) for x in ("high", "low")]
        y_cut, y_split, w_cut, w_split = sem("y_cut"), sem("y_split"), sem("w_cut"), sem("w_split")
        ps = [st.enter_context(nc.psum_tensor(f"{name}_ps{u}", [P, 3, BANK], F32)) for u in range(2)]
        w_in = [sem(f"w_in{u}") for u in range(2)]
        y_in = [sem(f"y_in{k}") for k in range(KD)]
        x_in, multiplied, added = sem("x_in"), sem("multiplied"), sem("added")
        block = st.enter_context(nc.Block(name))

        @block.sync
        def _(sp):
            if load_y is not None:
                for k in range(KD):
                    sp.dma_start(y[:, k, :], load_y[k, :, :]).then_inc(y_in[k], 16)
            if load_x is not None:
                for k in range(KD):
                    for s, e, v in parts:
                        sp.dma_start(x[:, k, s:e], load_x[v][k * P:(k + 1) * P, :]).then_inc(x_in, 16)
            with sp.Fori(0, KD // 2) as i:
                for u in range(2):
                    sp.wait_ge(w_split, free(i * 2 + u))
                    sp.dma_start(w[u][:], weights[:, :, bass.ds(i * 256 + u * P, P)]).then_inc(w_in[u], 16)

        @block.tensor
        def _(pe):
            pe.sem_inc(multiplied, 2)

            def chunk(m, u, first=False):
                pe.wait_ge(w_split, done(m))
                pe.wait_ge(added, free(m))
                for k in range(KD):
                    if first:
                        pe.wait_ge(y_split, k + 1)
                    for n, (s, e) in enumerate(segs):
                        mm = product3(nc, ps[u][:, n, 0:e - s], [x[:, k, :] for x in w_parts[u]], [x[:, k, s - lo:e - lo] for x in y_parts], k == 0, k == KD - 1)
                mm.then_inc(multiplied, 1)

            chunk(0, 0, first=True)
            chunk(1, 1)
            with pe.Fori(1, KD // 2) as i:
                for u in range(2):
                    chunk(i * 2 + u, u)

        @block.vector
        def _(dve):
            def split_weights(m, u, i):
                dve.wait_ge(w_in[u], i * 16 + 16)
                dve.wait_ge(multiplied, free(m))
                split(nc, w_parts[u][0][:], w_parts[u][1][:], w[u][:], (w_cut, m + 1), w_split)

            def add(m, u):
                dve.wait_ge(multiplied, done(m))
                flat = ps[u][:, :, :].rearrange("p b c -> p (b c)")
                for s, e, v in parts:
                    here = x[:, bass.ds(m, 1), s:e].rearrange("p o n -> p (o n)")
                    t = nc.vector.scalar_tensor_tensor(out=here, in0=flat[:, s - lo:e - lo], scalar=kit.mod[:, bass.ds(m + gate, 1), v],
                                                       in1=here, op0=ALU.mult, op1=ALU.add)
                t.then_inc(added, 1)

            dve.sem_inc(added, 2)
            dve.sem_inc(w_split, 2)
            split_weights(0, 0, 0)
            for k in range(KD):
                if load_y is not None:
                    dve.wait_ge(y_in[k], 16)
                split(nc, y_parts[0][:, k, :], y_parts[1][:, k, :], y[:, k, lo:], (y_cut, k + 1), y_split)
            if load_x is not None:
                dve.wait_ge(x_in, 16 * KD * len(parts))
            split_weights(1, 1, 0)
            add(0, 0)
            with dve.Fori(1, KD // 2) as i:
                for u in range(2):
                    split_weights(i * 2 + u, u, i)
                    add(i * 2 + (u - 1), 1 - u)
            add(KD - 1, 1)


def fourier(kit, h, f):
    nc, a = kit.nc, kit.args
    lat = SEQ // P
    with Stage(nc) as st:
        sb = lambda name, shape: st.enter_context(nc.sbuf_tensor(f"ft_{name}", list(shape), F32))
        sem = lambda name: st.sem(f"ft_{name}")
        chan = sb("chan", (P, 2 * P))
        pos = sb("pos", (P, 2, lat, SEQ))
        mid = [sb(f"mid{u}", (P, lat, 2 * P)) for u in range(2)]
        ps_c = [st.enter_context(nc.psum_tensor(f"ft_psc{u}", [P, 2, 2 * P], F32)) for u in range(2)]
        ps_f = [st.enter_context(nc.psum_tensor(f"ft_psf{u}", [P, 2, BANK], F32)) for u in range(2)]
        chan_in, pos_in = sem("chan_in"), [sem(f"pos_in{q}") for q in range(4)]
        chan_ps, mid_kept, f_ps, f_kept = sem("chan_ps"), sem("mid_kept"), sem("f_ps"), sem("f_kept")
        block = st.enter_context(nc.Block("fourier"))

        @block.sync
        def _(sp):
            sp.dma_start(chan[:], a["dft_chan"][:, :]).then_inc(chan_in, 16)
            for n in range(2):
                for q in range(2):
                    at = slice(n * BANK, (n + 1) * BANK)
                    sp.dma_start(pos[:, q, :, at], a["dft_pos"][:, q, :, at]).then_inc(pos_in[2 * n + q], 16)

        @block.tensor
        def _(pe):
            def channels(g):
                for t2 in range(lat // 2):
                    m = g * 4 + t2
                    if m >= 2:
                        pe.wait_ge(mid_kept, m - 1)
                    for t in range(2):
                        s = CTX + (2 * t2 + t) * P
                        mm = nc.tensor.matmul(ps_c[m % 2][:, t, :], h[:, g, s:s + P], chan[:], start=True, stop=True)
                    mm.then_inc(chan_ps, 1)

            pe.wait_ge(chan_in, 16)
            channels(0)
            for g in range(KD):
                if g + 1 < KD:
                    channels(g + 1)
                pe.wait_ge(mid_kept, g * 4 + 4)
                if g >= 2:
                    pe.wait_ge(f_kept, g - 1)
                for n in range(2):
                    for q in range(2):
                        if g == 0:
                            pe.wait_ge(pos_in[2 * n + q], 16)
                        for t in range(lat):
                            mm = nc.tensor.matmul(ps_f[g % 2][:, n, :], mid[g % 2][:, t, q * P:(q + 1) * P], pos[:, q, t, n * BANK:(n + 1) * BANK],
                                                  start=q == 0 and t == 0, stop=q == 1 and t == lat - 1)
                mm.then_inc(f_ps, 1)

        @block.vector
        def _(dve):
            for g in range(KD):
                if g >= 2:
                    dve.wait_ge(f_ps, g - 1)
                for t2 in range(lat // 2):
                    m = g * 4 + t2
                    dve.wait_ge(chan_ps, m + 1)
                    nc.vector.tensor_copy(mid[g % 2][:, 2 * t2:2 * t2 + 2, :], ps_c[m % 2][:]).then_inc(mid_kept, 1)

        @block.scalar
        def _(act):
            for g in range(KD):
                act.wait_ge(f_ps, g + 1)
                nc.scalar.activation(f[:, g, CTX:], ps_f[g % 2][:, :, :].rearrange("p n c -> p (n c)"), ACT.Copy).then_inc(f_kept, 1)


FF = 512
KF = FF // P


def slots(n_tok):
    return 2 * n_tok // P + EXPERTS


def route(kit, name, h, lo, xb, where, weight, table):
    nc, a = kit.nc, kit.args
    n_tok = N - lo
    T = n_tok // P
    NB = slots(n_tok)
    with Stage(nc) as st:
        sb = lambda s, shape, dt=F32: st.enter_context(nc.sbuf_tensor(f"{name}_{s}", list(shape), dt))
        sem = lambda s: st.sem(f"{name}_{s}")
        rw = sb("rw", (P, KD, EXPERTS))
        rb = sb("rb", (P, EXPERTS))
        earlier = sb("earlier", (P, P))
        order = sb("order", (P, 64))
        rows = [sb(f"rows{u}", (P, D)) for u in range(T)]
        sc, sel = sb("sc", (P, T, EXPERTS)), sb("sel", (P, T, EXPERTS))
        big = lambda s: sb(s, (P, T, EXPERTS))
        rank, cmp_, first, second, both, pos, slot, tmp = (big(s) for s in ("rank", "cmp", "first", "second", "both", "pos", "slot", "tmp"))
        pair = sb("pair", (P, T, GROUPS))
        gs, grank, gcmp, ghot = (sb(s, (P, T, GROUPS)) for s in ("gs", "grank", "gcmp", "ghot"))
        tile_sum = sb("tile_sum", (P, T, EXPERTS))
        count, blocks_e, start, end = (sb(s, (P, EXPERTS)) for s in ("count", "blocks_e", "start", "end"))
        over = sb("over", (P, EXPERTS, T + 1))
        of_block = sb("of_block", (P, NB, EXPERTS))
        tab = sb("tab", (P, 4, 64))
        even = sb("even", (P, NB // 2))
        total = sb("total", (P, T))
        where_f = sb("where_f", (P, 2, T))
        ps_s = st.enter_context(nc.psum_tensor(f"{name}_pss", [P, T, EXPERTS], F32))
        ps_e = st.enter_context(nc.psum_tensor(f"{name}_pse", [P, T, EXPERTS], F32))
        ps_t = st.enter_context(nc.psum_tensor(f"{name}_pst", [P, T, EXPERTS], F32))
        ps_r = [st.enter_context(nc.psum_tensor(f"{name}_psr{u}", [P, 2, BANK], F32)) for u in range(2)]
        s_in, scored, scores_ready, link, masks_ready, counted, routed, row_ps, row_kept, stored, scattered = (
            sem(s) for s in ("s_in", "scored", "scores_ready", "link", "masks_ready", "counted", "routed", "row_ps", "row_kept",
                             "stored", "scattered"))
        block = st.enter_context(nc.Block(name))

        @block.sync
        def _(sp):
            sp.dma_start(rw[:], a["router_w"][:, :, :]).then_inc(s_in, 16)
            sp.dma_start(rb[:], a["router_b"][:, :]).then_inc(s_in, 16)
            sp.dma_start(earlier[:], a["earlier"][:, :]).then_inc(s_in, 16)
            sp.dma_start(order[:], a["order"][:, :]).then_inc(s_in, 16)
            for t in range(T):
                sp.wait_ge(row_kept, t + 1)
                sp.dma_start(xb[t * P:(t + 1) * P, :], rows[t][:]).then_inc(stored, 16)
            sp.wait_ge(stored, 16 * T)

        @block.tensor
        def _(pe):
            pe.wait_ge(s_in, 64)
            for t in range(T):
                for k in range(KD):
                    mm = nc.tensor.matmul(ps_s[:, t, :], h[:, k, lo + t * P:lo + (t + 1) * P], rw[:, k, :], start=k == 0, stop=k == KD - 1)
            mm.then_inc(scored, 1)
            for t in range(T):
                if t >= 2:
                    pe.wait_ge(row_kept, t - 1)
                for k in range(KD):
                    mm = nc.tensor.transpose(ps_r[t % 2][:, k // 4, (k % 4) * P:(k % 4 + 1) * P], h[:, k, lo + t * P:lo + (t + 1) * P], kit.ident[:])
                mm.then_inc(row_ps, 1)
            pe.wait_ge(masks_ready, 1)
            nc.tensor.matmul(ps_e[:], earlier[:], both[:], start=True, stop=True)
            nc.tensor.matmul(ps_t[:], kit.ones[:], both[:], start=True, stop=True).then_inc(counted, 1)

        @block.scalar
        def _(act):
            act.wait_ge(scored, 1)
            nc.scalar.activation(sc[:], ps_s[:], ACT.Sigmoid).then_inc(scores_ready, 1)
            for t in range(T):
                act.wait_ge(row_ps, t + 1)
                nc.scalar.activation(rows[t][:], ps_r[t % 2][:, :, :].rearrange("p b c -> p (b c)"), ACT.Copy).then_inc(row_kept, 1)

        @block.vector
        def _(dve):
            own = Link(dve, link)
            tt = lambda out, x, y, op: own(nc.vector.tensor_tensor(out, x, y, op))
            grouped = lambda x: x[:, :, :].rearrange("p t (g e) -> p (t g) e", e=MEMBERS)
            dve.wait_ge(s_in, 64)
            dve.wait_ge(scores_ready, 1)
            tt(sel[:], sc[:], rb[:, :].rearrange("p (o e) -> p o e", o=1).broadcast_to((P, T, EXPERTS)), ALU.add)
            s4, g1 = grouped(sel), gs[:, :, :].rearrange("p t (g o) -> p (t g) o", o=1)
            p1 = pair[:, :, :].rearrange("p t (g o) -> p (t g) o", o=1)
            pairs = [(i, j) for i in range(MEMBERS) for j in range(i + 1, MEMBERS)]
            for n, (i, j) in enumerate(pairs):
                tt(p1 if n else g1, s4[:, :, i:i + 1], s4[:, :, j:j + 1], ALU.add)
                if n:
                    tt(g1, g1, p1, ALU.max)
            own(nc.vector.memset(grank[:], 0.0))
            for i in range(GROUPS):
                for j in range(GROUPS):
                    if i != j:
                        tt(gcmp[:, :, i:i + 1], gs[:, :, j:j + 1], gs[:, :, i:i + 1], ALU.is_ge if j < i else ALU.is_gt)
                        tt(grank[:, :, i:i + 1], grank[:, :, i:i + 1], gcmp[:, :, i:i + 1], ALU.add)
            own(nc.vector.tensor_scalar(ghot[:], grank[:], 0.0, None, ALU.is_equal))
            own(nc.vector.memset(rank[:], 0.0))
            r4, c4 = grouped(rank), grouped(cmp_)
            for i in range(MEMBERS):
                for j in range(MEMBERS):
                    if i != j:
                        tt(c4[:, :, i:i + 1], s4[:, :, j:j + 1], s4[:, :, i:i + 1], ALU.is_ge if j < i else ALU.is_gt)
                        tt(r4[:, :, i:i + 1], r4[:, :, i:i + 1], c4[:, :, i:i + 1], ALU.add)
            gh = ghot[:, :, :].rearrange("p t (g o) -> p (t g) o", o=1).broadcast_to((P, T * GROUPS, MEMBERS))
            for out, which in ((first, 0.0), (second, 1.0)):
                own(nc.vector.tensor_scalar(out[:], rank[:], which, None, ALU.is_equal))
                tt(grouped(out), grouped(out), gh, ALU.mult)
            nc.vector.tensor_tensor(both[:], first[:], second[:], ALU.add).then_inc(masks_ready, 1)
            for i, m in enumerate((first, second)):
                tt(tmp[:], sc[:], m[:], ALU.mult)
                own(nc.vector.reduce_sum(weight[:, i, :], tmp[:], AX.X))
            tt(total[:], weight[:, 0, :], weight[:, 1, :], ALU.add)
            own(nc.vector.reciprocal(total[:], total[:]))
            for i in range(2):
                tt(weight[:, i, :], weight[:, i, :], total[:], ALU.mult)
            dve.wait_ge(counted, 1)
            own(nc.vector.tensor_copy(tile_sum[:], ps_t[:]))
            own(nc.vector.memset(count[:], 0.0))
            for t in range(T):
                tt(pos[:, t, :], ps_e[:, t, :], count[:], ALU.add)
                tt(count[:], count[:], tile_sum[:, t, :], ALU.add)
            full = order[:, 1:T + 1].rearrange("p (o m) -> p o m", o=1).broadcast_to((P, EXPERTS, T))
            own(nc.vector.scalar_tensor_tensor(out=over[:, :, 0:T], in0=full, scalar=float(P),
                                               in1=count[:, :].rearrange("p (e o) -> p e o", o=1).broadcast_to((P, EXPERTS, T)),
                                               op0=ALU.mult, op1=ALU.is_lt))
            own(nc.vector.reduce_sum(blocks_e[:], over[:, :, 0:T], AX.X))
            own(nc.vector.tensor_scalar(blocks_e[:], blocks_e[:], 1.0, None, ALU.add))
            own(nc.vector.tensor_tensor_scan(end[:], kit.ones[:, 0:EXPERTS], blocks_e[:], 0.0, ALU.mult, ALU.add))
            tt(start[:], end[:], blocks_e[:], ALU.subtract)
            own(nc.vector.tensor_scalar(start[:], start[:], float(P), float(n_tok), ALU.mult, ALU.add))
            tt(slot[:], pos[:], start[:, :].rearrange("p (o e) -> p o e", o=1).broadcast_to((P, T, EXPERTS)), ALU.add)
            for i, m in enumerate((first, second)):
                tt(tmp[:], slot[:], m[:], ALU.mult)
                own(nc.vector.reduce_sum(where_f[:, i, :], tmp[:], AX.X))
            nc.vector.tensor_copy(where[:], where_f[:]).then_inc(routed, 1)
            own(nc.vector.tensor_tensor(of_block[:], end[:, :].rearrange("p (o e) -> p o e", o=1).broadcast_to((P, NB, EXPERTS)),
                                        order[:, 0:NB].rearrange("p (b o) -> p b o", o=1).broadcast_to((P, NB, EXPERTS)), ALU.is_le))
            own(nc.vector.memset(tab[:], 0.0))
            own(nc.vector.reduce_sum(tab[:, 0, 0:NB], of_block[:], AX.X))
            own(nc.vector.tensor_scalar(tab[:, 0, 0:NB], tab[:, 0, 0:NB], float(EXPERTS - 1), None, ALU.min))
            own(nc.vector.tensor_scalar(of_block[:], order[:, 0:2 * EXPERTS:2].rearrange("p (o e) -> p o e", o=1).broadcast_to((P, NB, EXPERTS)), 0.0, None, ALU.add))
            own(nc.vector.tensor_tensor(of_block[:], of_block[:], tab[:, 0, 0:NB].rearrange("p (b o) -> p b o", o=1).broadcast_to((P, NB, EXPERTS)), ALU.is_equal))
            own(nc.vector.reduce_sum(tab[:, 1, 1:NB + 1], of_block[:], AX.X))
            own(nc.vector.tensor_scalar(tab[:, 3, 0:NB], tab[:, 0, 0:NB], 0.5, 0.5, ALU.mult, ALU.add))
            own(nc.vector.scalar_tensor_tensor(out=tab[:, 3, 0:NB], in0=tab[:, 1, 1:NB + 1], scalar=0.5, in1=tab[:, 3, 0:NB], op0=ALU.mult, op1=ALU.add))
            own(nc.vector.scalar_tensor_tensor(out=tab[:, 2, 0:NB], in0=tab[:, 1, 1:NB + 1], scalar=-1.0, in1=tab[:, 3, 0:NB], op0=ALU.mult, op1=ALU.add))
            own(nc.vector.tensor_scalar(tab[:, 2, 0:NB], tab[:, 2, 0:NB], 1.0, None, ALU.add))
            own(nc.vector.tensor_scalar(tab[:, 0, 50:64], end[:, 0:14], float(T), None, ALU.add))
            own(nc.vector.memset(tab[:, 0, 49:50], float(T)))
            own(nc.vector.tensor_tensor(even[:], order[:, 0:NB:2], end[:, EXPERTS - 1:EXPERTS].broadcast_to((P, NB // 2)), ALU.is_lt))
            own(nc.vector.reduce_sum(tab[:, 0, 48:49], even[:], AX.X))
            own(nc.vector.tensor_scalar(tab[:, 2:4, 0:NB], tab[:, 2:4, 0:NB], 48.0, None, ALU.mult))
            own(nc.vector.tensor_copy(table[:], tab[:]))

        @block.gpsimd
        def _(pool):
            pool.wait_ge(routed, 1)
            for t in range(T):
                pool.wait_ge(row_kept, t + 1)
                for i in range(2):
                    pool.indirect_dma_start(xb[:, :], bass.IndirectOffsetOnAxis(ap=where[:, i, t:t + 1], axis=0), rows[t][:], None).then_inc(scattered, 16)
            pool.wait_ge(scattered, 32 * T)


def experts(kit, name, layer, n_tok, xb, yb, table):
    nc, a = kit.nc, kit.args
    T, NB = n_tok // P, slots(n_tok)
    G_AT, U_AT, D_AT = 0, KD * FF, 2 * KD * FF
    with Stage(nc) as st:
        sb = lambda s, shape, dt=F32: st.enter_context(nc.sbuf_tensor(f"{name}_{s}", list(shape), dt))
        sem = lambda s: st.sem(f"{name}_{s}")
        psum = lambda s, b: st.enter_context(nc.psum_tensor(f"{name}_{s}", [P, b * BANK], F32))
        w = sb("w", (P, 2, 2 * KD * FF + KF * D))
        x_row = [sb(f"x_row{u}", (P, D)) for u in range(2)]
        y_row = [sb(f"y_row{u}", (P, D)) for u in range(2)]
        xt, act_g, hid, hid_t = sb("xt", (P, KD, P)), sb("act_g", (P, FF)), sb("hid", (P, FF)), sb("hid_t", (P, KF, P))
        spare = sb("spare", (P, 2, 64))
        ps_x, ps_g, ps_u, ps_h, ps_y = psum("psx", 2), psum("psg", 1), psum("psu", 1), psum("psh", 1), psum("psy", 2)
        w_in = [sem(f"w_in{u}") for u in range(2)]
        x_in = [sem(f"x_in{u}") for u in range(2)]
        y_stored = [sem(f"y_stored{u}") for u in range(2)]
        x_turned, x_copied_a, x_copied_v, gate_ps, up_ps, gated, hidden, h_turned, h_copied, y_ps, y_copied_a, y_copied_v = (
            sem(s) for s in ("x_turned", "x_copied_a", "x_copied_v", "gate_ps", "up_ps", "gated", "hidden", "h_turned",
                             "h_copied", "y_ps", "y_copied_a", "y_copied_v"))
        block = st.enter_context(nc.Block(name))
        names = ("gate", "up", "down")
        places = (G_AT, U_AT, D_AT)
        pairs_of = lambda eng: eng.value_load(table[0:1, 0, 48:49], min_val=EXPERTS // 2, max_val=NB // 2)

        @block.sync
        def _(sp):
            def load(buf, sources, parts=slice(0, 3)):
                for src, at, k in list(zip(sources, places, (KD, KD, KF)))[parts]:
                    dst = w[:, buf, at:at + 4096].rearrange("p (k f) -> p k f", k=k)
                    sp.dma_start(dst, src.rearrange("(k p) f -> p k f", p=P)).then_inc(w_in[buf], 16)

            def reload(buf, e, ready):
                sp.wait_ge(up_ps, ready)
                load(buf, expert(e), slice(0, 2))
                sp.wait_ge(y_ps, ready)
                load(buf, expert(e), slice(2, 3))

            def expert(e):
                return [a[f"moe_{n}"][layer, bass.ds(e, 1), :, :].rearrange("o k f -> (o k) f") for n in names]

            load(0, [a[f"shared_{n}"][layer, :, :] for n in names])
            load(1, [a[f"moe_{n}"][layer, 0, :, :] for n in names])
            with sp.Fori(0, EXPERTS // 2 - 1) as i:
                for u in range(2):
                    e = i * 2 + (u + 1)
                    ready = sp.value_load(table[0:1, 0, bass.ds(i * 2 + (49 + u), 1)], min_val=1, max_val=T + NB)
                    reload(u, e, ready)
            ready = sp.value_load(table[0:1, 0, 63:64], min_val=1, max_val=T + NB)
            reload(0, EXPERTS - 1, ready)

        @block.tensor
        def _(pe):
            wt = lambda buf, at: (w[:, buf, at:at + BANK] if isinstance(buf, int) else
                                  w[:, bass.ds(buf, 1), at:at + BANK].rearrange("p o f -> p (o f)"))

            def turn_x(m, u, i2):
                pe.wait_ge(x_in[u], i2 * 16 + 16)
                for k in range(KD):
                    mm = nc.tensor.transpose(ps_x[:, k * P:(k + 1) * P], x_row[u][:, k * P:(k + 1) * P], kit.ident[:])
                mm.then_inc(x_turned, 1)

            def gate_up(m, buf):
                pe.wait_ge(x_copied_a, m + 1)
                pe.wait_ge(x_copied_v, m + 1)
                for ps, at, sem_ in ((ps_g, G_AT, gate_ps), (ps_u, U_AT, up_ps)):
                    for k in range(KD):
                        mm = nc.tensor.matmul(ps[:], xt[:, k, :], wt(buf, at + k * FF), start=k == 0, stop=k == KD - 1)
                    mm.then_inc(sem_, 1)

            def down(m, buf):
                pe.wait_ge(h_copied, m + 1)
                pe.wait_ge(y_copied_a, m + 1)
                pe.wait_ge(y_copied_v, m + 1)
                for n in range(2):
                    for k in range(KF):
                        mm = nc.tensor.matmul(ps_y[:, n * BANK:(n + 1) * BANK], hid_t[:, k, :], wt(buf, D_AT + k * D + n * BANK), start=k == 0, stop=k == KF - 1)
                mm.then_inc(y_ps, 1)

            def turn_h(m):
                pe.wait_ge(hidden, m + 1)
                for k in range(KF):
                    mm = nc.tensor.transpose(ps_h[:, k * P:(k + 1) * P], hid[:, k * P:(k + 1) * P], kit.ident[:])
                mm.then_inc(h_turned, 1)

            pe.wait_ge(w_in[0], 48)
            turn_x(0, 0, 0)
            gate_up(0, 0)
            turn_x(1, 1, 0)
            turn_h(0)
            gate_up(1, 0)
            turn_x(2, 0, 1)
            down(0, 0)
            turn_h(1)
            with pe.Fori(1, T // 2) as i:
                for u in range(2):
                    m = i * 2 + u
                    gate_up(m, 0)
                    turn_x(m + 1, 1 - u, i + u)
                    down(m - 1, 0)
                    turn_h(m)
            with pe.Fori(0, pairs_of(pe)) as i:
                for u in range(2):
                    b = i * 2 + u
                    m = b + T
                    before = pe.value_load(table[0:1, 1, bass.ds(b, 1)], min_val=0, max_val=1)
                    buf = pe.value_load(table[0:1, 1, bass.ds(b + 1, 1)], min_val=0, max_val=1)
                    for q in range(2):
                        loads = pe.value_load(table[0:1, 2 + q, bass.ds(b, 1)], min_val=48, max_val=48 * 9)
                        pe.wait_ge(w_in[q], loads)
                    gate_up(m, buf)
                    turn_x(m + 1, 1 - u, i + (T // 2 + u))
                    down(m - 1, before)
                    turn_h(m)
            pairs = pairs_of(pe)
            last = pe.value_load(table[0:1, 1, bass.ds(pairs * 2, 1)], min_val=0, max_val=1)
            down(pairs * 2 + (T - 1), last)

        @block.scalar
        def _(act):
            act.sem_inc(y_copied_a, 1)
            for u in range(2):
                act.dma_start(x_row[u][:], xb[u * P:(u + 1) * P, :]).then_inc(x_in[u], 16)
                act.dma_start(spare[:, u, :], a["order"][:, :]).then_inc(y_stored[u], 16)

            def next_x(m, u):
                act.wait_ge(x_turned, m + 1)
                act.dma_start(x_row[u][:], xb[bass.ds(m * P + 2 * P, P), :]).then_inc(x_in[u], 16)
                nc.scalar.activation(xt[:, 4:8, :], ps_x[:, BANK:2 * BANK].rearrange("p (k t) -> p k t", t=P), ACT.Copy).then_inc(x_copied_a, 1)

            def silu(m):
                act.wait_ge(gate_ps, m + 1)
                nc.scalar.activation(act_g[:], ps_g[:], ACT.Silu).then_inc(gated, 1)

            def y_half(m, u, i2):
                act.wait_ge(y_ps, m + 1)
                act.wait_ge(y_stored[u], i2 * 16 + 16)
                nc.scalar.activation(y_row[u][:, BANK:], ps_y[:, BANK:], ACT.Copy).then_inc(y_copied_a, 1)
                act.wait_ge(y_copied_a, m + 2)
                act.wait_ge(y_copied_v, m + 2)
                act.dma_start(yb[bass.ds(m * P, P), :], y_row[u][:]).then_inc(y_stored[u], 16)

            next_x(0, 0)
            silu(0)
            next_x(1, 1)
            silu(1)
            next_x(2, 0)
            y_half(0, 0, 0)

            def rest(first, end):
                with act.Fori(first, end) as i:
                    for u in range(2):
                        m = i * 2 + u
                        silu(m)
                        next_x(m + 1, 1 - u)
                        y_half(m - 1, 1 - u, i - (1 - u))

            rest(1, pairs_of(act) + T // 2)
            pairs = pairs_of(act)
            y_half(pairs * 2 + (T - 1), 1, pairs + (T // 2 - 1))

        @block.gpsimd
        def _(pool):
            pairs = pairs_of(pool)
            for u in range(2):
                pool.wait_ge(y_stored[u], pairs * 16 + 16 * (T // 2 + 1))
                pool.wait_ge(x_in[u], pairs * 16 + 16 * (T // 2 + 1 + (1 - u)))

        @block.vector
        def _(dve):
            dve.sem_inc(y_copied_v, 1)

            def next_x(m):
                dve.wait_ge(x_turned, m + 1)
                nc.vector.tensor_copy(xt[:, 0:4, :], ps_x[:, 0:BANK].rearrange("p (k t) -> p k t", t=P)).then_inc(x_copied_v, 1)

            def product(m):
                dve.wait_ge(gated, m + 1)
                dve.wait_ge(up_ps, m + 1)
                nc.vector.tensor_tensor(hid[:], act_g[:], ps_u[:], ALU.mult).then_inc(hidden, 1)

            def h_copy(m):
                dve.wait_ge(h_turned, m + 1)
                nc.vector.tensor_copy(hid_t[:, :, :], ps_h[:, :].rearrange("p (k t) -> p k t", t=P)).then_inc(h_copied, 1)

            def y_half(m, u, i2):
                dve.wait_ge(y_ps, m + 1)
                dve.wait_ge(y_stored[u], i2 * 16 + 16)
                nc.vector.tensor_copy(y_row[u][:, 0:BANK], ps_y[:, 0:BANK]).then_inc(y_copied_v, 1)

            next_x(0)
            product(0)
            next_x(1)
            h_copy(0)
            product(1)
            next_x(2)
            y_half(0, 0, 0)
            h_copy(1)

            with dve.Fori(1, pairs_of(dve) + T // 2) as i:
                for u in range(2):
                    m = i * 2 + u
                    product(m)
                    next_x(m + 1)
                    y_half(m - 1, 1 - u, i - (1 - u))
                    h_copy(m)
            pairs = pairs_of(dve)
            y_half(pairs * 2 + (T - 1), 1, pairs + (T // 2 - 1))


def combine(kit, name, x, lo, gate, yb, where, weight, out=None):
    nc = kit.nc
    T = (N - lo) // P
    with Stage(nc) as st:
        sb = lambda s: st.enter_context(nc.sbuf_tensor(f"{name}_{s}", [P, D], F32))
        sem = lambda s: st.sem(f"{name}_{s}")
        got = [[sb(f"got{i}{u}") for u in range(2)] for i in range(2)]
        own_row = [sb(f"own{u}") for u in range(2)]
        ps = [st.enter_context(nc.psum_tensor(f"{name}_ps{u}", [P, KD, P], F32)) for u in range(2)]
        own_in = [sem(f"own_in{u}") for u in range(2)]
        got_in = [sem(f"got_in{u}") for u in range(2)]
        part, mixed, turned, added, stored = sem("part"), sem("mixed"), sem("turned"), sem("added"), sem("stored")
        block = st.enter_context(nc.Block(name))

        @block.gpsimd
        def _(pool):
            for t in range(T):
                if t >= 2:
                    pool.wait_ge(mixed, t - 1)
                for i in range(2):
                    pool.indirect_dma_start(got[i][t % 2][:], None, yb[:, :], bass.IndirectOffsetOnAxis(ap=where[:, i, t:t + 1], axis=0)).then_inc(got_in[t % 2], 16)

        @block.sync
        def _(sp):
            for t in range(T):
                if t >= 2:
                    sp.wait_ge(turned, t - 1)
                sp.dma_start(own_row[t % 2][:], yb[t * P:(t + 1) * P, :]).then_inc(own_in[t % 2], 16)
            if out is not None:
                sp.wait_ge(added, T)
                for k in range(KD):
                    sp.dma_start(out[k * P:(k + 1) * P, :], x[:, k, lo:]).then_inc(stored, 16)
                sp.wait_ge(stored, 16 * KD)

        @block.vector
        def _(dve):
            def add(t):
                s = lo + t * P
                dve.wait_ge(turned, t + 1)
                for k in range(KD):
                    c = nc.vector.scalar_tensor_tensor(out=x[:, k, s:s + P], in0=ps[t % 2][:, k, :], scalar=kit.mod[:, gate + k, int(s < CTX):int(s < CTX) + 1],
                                                       in1=x[:, k, s:s + P], op0=ALU.mult, op1=ALU.add)
                c.then_inc(added, 1)

            for t in range(T):
                row = own_row[t % 2]
                dve.wait_ge(own_in[t % 2], 16 * (t // 2 + 1))
                dve.wait_ge(got_in[t % 2], 32 * (t // 2 + 1))
                nc.vector.scalar_tensor_tensor(out=row[:], in0=got[0][t % 2][:], scalar=weight[:, 0, t:t + 1], in1=row[:], op0=ALU.mult, op1=ALU.add).then_inc(part, 1)
                dve.wait_ge(part, t + 1)
                nc.vector.scalar_tensor_tensor(out=row[:], in0=got[1][t % 2][:], scalar=weight[:, 1, t:t + 1], in1=row[:], op0=ALU.mult, op1=ALU.add).then_inc(mixed, 1)
                if t:
                    add(t - 1)
            add(T - 1)

        @block.tensor
        def _(pe):
            for t in range(T):
                pe.wait_ge(mixed, t + 1)
                if t >= 2:
                    pe.wait_ge(added, t - 1)
                for k in range(KD):
                    mm = nc.tensor.transpose(ps[t % 2][:, k, :], own_row[t % 2][:, k * P:(k + 1) * P], kit.ident[:])
                mm.then_inc(turned, 1)


def mixture(kit, layer, x, h, lo, xb, yb, out=None):
    nc = kit.nc
    T = (N - lo) // P
    with ExitStack() as st:
        where = st.enter_context(nc.sbuf_tensor(f"where{layer}", [P, 2, T], U32))
        weight = st.enter_context(nc.sbuf_tensor(f"weight{layer}", [P, 2, T], F32))
        table = st.enter_context(nc.sbuf_tensor(f"table{layer}", [P, 4, 64], I32))
        with nc.sbuf_tensor(f"h{layer}_2", [P, KD, N], F32) as h:
            normalise(kit, f"norm{layer}2", x, h, lo, 2 * layer + 1, 48 * layer + 3 * KD)
            route(kit, f"route{layer}", h, lo, xb, where, weight, table)
        experts(kit, f"experts{layer}", layer, N - lo, xb, yb, table)
        combine(kit, f"combine{layer}", x, lo, 48 * layer + 5 * KD, yb, where, weight, out)


def program(nc, a, out):
    dram = lambda name, shape: nc.dram_tensor(name, list(shape), F32).ap()
    p = dram("p", (19, P, N))
    steps = dram("steps", (2, NT, P, 4, KINDS, P))
    y_steps = dram("y_steps", (2, NT, P, 4, P))
    gate, bonus = dram("gate", (4, P, N)), dram("bonus", (4, P, N))
    y_all = dram("y_all", (KD, P, N))
    xb = dram("xb", (N + (slots(N) + 3) * P, D))
    yb = dram("yb", (N + slots(N) * P, D))
    inputs = {0: a["xT"], 1: a["ctxT"]}
    with ExitStack() as st:
        kit = Kit(nc, a, st)
        modulation(kit)
        with nc.sbuf_tensor("h01", [P, KD, N], F32) as h:
            normalise(kit, "norm01", h, h, 0, 0, 0, load=inputs)
            project_in(kit, h, p)
        with nc.sbuf_tensor("half_decay", [P, 2, NT, 4], F32) as half_decay:
            mixing_inputs(kit, p, steps, half_decay, gate, bonus)
            mixing_scan(kit, steps, half_decay, y_steps)
        mixing_out(kit, y_steps, gate, bonus, y_all)
        attention(kit, p, y_all, xb, yb)
        x = st.enter_context(nc.sbuf_tensor("x", [P, KD, N], F32))
        with nc.sbuf_tensor("y01", [P, KD, N], F32) as y:
            project_out(kit, "out0", y, a["w_out_even"], x, 2 * KD, 0, load_y=y_all, load_x=inputs)
        mixture(kit, 0, x, None, 0, xb, yb)
        with nc.sbuf_tensor("h11", [P, KD, N], F32) as h:
            normalise(kit, "norm11", x, h, CTX, 2, 48)
            fourier(kit, h, h)
            project_out(kit, "out1", h, a["w_out_fourier"], x, 48 + 2 * KD, CTX)
        mixture(kit, 1, x, None, CTX, xb, yb, out)


def constants():
    f = np.float32
    i = np.arange(P)
    restart = np.ones((P, N), f)
    restart[:, ::P] = 0
    before = i[:, None] < i[None]
    pair = np.stack([np.stack([before, before | np.eye(P, dtype=bool)], 1), np.stack([before.T, before.T | np.eye(P, dtype=bool)], 1)], 1)
    level = []
    for v in range(LEVELS):
        m = 1 << v
        same = i[:, None] // (2 * m) == i[None] // (2 * m)
        level.append(same & (i[:, None] // m % 2 == 0) & (i[None] // m % 2 == 1))
    level = np.stack(level, 1)
    at = np.arange(SEQ)
    inv = 10000.0 ** (-np.arange(0, 16, 2) / 16)
    ang = np.concatenate([(at // 64)[:, None] * inv, (at % 64)[:, None] * inv], 1).T
    cos = np.concatenate([np.ones((64, SEQ)), np.cos(ang), np.cos(ang)])
    sin = np.concatenate([np.zeros((64, SEQ)), np.sin(ang), np.sin(ang)])
    rot = np.zeros((QK, QK), f)
    for c in range(16):
        rot[80 + c, 64 + c] = -1
        rot[64 + c, 80 + c] = 1
    b = np.arange(P)[:, None] * np.arange(P)[None] % P * (2 * np.pi / P)
    c = np.arange(SEQ)[:, None] * np.arange(SEQ)[None] % SEQ * (2 * np.pi / SEQ)
    by_rows = lambda m: m.reshape(SEQ // P, P, SEQ).transpose(1, 0, 2)
    pos = np.stack([by_rows(np.cos(c)), by_rows(np.sin(c))], 1) / np.sqrt(SEQ)
    chan = np.concatenate([np.cos(b), -np.sin(b)], 1) / np.sqrt(P)
    return {"dft_pos": pos.astype(f), "dft_chan": chan.astype(f), "earlier": before.astype(f),
            "order": np.tile(np.arange(64, dtype=f), (P, 1)), "cos": cos.astype(f), "sin": sin.astype(f), "rot": rot, "pair_mask": pair.astype(f), "level_mask": np.stack([level, level.transpose(2, 1, 0)], 1).astype(f), "ident": np.eye(P, dtype=f), "restart": restart, "head_ones": (i[:, None] // 64 == i[None] // 64).astype(f)}


def laid_out(inp):
    f = np.float32
    by_col = lambda v: np.ascontiguousarray(np.asarray(v, f).reshape(-1, P).T)
    pad = lambda v, n: np.concatenate([np.asarray(v, f).ravel(), np.zeros(n - np.size(v), f)])
    cond = np.stack([by_col(inp["c"]), by_col(inp["c_ctx"])], 2).reshape(P, 16)
    cols = [cond, by_col(inp["norm1_g"]), by_col(inp["norm2_g"]), by_col(pad(inp["a_mu"], 20 * P)), by_col(inp["a_w0"]),
            by_col(inp["a_a0"]), by_col(inp["a_k_k"]), by_col(inp["a_k_a"]), by_col(inp["a_r_k"]), by_col(inp["a_ln_w"]),
            by_col(inp["a_ln_b"]), by_col(inp["b_q_norm"]), by_col(inp["b_kv_norm"]), by_col(pad(inp["b_q_gain"], P)),
            by_col(pad(inp["b_k_gain"], P))]
    bias = by_col(inp["mod_b"])
    chunked = lambda w: np.ascontiguousarray(np.asarray(w, f).reshape(-1, P, w.shape[-1]).transpose(1, 0, 2))
    return {
        "xT": np.ascontiguousarray(np.asarray(inp["x"], f)[0].T), "ctxT": np.ascontiguousarray(np.asarray(inp["ctx"], f)[0].T),
        "cols": np.concatenate(cols, 1), "mod_bias": np.stack([bias, bias], 2),
        "mod_w": chunked(np.concatenate([inp["mod_w"][0], inp["mod_w"][1]], 1)),
        "w_in": chunked(inp["w_in"][0]),
        "w_out_even": chunked(inp["w_out_even"][0]), "w_out_fourier": chunked(inp["w_out_fourier"][0]),
        "router_w": chunked(inp["router_w"]), "router_b": np.tile(np.asarray(inp["router_b"], f), (P, 1)),
        "moe_gate": inp["moe_w_gate"], "moe_up": inp["moe_w_up"], "moe_down": inp["moe_w_down"],
        "shared_gate": inp["shared_w_gate"], "shared_up": inp["shared_w_up"], "shared_down": inp["shared_w_down"],
        "w_q": chunked(inp["b_w_q_up"][0]),
        "w_k": np.ascontiguousarray(inp["b_w_kv_up"][0].reshape(P, HEADS, 2, 64)[:, :, 0]).reshape(P, -1),
        "w_v": np.ascontiguousarray(inp["b_w_kv_up"][0].reshape(P, HEADS, 2, 64)[:, :, 1]).reshape(P, -1),
        "a_w2": inp["a_w2"][0].reshape(P, -1), "a_a2": inp["a_a2"][0].reshape(P, -1), "a_g2": inp["a_g2"][0],
    }


def kernel(**inputs):
    import concourse.bacc as _bacc
    from concourse.bass_utils import run_bass_kernel_spmd as _run

    nc = _bacc.Bacc("TRN2", target_bir_lowering=False, num_devices=1)
    arrays = {k: v for k, v in laid_out({k: np.asarray(v) for k, v in inputs.items()}).items()}
    arrays.update(constants())
    args = {k: nc.dram_tensor(f"in_{k}", v.shape, mybir.dt.from_np(v.dtype), kind="ExternalInput").ap() for k, v in arrays.items()}
    out = nc.dram_tensor("outT", (D, SEQ), F32, kind="ExternalOutput").ap()
    program(nc, args, out)
    r = _run(nc, [{f"in_{k}": v for k, v in arrays.items()}], core_ids=[0])
    return np.ascontiguousarray(r.results[0]["outT"].T)[None]
```
